# Optimizing a Trainium2 kernel written in Bass

```python
import math
import jax, jax.numpy as jnp
from jax import lax
import numpy as np

D_MODEL = 1024
BATCH = 1
SEQ = 256
DEPTH = 2
DEC_BATCH = 8
DEC_SEQ = 4
PAST_LEN = 2048
PAGE_SIZE = 128

CHUNK = 128
A_GROUPS = 8
A_GROUP_DIM = 128
D_A = A_GROUPS * A_GROUP_DIM
D_B = D_MODEL
CONV_W = 31
N_MEM = 256
M_HEADS = 4
M_HEAD_DIM = 256
D_M = M_HEADS * M_HEAD_DIM
PEER_HEADS = 8
PEER_KEY_DIM = 128
PEER_HALF = PEER_KEY_DIM // 2
N_KEYS = 128
N_EXPERTS = N_KEYS * N_KEYS
PEER_TOPK = 16
PEER_BLOCK = 256
EPS = 1e-6
SPLITS = [D_A, 2 * D_A, 2 * D_A + D_B, 2 * D_A + 2 * D_B, 2 * D_A + 2 * D_B + D_M,
          2 * D_A + 2 * D_B + D_M + D_MODEL, 2 * D_A + 2 * D_B + D_M + 2 * D_MODEL]
D_IN = 2 * D_A + 2 * D_B + D_M + 3 * D_MODEL

kernel_name = 'hybrid_sgu_conformer_peer_decoder_step'

def _rmsnorm(x, g):
    xf = x.astype(jnp.float32)
    y = xf * lax.rsqrt(jnp.mean(xf * xf, axis=-1, keepdims=True) + EPS)
    return (y * g.astype(jnp.float32)).astype(x.dtype)

def _layernorm(x, g, b):
    xf = x.astype(jnp.float32)
    mu = jnp.mean(xf, axis=-1, keepdims=True)
    var = jnp.mean(jnp.square(xf - mu), axis=-1, keepdims=True)
    y = (xf - mu) * lax.rsqrt(var + EPS)
    return (y * g.astype(jnp.float32) + b.astype(jnp.float32)).astype(x.dtype)

def _spatial_gate(u, v, ws, bs, ln_g, ln_b):
    n, t, _ = u.shape
    L = min(t, CHUNK)
    nc = t // L
    vn = _layernorm(v, ln_g, ln_b)
    vc = vn.reshape(n, nc, L, A_GROUPS, A_GROUP_DIM)
    w = jnp.tril(ws[:, :L, :L])
    s = jnp.einsum('gts,ncsgd->nctgd', w, vc) + bs[:, :L].T[None, None, :, :, None]
    return u * s.reshape(n, t, D_A), vn

def _causal_depthwise(x_ext, w, b):
    y = lax.conv_general_dilated(x_ext, w[:, None, :], (1,), 'VALID',
                                 dimension_numbers=('NWC', 'WIO', 'NWC'),
                                 feature_group_count=x_ext.shape[-1])
    return y + b

def _mem_attend(q, mk, mv):
    n, t, _ = q.shape
    qh = q.reshape(n, t, M_HEADS, M_HEAD_DIM)
    s = jnp.einsum('nthd,nmhd->nhtm', qh, mk).astype(jnp.float32) * (M_HEAD_DIM ** -0.5)
    p = jax.nn.softmax(s, axis=-1).astype(q.dtype)
    o = jnp.einsum('nhtm,nmhd->nthd', p, mv)
    return o.reshape(n, t, D_M)

def _mixing_sublayer(x, mem_k, mem_v, conv_past, w):
    xn = _rmsnorm(x, w['norm_mix_g'])
    h = xn @ w['w_in']
    u_a, v_a, val_b, gate_b, q_m, gl_a, gl_b, gl_m = jnp.split(h, SPLITS, axis=-1)
    y_a, vn = _spatial_gate(jax.nn.gelu(u_a, approximate=False), jax.nn.gelu(v_a, approximate=False),
                            w['a_ws'], w['a_bs'], w['a_ln_g'], w['a_ln_b'])
    glu = val_b * jax.nn.sigmoid(gate_b)
    ext = jnp.concatenate([conv_past, glu], axis=1)
    new_conv = ext[:, -(CONV_W - 1):]
    c = _causal_depthwise(ext, w['b_conv_w'], w['b_conv_b'])
    y_b = jax.nn.silu(_layernorm(c, w['b_ln_g'], w['b_ln_b']))
    y_m = _mem_attend(q_m, mem_k, mem_v)
    merged = (jax.nn.sigmoid(gl_a) * (y_a @ w['w_o_a'])
              + jax.nn.sigmoid(gl_b) * (y_b @ w['w_o_b'])
              + jax.nn.sigmoid(gl_m) * (y_m @ w['w_o_m']))
    return x + merged @ w['w_out'], vn, new_conv

def _peer(xn, wq, keys, u_tab, v_tab):
    n, t, d = xn.shape
    n_tok = n * t
    n_blk = -(-n_tok // PEER_BLOCK)
    pad = n_blk * PEER_BLOCK - n_tok
    xt = jnp.pad(xn.reshape(n_tok, d), ((0, pad), (0, 0))).reshape(n_blk, PEER_BLOCK, d)

    def block(xb):
        q = (xb @ wq).reshape(PEER_BLOCK, PEER_HEADS, 2, PEER_HALF)
        s = jnp.einsum('bhpk,hpnk->bhpn', q, keys)
        v1, i1 = lax.top_k(s[:, :, 0], PEER_TOPK)
        v2, i2 = lax.top_k(s[:, :, 1], PEER_TOPK)
        cand = (v1[..., :, None] + v2[..., None, :]).reshape(PEER_BLOCK, PEER_HEADS, PEER_TOPK * PEER_TOPK)
        cv, ci = lax.top_k(cand, PEER_TOPK)
        e1 = jnp.take_along_axis(i1, ci // PEER_TOPK, axis=-1)
        e2 = jnp.take_along_axis(i2, ci % PEER_TOPK, axis=-1)
        eid = e1 * N_KEYS + e2
        g = jax.nn.softmax(cv.astype(jnp.float32), axis=-1).astype(xb.dtype)
        hid = jax.nn.gelu(jnp.einsum('bd,bhkd->bhk', xb, u_tab[eid]), approximate=False)
        return jnp.einsum('bhk,bhkd->bd', g * hid, v_tab[eid])

    y = lax.map(block, xt)
    return y.reshape(n_blk * PEER_BLOCK, d)[:n_tok].reshape(n, t, d)

def setup_inputs(seed: int = 0) -> dict:
    key = jax.random.key(seed)
    ks = iter(jax.random.split(key, 40))
    f32 = jnp.float32

    def nrm(shape, scale):
        return jax.random.normal(next(ks), shape, f32) * scale

    def gain(shape):
        return 1.0 + 0.05 * jax.random.normal(next(ks), shape, f32)

    return {
        'x_prompt': nrm((BATCH, SEQ, D_MODEL), 1.0),
        'x_sample': nrm((DEC_BATCH, DEC_SEQ, D_MODEL), 1.0),
        'mem_prompt': nrm((BATCH, N_MEM, D_MODEL), 1.0),
        'cache_mem_k': nrm((DEPTH, DEC_BATCH, N_MEM, M_HEADS, M_HEAD_DIM), 1.0),
        'cache_mem_v': nrm((DEPTH, DEC_BATCH, N_MEM, M_HEADS, M_HEAD_DIM), 1.0),
        'state_conv': nrm((DEPTH, DEC_BATCH, CONV_W - 1, D_B), 0.5),
        'norm_mix_g': gain((DEPTH, D_MODEL)),
        'w_in': nrm((DEPTH, D_MODEL, D_IN), D_MODEL ** -0.5),
        'a_ln_g': gain((DEPTH, D_A)),
        'a_ln_b': nrm((DEPTH, D_A), 0.02),
        'a_ws': nrm((DEPTH, A_GROUPS, CHUNK, CHUNK), 0.5 * CHUNK ** -0.5),
        'a_bs': gain((DEPTH, A_GROUPS, CHUNK)),
        'b_conv_w': nrm((DEPTH, CONV_W, D_B), CONV_W ** -0.5),
        'b_conv_b': nrm((DEPTH, D_B), 0.02),
        'b_ln_g': gain((DEPTH, D_B)),
        'b_ln_b': nrm((DEPTH, D_B), 0.02),
        'mem_norm_g': gain((DEPTH, D_MODEL)),
        'w_mem_k': nrm((DEPTH, D_MODEL, D_M), D_MODEL ** -0.5),
        'w_mem_v': nrm((DEPTH, D_MODEL, D_M), D_MODEL ** -0.5),
        'w_o_a': nrm((DEPTH, D_A, D_MODEL), D_A ** -0.5),
        'w_o_b': nrm((DEPTH, D_B, D_MODEL), D_B ** -0.5),
        'w_o_m': nrm((DEPTH, D_M, D_MODEL), D_M ** -0.5),
        'w_out': nrm((DEPTH, D_MODEL, D_MODEL), 0.5 * D_MODEL ** -0.5),
        'norm_ffn_g': gain((DEPTH, D_MODEL)),
        'peer_wq': nrm((DEPTH, D_MODEL, PEER_HEADS * PEER_KEY_DIM), D_MODEL ** -0.5),
        'peer_keys': nrm((DEPTH, PEER_HEADS, 2, N_KEYS, PEER_HALF), PEER_HALF ** -0.5),
        'peer_u': nrm((DEPTH, N_EXPERTS, D_MODEL), D_MODEL ** -0.5),
        'peer_v': nrm((DEPTH, N_EXPERTS, D_MODEL), (PEER_HEADS * PEER_TOPK) ** -0.5),
        'final_norm_g': gain((D_MODEL,)),
    }

def reference(x_prompt, x_sample, mem_prompt, cache_mem_k, cache_mem_v, state_conv,
              norm_mix_g, w_in, a_ln_g, a_ln_b, a_ws, a_bs, b_conv_w, b_conv_b, b_ln_g, b_ln_b,
              mem_norm_g, w_mem_k, w_mem_v, w_o_a, w_o_b, w_o_m, w_out,
              norm_ffn_g, peer_wq, peer_keys, peer_u, peer_v, final_norm_g):
    xp, xs = x_prompt, x_sample
    n_p, n_mem = mem_prompt.shape[0], mem_prompt.shape[1]
    mk_p, mv_p, conv_p, conv_s, chunk_v_s = [], [], [], [], []
    for l in range(DEPTH):
        lw = {'norm_mix_g': norm_mix_g[l], 'w_in': w_in[l], 'a_ln_g': a_ln_g[l], 'a_ln_b': a_ln_b[l],
              'a_ws': a_ws[l], 'a_bs': a_bs[l], 'b_conv_w': b_conv_w[l], 'b_conv_b': b_conv_b[l],
              'b_ln_g': b_ln_g[l], 'b_ln_b': b_ln_b[l], 'w_o_a': w_o_a[l], 'w_o_b': w_o_b[l],
              'w_o_m': w_o_m[l], 'w_out': w_out[l]}
        mem_n = _rmsnorm(mem_prompt, mem_norm_g[l])
        kp = (mem_n @ w_mem_k[l]).reshape(n_p, n_mem, M_HEADS, M_HEAD_DIM)
        vp = (mem_n @ w_mem_v[l]).reshape(n_p, n_mem, M_HEADS, M_HEAD_DIM)
        zero_past = jnp.zeros((xp.shape[0], CONV_W - 1, D_B), xp.dtype)
        xp, _, cp = _mixing_sublayer(xp, kp, vp, zero_past, lw)
        xp = xp + _peer(_rmsnorm(xp, norm_ffn_g[l]), peer_wq[l], peer_keys[l], peer_u[l], peer_v[l])
        xs, vns, cs = _mixing_sublayer(xs, cache_mem_k[l], cache_mem_v[l], state_conv[l], lw)
        xs = xs + _peer(_rmsnorm(xs, norm_ffn_g[l]), peer_wq[l], peer_keys[l], peer_u[l], peer_v[l])
        mk_p.append(kp)
        mv_p.append(vp)
        conv_p.append(cp)
        conv_s.append(cs)
        chunk_v_s.append(vns)
    y_prompt = _rmsnorm(xp, final_norm_g)
    y_sample = _rmsnorm(xs, final_norm_g)
    new_mem_k_prompt = jnp.stack(mk_p)
    new_mem_v_prompt = jnp.stack(mv_p)
    new_conv_prompt = jnp.stack(conv_p)
    new_conv_sample = jnp.stack(conv_s)
    new_chunk_v_sample = jnp.stack(chunk_v_s)
    return (y_prompt, y_sample, new_mem_k_prompt, new_mem_v_prompt, new_conv_prompt, new_conv_sample, new_chunk_v_sample)


_drawn_inputs = setup_inputs


def setup_inputs(seed=0):
    import zlib

    import numpy as np

    out = dict(_drawn_inputs(seed))
    spreads = {}
    factors = {'a_ln_b': 2.787,
     'a_bs': 4.172,
     'b_conv_b': 4.812,
     'b_ln_g': 3.731,
     'b_ln_b': 8.0,
     'norm_ffn_g': 3.812}
    for name, (base, spread) in spreads.items():
        noise = np.random.default_rng([zlib.crc32(name.encode()), seed]).standard_normal(out[name].shape)
        drawn = base * np.exp(spread * noise) if base else spread * noise
        out[name] = __import__('jax').numpy.asarray(drawn.astype(out[name].dtype))
    for name, factor in factors.items():
        out[name] = (out[name] * factor).astype(out[name].dtype)
    return out
```

```python
from contextlib import ExitStack

import numpy as np
import concourse.bass as bass
from concourse import mybir

F32 = mybir.dt.float32
U32 = mybir.dt.uint32
ALU = mybir.AluOpType
ACT = mybir.ActivationFunctionType
AX = mybir.AxisListType

P = 128
DEPTH = 2
D = 1024
KB = D // P
T_P, T_S = 256, 32
T = T_P + T_S
NSEQ, DSEQ = 8, 4
TILES = 3
CONV_W = 31
PAST = CONV_W - 1
M = 256
HEADS, HD = 4, 256
EPS = 1e-6
PH, NK, TOPK = 8, 128, 16
NEXP = NK * NK
STEPS = 2 * PH + 2
GROUPS = 4
NEG = -3.0e38

WTILES = [("glu", 4), ("mk", 2), ("mv", 2), ("va", 2), ("ua", 2), ("q", 2), ("merge", 12), ("out", 2), ("wq", 2)]
NW = sum(n for _, n in WTILES)
WFIRST = {}
_n = 0
for _kind, _c in WTILES:
    WFIRST[_kind] = _n
    _n += _c


def wslot(i):
    if i < WFIRST["out"]:
        return i % 4
    return (2, 3, 0, 1)[i - WFIRST["out"]]


def wuse(i):
    return sum(wslot(j) == wslot(i) for j in range(i))


WUSES = [sum(wslot(i) == s for i in range(NW)) for s in range(4)]

PER = dict(
    squares=6, meansq=2, roots=5, rstd=5, xrows=6,
    pe_xt=8, xnt=8, memsq=8, pe_memsq=8, varsum=2, memn=8,
    sig=32, pe_glu=16, glu=16, past_zero=1, ws_masked=2,
    pe_mk=8, pe_mv=4, kv=12, pe_va=6, va=6, lnv_var=1, ln_norm=3, ln_g=3, ln_done=3,
    pe_ua=8, ua=8, pe_q=8, q=8, pe_sgu=8, ya=8,
    pe_s=5, nm=5, pexp=9, p=5, pe_pt=5, pt=5, pe_o=4, o=5, pe_sk=8, st=1, pe_so=8,
    conv=1, pe_csum=1, cd=1, csq=8, pe_csq=8, cn=1, yb=8,
    merged_zero=1, pe_mg=48, mg=24, mrep=1, pe_out=6, x_updated=6 + 2 * STEPS,
    pe_xt2=8, xnt2=8, pe_wq=8, pq=16, qpad_zero=1, pe_sc=STEPS, score=STEPS,
    stage=STEPS, ids=STEPS, cmax=STEPS, gexp=STEPS, xcur=STEPS,
    dots=GROUPS * STEPS, gel=GROUPS * STEPS, diag=GROUPS * STEPS, v_used=GROUPS * STEPS, offset=1,
)
PRIME = dict(x_updated=1, mg=2, dots=GROUPS, v_used=GROUPS, diag=1)


def at(l, name, k):
    return l * PER[name] + (k + PRIME.get(name, 0))


def build(nc, x_in, consts_in, mem_in, cache_in, state_in, w_in, small_in, rows_in, fing_in, ws_in, wss_in, bs_in,
          keys_in, u_in, v_in, y_out, memk_out, memv_out, convp_out, convs_out, vn_out):
    with ExitStack() as ctx:
        def sb(name, shape, dt=F32):
            return ctx.enter_context(nc.sbuf_tensor(name, shape, dt))

        def sem(name):
            return ctx.enter_context(nc.semaphore(name))

        S = {name: sem("s_" + name) for name in PER}
        w_landed = [sem(f"w_landed{i}") for i in range(4)]
        cache_landed = [sem(f"cache_landed{i}") for i in range(3)]
        u_landed = [sem(f"u_landed{g}") for g in range(GROUPS)]
        v_landed = [sem(f"v_landed{g}") for g in range(GROUPS)]
        x_landed, consts_landed, small_landed, rows_landed = sem("x_landed"), sem("consts_landed"), sem("small_landed"), sem("rows_landed")
        mem_landed, state_landed, ws_landed, bs_landed = sem("mem_landed"), sem("state_landed"), sem("ws_landed"), sem("bs_landed")
        keys_landed, fing_landed = sem("keys_landed"), sem("fing_landed")
        kv_stored, conv_stored, vn_stored, y_stored = sem("kv_stored"), sem("conv_stored"), sem("vn_stored"), sem("y_stored")
        sp_passed, pool_passed, dve_passed, pe_passed = sem("sp_passed"), sem("pool_passed"), sem("dve_passed"), sem("pe_passed")

        arena = sb("arena", [P, 32 * D])
        wbuf = [arena[:, 4096 * s:4096 * (s + 1)].rearrange("p (k c) -> p k c", k=KB) for s in range(4)]
        ubuf = [arena[:, D * i:D * (i + 1)] for i in range(TOPK)]
        vbuf = [arena[:, D * (TOPK + i):D * (TOPK + i + 1)] for i in range(TOPK)]

        base = [TOPK * D]

        def cut(n):
            base[0] += n
            assert base[0] <= 32 * D
            return arena[:, base[0] - n:base[0]]

        ext_region = cut(KB * (PAST + T_P) + KB * NSEQ * (PAST + DSEQ))
        ext_p = ext_region[:, 0:KB * (PAST + T_P)].rearrange("p (c t) -> p c t", c=KB)
        ext_s_flat = ext_region[:, KB * (PAST + T_P):]
        ext_s = ext_s_flat.rearrange("p (c n t) -> p c n t", c=KB, n=NSEQ)
        merged = ext_region[:, 0:KB * 384].rearrange("p (c t) -> p c t", c=KB)
        y_flat = cut(3 * KB * T)
        Y = [y_flat[:, m * KB * T:(m + 1) * KB * T].rearrange("p (c t) -> p c t", c=KB) for m in range(3)]
        yA, yM, yB = Y
        xnT = cut(KB * T).rearrange("p (c t) -> p c t", c=KB)
        sg = cut(2 * T).rearrange("p (b t) -> p b t", b=2)
        rb = cut(T)
        wsT = cut(KB * P).rearrange("p (g t) -> p g t", g=KB)
        qpad = wsT
        wsS = cut(KB * T_S).rearrange("p (g t) -> p g t", g=KB)

        x = sb("x", [P, TILES, D])
        xn_region = sb("xn", [P, 3 * D])
        xn = xn_region[:, :].rearrange("p (t d) -> p t d", t=TILES)
        a_ln_g, a_ln_b = xn_region[:, 0:D], xn_region[:, D:2 * D]
        bsrow = xn_region[0:1, 0:KB * 160].rearrange("p (g t) -> p g t", g=KB)
        prob = xn_region[:, 2 * D:2 * D + 512]
        probT = xn_region[:, 2 * D + 512:3 * D]
        vn_region = sb("vn", [P, 3 * D])
        vn = vn_region[:, :].rearrange("p (t d) -> p t d", t=TILES)
        memT = vn_region[:, 0:KB * M].rearrange("p (c t) -> p c t", c=KB)
        pqT = vn_region[:, 0:KB * T].rearrange("p (c t) -> p c t", c=KB)
        xcur = vn_region[:, 0:D]
        small_r = [KB * T]

        def cut_small(n):
            small_r[0] += n
            assert small_r[0] <= 3 * D
            return vn_region[:, small_r[0] - n:small_r[0]]

        selcur = cut_small(P)
        top_v = cut_small(32)
        top_if = cut_small(32)
        cand_v = cut_small(16)
        ab_f = cut_small(32)
        pick_k = cut_small(32)
        eid_f = cut_small(16)
        gexp = cut_small(16)
        gsum, grec, ncmax = cut_small(1), cut_small(1), cut_small(1)
        gate = cut_small(32)
        hid = cut_small(32)
        gel = cut_small(32)

        kv_region = sb("kv", [P, 4 * D])
        kT = kv_region[:, 0:KB * M].rearrange("p (c t) -> p c t", c=KB)
        vmem = kv_region[:, KB * M:].rearrange("p (m d) -> p m d", m=2)
        keys = kv_region[:, 0:PH * M].rearrange("p (h n) -> p h n", h=PH)
        ffn_g = kv_region[:, 2 * D:3 * D]
        diag = kv_region[:, 3 * D:4 * D].rearrange("p (i c) -> p i c", i=8)

        c_region = sb("cache", [P, 3 * 2 * D])
        cache = [c_region[:, 2 * D * i:2 * D * (i + 1)] for i in range(3)]
        scores = c_region[:, 0:STEPS * 256]
        stg = c_region[:, STEPS * 256:(STEPS + 1) * 256]
        cand = c_region[:, (STEPS + 1) * 256:(STEPS + 2) * 256]
        rest = c_region[:, (STEPS + 2) * 256:(STEPS + 3) * 256]
        onehot = c_region[:, (STEPS + 3) * 256:(STEPS + 5) * 256]

        consts = sb("consts", [P, 3 * P + P + 16])
        ident = consts[:, 0:P]
        ones = consts[:, 3 * P:4 * P]
        iota16 = consts[:, 4 * P:4 * P + 16]
        small = sb("small", [P, KB * CONV_W + 5 * KB])
        wconv = small[:, 0:KB * CONV_W].rearrange("p (c w) -> p c w", c=KB)
        g_mix, g_mem, conv_b, bln_g, bln_b = (small[:, KB * (CONV_W + i):KB * (CONV_W + i + 1)] for i in range(5))
        stat = sb("stat", [P, 40])
        ssq, msq, rt, rstd = (stat[:, 3 * i:3 * i + 3] for i in range(4))
        rsum, rmax, nmax, rinv = (stat[:, 12 + 2 * i:14 + 2 * i] for i in range(4))
        mv = stat[:, 20:26].rearrange("p (t c) -> p t c", t=3)
        bnst = stat[:, 26:38]
        eoff = stat[:, 38:39]
        idx_u = sb("idx_u", [P, 112], U32)
        ids = idx_u[:, 0:32]
        top_i = idx_u[:, 32:64]
        cand_i = idx_u[:, 64:80]
        ab_u = idx_u[:, 80:112]

        bank = [ctx.enter_context(nc.psum_tensor(f"bank{i}", [P, 512], F32)) for i in range(8)]
        block = ctx.enter_context(nc.Block())

        TOK = [(0, 128), (128, 128), (256, 32)]

        @block.sync
        def _(sp):
            sp.dma_start(x[:, :, :], x_in).then_inc(x_landed, 16)
            sp.dma_start(consts[:, :], consts_in).then_inc(consts_landed, 16)
            with sp.Fori(0, DEPTH) as l:
                def rows(ap, per, off, n=P):
                    return ap[bass.ds(l * per + off, n), :]

                def load_w(i):
                    sp.dma_start(arena[:, 4096 * wslot(i):4096 * (wslot(i) + 1)],
                                 rows(w_in, NW * P, i * P)).then_inc(w_landed[wslot(i)], 16)

                def load_cache(i):
                    sp.dma_start(cache[i % 3], rows(cache_in, 16 * P, i * P)).then_inc(cache_landed[i % 3], 16)

                sp.wait_ge(S["x_updated"], at(l, "x_updated", 0))
                sp.dma_start(small[:, :], rows(small_in, P, 0)).then_inc(small_landed, 16)
                load_w(0)
                sp.dma_start(vn_region[:, 0:KB * M], mem_in).then_inc(mem_landed, 16)
                load_w(1)
                sp.dma_start(ext_s_flat, rows(state_in, P, 0)).then_inc(state_landed, 16)
                load_w(2)
                load_w(3)
                sp.wait_ge(S["pe_xt"], at(l, "pe_xt", 8))
                sp.dma_start(xn_region[:, 0:2 * D], rows(rows_in, P, 0)[:, 0:2 * D]).then_inc(rows_landed, 16)
                sp.dma_start(wsT, rows(ws_in, P, 0).rearrange("p (g t) -> p g t", g=KB)).then_inc(ws_landed, 16)
                sp.dma_start(wsS[0:T_S], rows(wss_in, T_S, 0, T_S).rearrange("p (g t) -> p g t", g=KB)).then_inc(ws_landed, 16)
                for i in range(3):
                    load_cache(i)
                freed = [("pe_glu", 4 * (i + 1)) for i in range(4)] + [("pe_mk", 4), ("pe_mk", 8), ("pe_mv", 2), ("pe_mv", 4),
                         ("pe_va", 3), ("pe_va", 6), ("pe_ua", 4), ("pe_ua", 8), ("pe_q", 4), ("pe_q", 8)]
                freed += [("pe_mg", 4 * (i + 1)) for i in range(12)]
                prev = {i: max((j for j in range(i) if wslot(j) == wslot(i)), default=None) for i in range(NW)}

                def load_next(i):
                    name, k = freed[prev[i]]
                    sp.wait_ge(S[name], at(l, name, k))
                    load_w(i)

                for i in range(4, 8):
                    load_next(i)
                sp.wait_ge(S["glu"], at(l, "glu", 16))
                sp.dma_start(rows(convp_out, P, 0).rearrange("p (c t) -> p c t", c=KB),
                             ext_p[:, :, T_P:T_P + PAST]).then_inc(conv_stored, 16)
                sp.dma_start(rows(convs_out, P, 0), ext_s_flat).then_inc(conv_stored, 16)
                for i in range(8, 14):
                    load_next(i)
                sp.wait_ge(S["kv"], at(l, "kv", 12))
                sp.dma_start(rows(memk_out, P, 0), kv_region[:, 0:2 * D]).then_inc(kv_stored, 16)
                sp.dma_start(rows(memv_out, P, 0), kv_region[:, 2 * D:4 * D]).then_inc(kv_stored, 16)
                for i in range(14, 18):
                    load_next(i)
                sp.wait_ge(S["ln_done"], at(l, "ln_done", 3))
                sp.dma_start(rows(vn_out, T_S, 0, T_S), vn[0:T_S, 2, :]).then_inc(vn_stored, 16)
                for i in range(3, 16):
                    name, k = ("pe_sk", i - 2) if i - 3 < 8 else ("pe_so", i - 10)
                    sp.wait_ge(S[name], at(l, name, k))
                    load_cache(i)
                for i in range(18, NW):
                    load_next(i)
                sp.wait_ge(S["o"], at(l, "o", 5))
                sp.sem_inc(sp_passed, 1)
                sp.wait_ge(kv_stored, l * 32 + 32)
                sp.dma_start(kv_region[:, 0:2 * D], rows(keys_in, P, 0)).then_inc(keys_landed, 16)
                sp.dma_start(ffn_g, rows(rows_in, P, 0)[:, 2 * D:3 * D]).then_inc(keys_landed, 16)
            sp.wait_ge(S["x_updated"], DEPTH * PER["x_updated"] + 1)
            sp.dma_start(ffn_g, fing_in).then_inc(fing_landed, 16)
            sp.wait_ge(S["xrows"], DEPTH * PER["xrows"] + 3)
            sp.dma_start(y_out, xn_region[:, :]).then_inc(y_stored, 16)
            sp.wait_ge(kv_stored, DEPTH * 32)
            sp.wait_ge(conv_stored, DEPTH * 32)
            sp.wait_ge(vn_stored, DEPTH * 16)
            sp.wait_ge(y_stored, 16)

        @block.gpsimd
        def _(pool):
            with pool.Fori(0, DEPTH) as l:
                pool.wait_ge(S["x_updated"], at(l, "x_updated", 0))
                pool.sem_inc(pool_passed, 1)
                nc.gpsimd.memset(ext_p[:, :, 0:PAST], 0.0).then_inc(S["past_zero"], 1)
                pool.wait_ge(ws_landed, l * 32 + 32)
                pool.sem_inc(pool_passed, 1)
                nc.gpsimd.affine_select(out=wsT, in_=wsT, compare_op=ALU.is_ge, fill=0.0, base=0,
                                        pattern=[[0, KB], [1, P]], channel_multiplier=-1).then_inc(S["ws_masked"], 1)
                nc.gpsimd.affine_select(out=wsS[0:T_S], in_=wsS[0:T_S], compare_op=ALU.is_ge, fill=0.0, base=0,
                                        pattern=[[0, KB], [1, T_S]], channel_multiplier=-1).then_inc(S["ws_masked"], 1)
                pool.wait_ge(rows_landed, l * 16 + 16)
                for t, n in enumerate((P, P, T_S)):
                    pool.wait_ge(S["ln_norm"], at(l, "ln_norm", t + 1))
                    nc.gpsimd.tensor_tensor(vn[0:n, t], vn[0:n, t], a_ln_g[0:n], ALU.mult).then_inc(S["ln_g"], 1)
                for t, n in enumerate((P, P, T_S)):
                    pool.wait_ge(S["ln_g"], at(l, "ln_g", t + 1))
                    nc.gpsimd.tensor_tensor(vn[0:n, t], vn[0:n, t], a_ln_b[0:n], ALU.add).then_inc(S["ln_done"], 1)
                pool.wait_ge(S["ln_done"], at(l, "ln_done", 3))
                pool.dma_start(xn_region[0:1, 0:KB * 160], bs_in[bass.ds(l, 1), :]).then_inc(bs_landed, 16)
                pool.wait_ge(S["pe_sgu"], at(l, "pe_sgu", 8))
                pool.sem_inc(pool_passed, 1)
                nc.gpsimd.memset(qpad, 0.0).then_inc(S["qpad_zero"], 1)
                pool.wait_ge(S["conv"], at(l, "conv", 1))
                pool.wait_ge(conv_stored, l * 32 + 32)
                pool.sem_inc(pool_passed, 1)
                nc.gpsimd.memset(merged, 0.0).then_inc(S["merged_zero"], 1)

                def gathers(s, q):
                    for g in range(GROUPS):
                        pool.wait_ge(S["ids"], at(l, "ids", s + 1))
                        pool.wait_ge(S["dots"], at(l, "dots", GROUPS * (s - 1) + g + 1))
                        pool.sem_inc(pool_passed, 1)
                        for i in range(4 * g, 4 * g + 4):
                            nc.gpsimd.indirect_dma_start(
                                out=ubuf[i], out_offset=None, in_=u_in,
                                in_offset=bass.IndirectOffsetOnAxis(ap=ids[:, 16 * q + i:16 * q + i + 1], axis=0),
                            ).then_inc(u_landed[g], 16)
                        pool.wait_ge(S["v_used"], at(l, "v_used", GROUPS * (s - 1) + g + 1))
                        pool.sem_inc(pool_passed, 1)
                        for i in range(4 * g, 4 * g + 4):
                            nc.gpsimd.indirect_dma_start(
                                out=vbuf[i], out_offset=None, in_=v_in,
                                in_offset=bass.IndirectOffsetOnAxis(ap=ids[:, 16 * q + i:16 * q + i + 1], axis=0),
                            ).then_inc(v_landed[g], 16)

                with pool.Fori(0, STEPS // 2) as j:
                    for q in range(2):
                        gathers(j * 2 + q, q)

        @block.scalar
        def _(act):
            def A(out, in_, func, name, bias=0.0, scale=1.0, accum=None):
                ins = nc.scalar.activation(out, in_, func, bias=bias, scale=scale, **({} if accum is None else {"accum_out": accum}))
                return ins.then_inc(S[name], 1)

            act.wait_ge(x_landed, 16)
            act.wait_ge(consts_landed, 16)

            def norm_rows(l, which, updated):
                act.wait_ge(S["x_updated"], at(l, "x_updated", updated))
                for t in range(TILES):
                    A(xn[:, t], x[:, t], ACT.Square, "squares", accum=ssq[:, t:t + 1])

            def root(l, out, in_):
                A(out, in_, ACT.Sqrt, "roots")

            with act.Fori(0, DEPTH) as l:
                norm_rows(l, 0, 0)
                act.wait_ge(S["meansq"], at(l, "meansq", 1))
                root(l, rt, msq)
                act.wait_ge(mem_landed, l * 16 + 16)
                for k in range(KB):
                    if k >= 2:
                        act.wait_ge(S["pe_memsq"], at(l, "pe_memsq", k - 1))
                    A(sg[:, k % 2, 0:M], memT[:, k], ACT.Square, "memsq")
                act.wait_ge(S["varsum"], at(l, "varsum", 1))
                root(l, rb[:, 0:M], rb[:, 0:M])
                for c in range(KB):
                    act.wait_ge(S["pe_glu"], at(l, "pe_glu", 2 * c + 1))
                    if c < 2:
                        act.wait_ge(S["pe_memsq"], at(l, "pe_memsq", 8))
                    else:
                        act.wait_ge(S["glu"], at(l, "glu", 2 * (c - 1)))
                    A(sg[:, c % 2], bank[2 * (c % 2)][:, 0:T], ACT.Sigmoid, "sig")
                for b in range(KB):
                    act.wait_ge(S["pe_mk"], at(l, "pe_mk", b + 1))
                    A(kT[:, b], bank[4 + b % 4][:, 0:M], ACT.Copy, "kv")
                for r in range(4):
                    act.wait_ge(S["pe_mv"], at(l, "pe_mv", r + 1))
                    A(vmem[:, r % 2, 512 * (r // 2):512 * (r // 2 + 1)], bank[r][:, :], ACT.Copy, "kv")
                for r in range(6):
                    n = (P, P, T_S)[r % 3]
                    act.wait_ge(S["pe_va"], at(l, "pe_va", r + 1))
                    A(vn[0:n, r % 3, 512 * (r // 3):512 * (r // 3 + 1)], bank[4 + r % 4][0:n, :], ACT.Gelu, "va")
                for b in range(KB):
                    act.wait_ge(S["pe_ua"], at(l, "pe_ua", b + 1))
                    A(yA[:, b], bank[b % 4][:, 0:T], ACT.Gelu, "ua")
                for b in range(KB):
                    act.wait_ge(S["pe_q"], at(l, "pe_q", b + 1))
                    A(yM[:, b], bank[4 + b % 4][:, 0:T], ACT.Copy, "q")
                act.wait_ge(S["lnv_var"], at(l, "lnv_var", 1))
                root(l, rt, msq)
                for h in range(HEADS):
                    act.wait_ge(S["nm"], at(l, "nm", h + 1))
                    if h:
                        act.wait_ge(S["pe_pt"], at(l, "pe_pt", h))
                    for t in range(2):
                        A(prob[:, M * t:M * (t + 1)], bank[4 + h % 2][:, M * t:M * (t + 1)], ACT.Exp, "pexp",
                          bias=nmax[:, t:t + 1], scale=HD ** -0.5, accum=rsum[:, t:t + 1])
                    act.wait_ge(S["pe_pt"], at(l, "pe_pt", h + 1))
                    if h:
                        act.wait_ge(S["pe_o"], at(l, "pe_o", h))
                    A(probT, bank[6][:, :], ACT.Copy, "pt")
                    act.wait_ge(S["pe_o"], at(l, "pe_o", h + 1))
                    A(yM[:, 2 * h:2 * h + 2, 0:T_P], bank[7][:, :].rearrange("p (c t) -> p c t", c=2), ACT.Copy, "o")
                act.wait_ge(S["pe_sk"], at(l, "pe_sk", 8))
                A(prob[:, 0:256], bank[4][:, 0:256], ACT.Copy, "st")
                act.wait_ge(S["nm"], at(l, "nm", 5))
                A(prob[:, 256:512], bank[5][:, 0:256], ACT.Exp, "pexp", bias=nmax[:, 0:1], scale=HD ** -0.5, accum=rsum[:, 0:1])
                act.wait_ge(S["pe_pt"], at(l, "pe_pt", 5))
                A(probT[:, 0:256], bank[6][:, 0:256], ACT.Copy, "pt")
                act.wait_ge(S["pe_so"], at(l, "pe_so", 8))
                A(yM[:, :, T_P:T], bank[7][:, 0:256].rearrange("p (c t) -> p c t", c=KB), ACT.Copy, "o")
                act.wait_ge(S["cd"], at(l, "cd", 1))
                for c in range(KB):
                    if c >= 2:
                        act.wait_ge(S["pe_csq"], at(l, "pe_csq", c - 1))
                    A(sg[:, c % 2], yB[:, c], ACT.Square, "csq")
                act.wait_ge(S["varsum"], at(l, "varsum", 2))
                root(l, rb, rb)
                act.wait_ge(S["cn"], at(l, "cn", 1))
                for c in range(KB):
                    A(yB[:, c], yB[:, c], ACT.Silu, "yb", bias=bln_b[:, c:c + 1], scale=bln_g[:, c:c + 1])
                act.wait_ge(S["pe_csq"], at(l, "pe_csq", 8))
                with act.Fori(0, 3) as m:
                    for c in range(KB):
                        act.wait_ge(S["pe_mg"], at(l, "pe_mg", m * 16 + 2 * c + 1))
                        act.wait_ge(S["mg"], at(l, "mg", m * 8 + c - 1))
                        A(sg[:, c % 2], bank[2 * (c % 2)][:, 0:T], ACT.Sigmoid, "sig")
                norm_rows(l, 1, 6)
                act.wait_ge(S["meansq"], at(l, "meansq", 2))
                root(l, rt, msq)
                for k in range(KB):
                    act.wait_ge(S["pe_xt2"], at(l, "pe_xt2", k + 1))
                    A(xnT[:, k], bank[k % 4][:, 0:T], ACT.Copy, "xnt2")
                act.wait_ge(S["qpad_zero"], at(l, "qpad_zero", 1))
                act.wait_ge(vn_stored, l * 16 + 16)
                for h in range(PH):
                    act.wait_ge(S["pe_wq"], at(l, "pe_wq", h + 1))
                    A(pqT[:, h], bank[4 + h % 4][:, 0:T], ACT.Copy, "pq")
                    j0 = T_S * (h // 2)
                    A(qpad[:, h, j0:j0 + T_S], bank[4 + h % 4][:, T_P:T], ACT.Copy, "pq")
                for s in range(STEPS):
                    act.wait_ge(S["pe_sc"], at(l, "pe_sc", s + 1))
                    A(scores[:, 256 * s:256 * (s + 1)], bank[4 + s % 4][:, 0:256], ACT.Copy, "score")

                def stage(s):
                    act.wait_ge(S["ids"], at(l, "ids", s))
                    A(stg, scores[:, bass.ds(s * 256, 256)] if not isinstance(s, int) else scores[:, 256 * s:256 * (s + 1)], ACT.Copy, "stage")

                def gate_exp(s):
                    act.wait_ge(S["cmax"], at(l, "cmax", s + 1))
                    A(gexp, cand_v, ACT.Exp, "gexp", bias=ncmax, accum=gsum)

                def step(s, q, last):
                    if not last:
                        stage(s + 1)
                    for g in range(GROUPS):
                        act.wait_ge(S["dots"], at(l, "dots", GROUPS * s + g + 1))
                        a = 16 * q + 4 * g
                        A(gel[:, a:a + 4], hid[:, a:a + 4], ACT.Gelu, "gel")
                        if g == 1 and not last:
                            gate_exp(s + 1)

                def tile_of(j):
                    act.wait_ge(S["dots"], at(l, "dots", j * 8))
                    t = j // 4
                    A(xcur, xn_region[:, bass.ds(t * D, D)] if not isinstance(t, int) else xn[:, t], ACT.Copy, "xcur")
                    act.wait_ge(S["diag"], at(l, "diag", j * 8))
                    A(selcur, consts[:, bass.ds(t * P, P)] if not isinstance(t, int) else consts[:, P * t:P * (t + 1)], ACT.Copy, "xcur")

                act.wait_ge(S["score"], at(l, "score", STEPS))
                A(stg, scores[:, 0:256], ACT.Copy, "stage")
                gate_exp(0)
                with act.Fori(0, STEPS // 2 - 1) as j:
                    tile_of(j)
                    step(j * 2, 0, False)
                    step(j * 2 + 1, 1, False)
                tile_of(STEPS // 2 - 1)
                step(STEPS - 2, 0, False)
                step(STEPS - 1, 1, True)
            norm_rows(DEPTH, 0, 0)
            act.wait_ge(S["meansq"], DEPTH * PER["meansq"] + 1)
            root(DEPTH, rt, msq)

        @block.vector
        def _(dve):
            V = nc.vector
            for name in ("x_updated", "mg", "dots", "diag"):
                dve.sem_inc(S[name], PRIME[name])
            V.memset(eoff, 0.0)
            dve.wait_ge(x_landed, 16)
            dve.wait_ge(consts_landed, 16)

            def mean_sq(l, k):
                dve.wait_ge(S["squares"], at(l, "squares", 3 * k))
                V.tensor_scalar(msq, ssq, 1.0 / D, EPS, ALU.mult, ALU.add).then_inc(S["meansq"], 1)

            def one_over_root(l, k):
                dve.wait_ge(S["roots"], at(l, "roots", k))
                V.reciprocal(rstd, rt).then_inc(S["rstd"], 1)
                dve.drain()

            with dve.Fori(0, DEPTH) as l:
                mean_sq(l, 1)
                one_over_root(l, 1)
                for t in range(TILES):
                    V.tensor_scalar(xn[:, t], x[:, t], rstd[:, t:t + 1], None, ALU.mult).then_inc(S["xrows"], 1)
                dve.wait_ge(small_landed, l * 16 + 16)
                for k in range(KB):
                    dve.wait_ge(S["pe_xt"], at(l, "pe_xt", k + 1))
                    V.tensor_scalar(xnT[:, k], bank[k % 4][:, 0:T], g_mix[:, k:k + 1], None, ALU.mult).then_inc(S["xnt"], 1)
                dve.wait_ge(S["pe_memsq"], at(l, "pe_memsq", 8))
                V.tensor_scalar(rb[:, 0:M], bank[4][:, 0:M], 1.0 / D, EPS, ALU.mult, ALU.add).then_inc(S["varsum"], 1)
                dve.wait_ge(S["roots"], at(l, "roots", 2))
                V.reciprocal(rb[:, 0:M], rb[:, 0:M]).then_inc(S["rstd"], 1)
                dve.drain()
                for k in range(KB):
                    V.scalar_tensor_tensor(out=memT[:, k], in0=memT[:, k], scalar=g_mem[:, k:k + 1], in1=rb[:, 0:M],
                                           op0=ALU.mult, op1=ALU.mult).then_inc(S["memn"], 1)
                dve.wait_ge(state_landed, l * 16 + 16)
                for c in range(KB):
                    dve.wait_ge(S["pe_glu"], at(l, "pe_glu", 2 * c + 2))
                    dve.wait_ge(S["sig"], at(l, "sig", c + 1))
                    val = bank[2 * (c % 2) + 1]
                    V.tensor_tensor(ext_p[:, c, PAST:], val[:, 0:T_P], sg[:, c % 2, 0:T_P], ALU.mult).then_inc(S["glu"], 1)
                    V.tensor_tensor(ext_s[:, c, :, PAST:], val[:, T_P:T].rearrange("p (n t) -> p n t", n=NSEQ),
                                    sg[:, c % 2, T_P:T].rearrange("p (n t) -> p n t", n=NSEQ), ALU.mult).then_inc(S["glu"], 1)
                dve.wait_ge(S["past_zero"], at(l, "past_zero", 1))
                dve.sem_inc(dve_passed, 1)
                dve.drain()
                for c0 in (0, 4):
                    for c in range(c0, c0 + 4):
                        V.tensor_scalar(yB[:, c, 0:T_P], ext_p[:, c, 0:T_P], wconv[:, c, 0:1], conv_b[:, c:c + 1], ALU.mult, ALU.add)
                        V.tensor_scalar(yB[:, c, T_P:T].rearrange("p (n t) -> p n t", n=NSEQ), ext_s[:, c, :, 0:DSEQ],
                                        wconv[:, c, 0:1], conv_b[:, c:c + 1], ALU.mult, ALU.add)
                    for w in range(1, CONV_W):
                        dve.drain()
                        for c in range(c0, c0 + 4):
                            V.scalar_tensor_tensor(out=yB[:, c, 0:T_P], in0=ext_p[:, c, w:w + T_P], scalar=wconv[:, c, w:w + 1],
                                                   in1=yB[:, c, 0:T_P], op0=ALU.mult, op1=ALU.add)
                            ys = yB[:, c, T_P:T].rearrange("p (n t) -> p n t", n=NSEQ)
                            ins = V.scalar_tensor_tensor(out=ys, in0=ext_s[:, c, :, w:w + DSEQ], scalar=wconv[:, c, w:w + 1],
                                                         in1=ys, op0=ALU.mult, op1=ALU.add)
                ins.then_inc(S["conv"], 1)
                dve.wait_ge(S["va"], at(l, "va", 6))
                for t, n in enumerate((P, P, T_S)):
                    for i in range(2):
                        V.bn_stats(bnst[0:n, 6 * i:6 * i + 6], vn[0:n, t, 512 * i:512 * (i + 1)])
                    dve.drain()
                    V.bn_aggr(mv[0:n, t], bnst[0:n, :])
                    dve.drain()
                V.memset(msq, 1.0)
                dve.drain()
                for t, n in enumerate((P, P, T_S)):
                    ins = V.tensor_scalar(msq[0:n, t:t + 1], mv[0:n, t, 1:2], 1.0, EPS, ALU.mult, ALU.add)
                ins.then_inc(S["lnv_var"], 1)
                one_over_root(l, 3)
                for t, n in enumerate((P, P, T_S)):
                    V.tensor_scalar(vn[0:n, t], vn[0:n, t], mv[0:n, t, 0:1], rstd[0:n, t:t + 1], ALU.subtract, ALU.mult).then_inc(S["ln_norm"], 1)
                for h in range(HEADS):
                    dve.wait_ge(S["pe_s"], at(l, "pe_s", h + 1))
                    V.tensor_reduce(rmax, bank[4 + h % 2][:, :].rearrange("p (t m) -> p t m", t=2), AX.X, ALU.max)
                    dve.drain()
                    V.tensor_scalar(nmax, rmax, -HD ** -0.5, None, ALU.mult).then_inc(S["nm"], 1)
                    dve.wait_ge(S["pexp"], at(l, "pexp", 2 * h + 2))
                    V.reciprocal(rinv, rsum)
                    dve.drain()
                    pr = prob.rearrange("p (t m) -> p t m", t=2)
                    V.tensor_tensor(pr, pr, rinv.unsqueeze(2).to_broadcast([P, 2, M]), ALU.mult).then_inc(S["p"], 1)
                dve.wait_ge(S["pe_s"], at(l, "pe_s", 5))
                V.tensor_reduce(rmax[:, 0:1], bank[5][:, 0:256], AX.X, ALU.max)
                dve.drain()
                V.tensor_scalar(nmax[:, 0:1], rmax[:, 0:1], -HD ** -0.5, None, ALU.mult).then_inc(S["nm"], 1)
                dve.wait_ge(S["pexp"], at(l, "pexp", 9))
                V.reciprocal(rinv[:, 0:1], rsum[:, 0:1])
                dve.drain()
                V.tensor_scalar(prob[:, 256:512], prob[:, 256:512], rinv[:, 0:1], None, ALU.mult).then_inc(S["p"], 1)
                for g in range(KB):
                    dve.wait_ge(S["pe_sgu"], at(l, "pe_sgu", g + 1))
                    V.tensor_tensor(yA[:, g], yA[:, g], bank[g % 4][:, 0:T], ALU.mult).then_inc(S["ya"], 1)
                dve.wait_ge(S["pe_csum"], at(l, "pe_csum", 1))
                for c in range(KB):
                    ins = V.scalar_tensor_tensor(out=yB[:, c], in0=bank[0][:, 0:T], scalar=-1.0 / D, in1=yB[:, c], op0=ALU.mult, op1=ALU.add)
                ins.then_inc(S["cd"], 1)
                dve.wait_ge(S["pe_csq"], at(l, "pe_csq", 8))
                V.tensor_scalar(rb, bank[1][:, 0:T], 1.0 / D, EPS, ALU.mult, ALU.add).then_inc(S["varsum"], 1)
                dve.wait_ge(S["roots"], at(l, "roots", 4))
                V.reciprocal(rb, rb).then_inc(S["rstd"], 1)
                dve.drain()
                V.tensor_tensor(yB, yB, rb.unsqueeze(1).to_broadcast([P, KB, T]), ALU.mult).then_inc(S["cn"], 1)
                dve.wait_ge(S["merged_zero"], at(l, "merged_zero", 1))
                dve.sem_inc(dve_passed, 1)
                with dve.Fori(0, 3) as m:
                    for c in range(KB):
                        dve.wait_ge(S["pe_mg"], at(l, "pe_mg", m * 16 + 2 * c + 2))
                        dve.wait_ge(S["sig"], at(l, "sig", m * 8 + 8 + c + 1))
                        V.tensor_tensor(sg[:, c % 2], sg[:, c % 2], bank[2 * (c % 2) + 1][:, 0:T], ALU.mult)
                        dve.drain()
                        V.tensor_tensor(merged[:, c, 0:T], merged[:, c, 0:T], sg[:, c % 2], ALU.add).then_inc(S["mg"], 1)
                dve.drain()
                src = merged[:, :, T_P:T].unsqueeze(2).to_broadcast([P, KB, 3, T_S])
                V.tensor_copy(merged[:, :, T:384].rearrange("p c (j t) -> p c j t", j=3), src).then_inc(S["mrep"], 1)
                for r in range(6):
                    dve.wait_ge(S["pe_out"], at(l, "pe_out", r + 1))
                    xs = x[:, r % 3, 512 * (r // 3):512 * (r // 3 + 1)]
                    V.tensor_tensor(xs, xs, bank[4 + r % 4][:, :], ALU.add).then_inc(S["x_updated"], 1)
                dve.drain()
                mean_sq(l, 2)
                one_over_root(l, 5)
                dve.wait_ge(keys_landed, l * 32 + 32)
                for t in range(TILES):
                    V.scalar_tensor_tensor(out=xn[:, t], in0=x[:, t], scalar=rstd[:, t:t + 1], in1=ffn_g,
                                           op0=ALU.mult, op1=ALU.mult).then_inc(S["xrows"], 1)

                def top16(vals, idx, src, scratch):
                    V.max(vals[:, 0:8], src)
                    dve.drain()
                    V.max_index(idx[:, 0:8], vals[:, 0:8], src)
                    V.match_replace(scratch, vals[:, 0:8], src, NEG)
                    dve.drain()
                    V.max(vals[:, 8:16], scratch)
                    dve.drain()
                    V.max_index(idx[:, 8:16], vals[:, 8:16], scratch)

                def picks(s, q):
                    dve.wait_ge(S["stage"], at(l, "stage", s + 1))
                    dve.sem_inc(dve_passed, 1)
                    dve.drain()
                    for half in range(2):
                        top16(top_v[:, 16 * half:16 * half + 16], top_i[:, 16 * half:16 * half + 16],
                              stg[:, NK * half:NK * (half + 1)], rest[:, NK * half:NK * (half + 1)])
                    dve.drain()
                    V.tensor_tensor(cand.rearrange("p (a b) -> p a b", a=16), top_v[:, 0:16].unsqueeze(2).to_broadcast([P, 16, 16]),
                                    top_v[:, 16:32].unsqueeze(1).to_broadcast([P, 16, 16]), ALU.add)
                    V.tensor_copy(top_if, top_i)
                    dve.drain()
                    top16(cand_v, cand_i, cand, rest)
                    dve.drain()
                    V.tensor_scalar(ncmax, cand_v[:, 0:1], -1.0, None, ALU.mult).then_inc(S["cmax"], 1)
                    V.tensor_scalar(ab_u[:, 0:16], cand_i, 4, None, ALU.logical_shift_right)
                    V.tensor_scalar(ab_u[:, 16:32], cand_i, 15, None, ALU.bitwise_and)
                    dve.drain()
                    V.tensor_copy(ab_f, ab_u)
                    dve.drain()
                    oh3 = onehot.rearrange("p (k a) -> p k a", a=16)
                    V.tensor_tensor(oh3, ab_f.unsqueeze(2).to_broadcast([P, 32, 16]),
                                    iota16.unsqueeze(1).to_broadcast([P, 32, 16]), ALU.is_equal)
                    dve.drain()
                    for half in range(2):
                        part = oh3[:, 16 * half:16 * half + 16]
                        V.tensor_tensor(part, part, top_if[:, 16 * half:16 * half + 16].unsqueeze(1).to_broadcast([P, 16, 16]), ALU.mult)
                    dve.drain()
                    V.tensor_reduce(pick_k, oh3, AX.X, ALU.add)
                    dve.drain()
                    V.scalar_tensor_tensor(out=eid_f, in0=pick_k[:, 0:16], scalar=float(NK), in1=pick_k[:, 16:32], op0=ALU.mult, op1=ALU.add)
                    dve.drain()
                    V.tensor_scalar(ids[:, 16 * q:16 * q + 16], eid_f, eoff, None, ALU.add).then_inc(S["ids"], 1)

                def diags(s, q, g):
                    dve.wait_ge(S["gel"], at(l, "gel", GROUPS * s + g + 1))
                    dve.wait_ge(S["v_used"], at(l, "v_used", GROUPS * s + g - 1))
                    for i in range(4):
                        a = 16 * q + 4 * g + i
                        ins = V.tensor_scalar(diag[:, 4 * (g % 2) + i], selcur, gel[:, a:a + 1], gate[:, a:a + 1], ALU.mult, ALU.mult)
                    ins.then_inc(S["diag"], 1)

                def step(s, q, last, tile):
                    dve.wait_ge(S["gexp"], at(l, "gexp", s + 1))
                    V.reciprocal(grec, gsum)
                    dve.drain()
                    V.tensor_scalar(gate[:, 16 * q:16 * q + 16], gexp, grec, None, ALU.mult)
                    dve.drain()
                    for g in range(GROUPS):
                        dve.wait_ge(u_landed[g], l * (64 * STEPS) + (s * 64 + 64))
                        for i in range(4 * g, 4 * g + 4):
                            ins = V.tensor_tensor_reduce(out=ubuf[i], in0=ubuf[i], in1=xcur, scale=1.0, scalar=0.0,
                                                         op0=ALU.mult, op1=ALU.add, accum_out=hid[:, 16 * q + i:16 * q + i + 1])
                        ins.then_inc(S["dots"], 1)
                        if g == 1 and not last:
                            picks(s + 1, 1 - q)
                        if g:
                            diags(s, q, g - 1)
                    diags(s, q, GROUPS - 1)
                    dve.wait_ge(S["v_used"], at(l, "v_used", GROUPS * s + GROUPS))
                    for n in range(2):
                        if isinstance(tile, int):
                            xs = x[:, tile, 512 * n:512 * (n + 1)]
                        else:
                            xs = x[:, :, :].rearrange("p t d -> p (t d)")[:, bass.ds(tile * D + 512 * n, 512)]
                        V.tensor_tensor(xs, xs, bank[2 * q + n][:, :], ALU.add).then_inc(S["x_updated"], 1)
                    dve.drain()

                picks(0, 0)
                with dve.Fori(0, STEPS // 2 - 1) as j:
                    dve.wait_ge(S["xcur"], at(l, "xcur", j * 2 + 2))
                    step(j * 2, 0, False, j // 4)
                    step(j * 2 + 1, 1, False, j // 4)
                dve.wait_ge(S["xcur"], at(l, "xcur", STEPS))
                step(STEPS - 2, 0, False, TILES - 1)
                step(STEPS - 1, 1, True, TILES - 1)
                V.tensor_scalar(eoff, eoff, float(NEXP), None, ALU.add).then_inc(S["offset"], 1)
                dve.drain()
            mean_sq(DEPTH, 1)
            one_over_root(DEPTH, 1)
            dve.wait_ge(fing_landed, 16)
            for t in range(TILES):
                V.scalar_tensor_tensor(out=xn[:, t], in0=x[:, t], scalar=rstd[:, t:t + 1], in1=ffn_g,
                                       op0=ALU.mult, op1=ALU.mult).then_inc(S["xrows"], 1)

        @block.tensor
        def _(pe):
            MM = nc.tensor.matmul
            pe.sem_inc(S["v_used"], PRIME["v_used"])
            pe.wait_ge(consts_landed, 16)

            with pe.Fori(0, DEPTH) as l:
                def tile_in(i):
                    pe.wait_ge(w_landed[wslot(i)], l * (16 * WUSES[wslot(i)]) + 16 * (wuse(i) + 1))
                    return wbuf[wslot(i)]

                def down(out, w, b, rhs):
                    for k in range(KB):
                        ins = MM(out, w[:, k, P * b:P * (b + 1)], rhs[:, k], start=k == 0, stop=k == KB - 1)
                    return ins

                def transposes(rows_done, first, last, name, free):
                    for k in range(KB):
                        if k == 0:
                            pe.wait_ge(S["xrows"], at(l, "xrows", rows_done))
                        if k >= 4:
                            pe.wait_ge(S[free], at(l, free, k - 3))
                        for t, (a, n) in enumerate(TOK):
                            ins = nc.tensor.transpose(bank[k % 4][:, a:a + n], xn[0:n, t, P * k:P * (k + 1)], ident[0:n, 0:n])
                        ins.then_inc(S[name], 1)

                pe.wait_ge(S["x_updated"], at(l, "x_updated", 0))
                transposes(3, None, None, "pe_xt", "xnt")
                for k in range(KB):
                    pe.wait_ge(S["memsq"], at(l, "memsq", k + 1))
                    MM(bank[4][:, 0:M], ones, sg[:, k % 2, 0:M], start=k == 0, stop=k == KB - 1).then_inc(S["pe_memsq"], 1)
                pe.wait_ge(S["xnt"], at(l, "xnt", 8))
                for c in range(KB):
                    if c % 2 == 0:
                        w = tile_in(WFIRST["glu"] + c // 2)
                    if c >= 2:
                        pe.wait_ge(S["glu"], at(l, "glu", 2 * (c - 1)))
                    for v in range(2):
                        down(bank[2 * (c % 2) + v][:, 0:T], w, 2 * (c % 2) + v, xnT).then_inc(S["pe_glu"], 1)
                pe.wait_ge(S["memn"], at(l, "memn", 8))
                for b in range(KB):
                    if b % 4 == 0:
                        w = tile_in(WFIRST["mk"] + b // 4)
                    else:
                        pass
                    if b >= 4:
                        pe.wait_ge(S["kv"], at(l, "kv", b - 3))
                    down(bank[4 + b % 4][:, 0:M], w, b % 4, memT).then_inc(S["pe_mk"], 1)
                pe.wait_ge(S["glu"], at(l, "glu", 16))
                for r in range(4):
                    if r % 2 == 0:
                        w = tile_in(WFIRST["mv"] + r // 2)
                    for k in range(KB):
                        ins = MM(bank[r][:, :], memT[:, k, P * (r % 2):P * (r % 2 + 1)], w[:, k, :], start=k == 0, stop=k == KB - 1)
                    ins.then_inc(S["pe_mv"], 1)
                for r in range(6):
                    if r % 3 == 0:
                        w = tile_in(WFIRST["va"] + r // 3)
                    if r < 4:
                        pe.wait_ge(S["kv"], at(l, "kv", 5 + r))
                    else:
                        pe.wait_ge(S["va"], at(l, "va", r - 3))
                    a, n = TOK[r % 3]
                    for k in range(KB):
                        ins = MM(bank[4 + r % 4][0:n, :], xnT[:, k, a:a + n], w[:, k, :], start=k == 0, stop=k == KB - 1)
                    ins.then_inc(S["pe_va"], 1)
                for b in range(KB):
                    if b % 4 == 0:
                        w = tile_in(WFIRST["ua"] + b // 4)
                    if b < 4:
                        pe.wait_ge(S["kv"], at(l, "kv", 9 + b))
                    else:
                        pe.wait_ge(S["ua"], at(l, "ua", b - 3))
                    down(bank[b % 4][:, 0:T], w, b % 4, xnT).then_inc(S["pe_ua"], 1)
                for b in range(KB):
                    if b % 4 == 0:
                        w = tile_in(WFIRST["q"] + b // 4)
                    if b < 4:
                        pe.wait_ge(S["va"], at(l, "va", 6))
                    else:
                        pe.wait_ge(S["q"], at(l, "q", b - 3))
                    down(bank[4 + b % 4][:, 0:T], w, b % 4, xnT).then_inc(S["pe_q"], 1)
                pe.wait_ge(S["q"], at(l, "q", 8))

                def att_scores(h):
                    if h >= 2:
                        pe.wait_ge(S["pexp"], at(l, "pexp", 2 * (h - 1)))
                    for t in range(2):
                        for d in range(2):
                            ins = MM(bank[4 + h % 2][:, M * t:M * (t + 1)], yM[:, 2 * h + d, P * t:P * (t + 1)], kT[:, 2 * h + d],
                                     start=d == 0, stop=d == 1)
                    ins.then_inc(S["pe_s"], 1)

                att_scores(0)
                for h in range(HEADS):
                    if h + 1 < HEADS:
                        att_scores(h + 1)
                    pe.wait_ge(S["p"], at(l, "p", h + 1))
                    if h:
                        pe.wait_ge(S["pt"], at(l, "pt", h))
                    for m in range(2):
                        for t in range(2):
                            ins = nc.tensor.transpose(bank[6][:, 256 * m + P * t:256 * m + P * (t + 1)],
                                                      prob[:, M * t + P * m:M * t + P * (m + 1)], ident)
                    ins.then_inc(S["pe_pt"], 1)
                    pe.wait_ge(S["pt"], at(l, "pt", h + 1))
                    if h:
                        pe.wait_ge(S["o"], at(l, "o", h))
                    for d in range(2):
                        for m in range(2):
                            ins = MM(bank[7][:, T_P * d:T_P * (d + 1)], vmem[:, m, HD * h + P * d:HD * h + P * (d + 1)],
                                     probT[:, 256 * m:256 * (m + 1)], start=m == 0, stop=m == 1)
                    ins.then_inc(S["pe_o"], 1)
                for n in range(NSEQ):
                    pe.wait_ge(cache_landed[n % 3], l * (16 * (6 if n % 3 == 0 else 5)) + 16 * (n // 3 + 1))
                    kc = cache[n % 3].rearrange("p (c t) -> p c t", c=KB)
                    for h in range(HEADS):
                        for m in range(2):
                            col = 128 * m + 16 * n + 4 * h
                            for d in range(2):
                                ins = MM(bank[4][:, col:col + 4], kc[:, 2 * h + d, P * m:P * (m + 1)],
                                         yM[:, 2 * h + d, T_P + 4 * n:T_P + 4 * n + 4], start=d == 0, stop=d == 1)
                    ins.then_inc(S["pe_sk"], 1)
                pe.wait_ge(S["st"], at(l, "st", 1))
                for m in range(2):
                    ins = nc.tensor.transpose(bank[5][:, P * m:P * (m + 1)], prob[:, P * m:P * (m + 1)], ident)
                ins.then_inc(S["pe_s"], 1)
                pe.wait_ge(S["ln_done"], at(l, "ln_done", 3))
                pe.wait_ge(S["ws_masked"], at(l, "ws_masked", 2))
                pe.wait_ge(bs_landed, l * 16 + 16)
                pe.wait_ge(S["ua"], at(l, "ua", 8))
                for g in range(KB):
                    if g >= 4:
                        pe.wait_ge(S["ya"], at(l, "ya", g - 3))
                    ch = slice(P * g, P * (g + 1))
                    for t in range(2):
                        MM(bank[g % 4][:, P * t:P * (t + 1)], vn[:, t, ch], wsT[:, g], start=True, stop=False)
                        MM(bank[g % 4][:, P * t:P * (t + 1)], ones[0:1, :], bsrow[:, g, 0:P], start=False, stop=True)
                    MM(bank[g % 4][:, T_P:T], vn[0:T_S, 2, ch], wsS[0:T_S, g], start=True, stop=False)
                    MM(bank[g % 4][:, T_P:T], ones[0:1, :], bsrow[:, g, P:160], start=False, stop=True).then_inc(S["pe_sgu"], 1)
                pe.wait_ge(S["p"], at(l, "p", 5))
                pe.wait_ge(S["pt"], at(l, "pt", 4))
                for m in range(2):
                    ins = nc.tensor.transpose(bank[6][:, P * m:P * (m + 1)], prob[:, 256 + P * m:256 + P * (m + 1)], ident)
                ins.then_inc(S["pe_pt"], 1)
                pe.wait_ge(S["pt"], at(l, "pt", 5))
                pe.wait_ge(S["o"], at(l, "o", 4))
                for n in range(NSEQ):
                    i = 8 + n
                    pe.wait_ge(cache_landed[i % 3], l * (16 * (6 if i % 3 == 0 else 5)) + 16 * (i // 3 + 1))
                    vc = cache[i % 3].rearrange("p (m d) -> p m d", m=2)
                    for h in range(HEADS):
                        for d in range(2):
                            col = T_S * (2 * h + d) + 4 * n
                            for m in range(2):
                                ins = MM(bank[7][:, col:col + 4], vc[:, m, HD * h + P * d:HD * h + P * (d + 1)],
                                         probT[:, P * m + 16 * n + 4 * h:P * m + 16 * n + 4 * h + 4], start=m == 0, stop=m == 1)
                    ins.then_inc(S["pe_so"], 1)
                pe.wait_ge(S["conv"], at(l, "conv", 1))
                pe.wait_ge(S["ya"], at(l, "ya", 8))
                for c in range(KB):
                    ins = MM(bank[0][:, 0:T], ones, yB[:, c], start=c == 0, stop=c == KB - 1)
                ins.then_inc(S["pe_csum"], 1)
                for c in range(KB):
                    pe.wait_ge(S["csq"], at(l, "csq", c + 1))
                    MM(bank[1][:, 0:T], ones, sg[:, c % 2], start=c == 0, stop=c == KB - 1).then_inc(S["pe_csq"], 1)
                pe.wait_ge(S["o"], at(l, "o", 5))
                pe.wait_ge(S["varsum"], at(l, "varsum", 2))
                pe.wait_ge(S["yb"], at(l, "yb", 8))
                pe.sem_inc(pe_passed, 1)
                with pe.Fori(0, 3) as m:
                    for c in range(KB):
                        i = WFIRST["merge"] + c // 2
                        if c % 2 == 0:
                            s = wslot(i)
                            pe.wait_ge(w_landed[s], l * (16 * WUSES[s]) + (m * 16 + 16 * (wuse(i) + 1)))
                        pe.wait_ge(S["mg"], at(l, "mg", m * 8 + c - 1))
                        for k in range(KB):
                            ins = MM(bank[2 * (c % 2)][:, 0:T], wbuf[wslot(i)][:, k, 256 * (c % 2):256 * (c % 2) + P], xnT[:, k],
                                     start=k == 0, stop=k == KB - 1)
                        ins.then_inc(S["pe_mg"], 1)
                        for k in range(KB):
                            ins = MM(bank[2 * (c % 2) + 1][:, 0:T], wbuf[wslot(i)][:, k, 256 * (c % 2) + P:256 * (c % 2) + 2 * P],
                                     y_flat[:, bass.ds(m * (KB * T) + k * T, T)], start=k == 0, stop=k == KB - 1)
                        ins.then_inc(S["pe_mg"], 1)
                pe.wait_ge(S["mrep"], at(l, "mrep", 1))
                for r in range(6):
                    if r % 3 == 0:
                        w = tile_in(WFIRST["out"] + r // 3)
                    if r >= 4:
                        pe.wait_ge(S["x_updated"], at(l, "x_updated", r - 3))
                    for k in range(KB):
                        ins = MM(bank[4 + r % 4][:, :], merged[:, k, P * (r % 3):P * (r % 3 + 1)], w[:, k, :], start=k == 0, stop=k == KB - 1)
                    ins.then_inc(S["pe_out"], 1)
                pe.wait_ge(S["mg"], at(l, "mg", 24))
                transposes(6, None, None, "pe_xt2", "xnt2")
                pe.wait_ge(S["xnt2"], at(l, "xnt2", 8))
                pe.wait_ge(S["x_updated"], at(l, "x_updated", 6))
                for b in range(KB):
                    if b % 4 == 0:
                        w = tile_in(WFIRST["wq"] + b // 4)
                    if b >= 4:
                        pe.wait_ge(S["pq"], at(l, "pq", 2 * (b - 3)))
                    down(bank[4 + b % 4][:, 0:T], w, b % 4, xnT).then_inc(S["pe_wq"], 1)
                pe.wait_ge(keys_landed, l * 32 + 32)
                pe.wait_ge(S["pq"], at(l, "pq", 16))
                for s in range(STEPS):
                    if s >= 4:
                        pe.wait_ge(S["score"], at(l, "score", s - 3))
                    out = bank[4 + s % 4][:, 0:256]
                    if s < 2 * PH:
                        t, h = divmod(s, PH)
                        ins = MM(out, pqT[:, h, P * t:P * (t + 1)], keys[:, h], start=True, stop=True)
                    else:
                        for j in range(4):
                            h = 2 * j + s - 2 * PH
                            ins = MM(out, qpad[:, h], keys[:, h], start=j == 0, stop=j == 3)
                    ins.then_inc(S["pe_sc"], 1)

                with pe.Fori(0, STEPS // 2) as j:
                    for q in range(2):
                        s = j * 2 + q
                        pe.wait_ge(S["x_updated"], at(l, "x_updated", s * 2 + 4))
                        for g in range(GROUPS):
                            pe.wait_ge(S["diag"], at(l, "diag", GROUPS * s + g + 1))
                            pe.wait_ge(v_landed[g], l * (64 * STEPS) + (s * 64 + 64))
                            for i in range(4):
                                for n in range(2):
                                    ins = MM(bank[2 * q + n][:, :], diag[:, 4 * (g % 2) + i], vbuf[4 * g + i][:, 512 * n:512 * (n + 1)],
                                             start=g == 0 and i == 0, stop=g == GROUPS - 1 and i == 3)
                            ins.then_inc(S["v_used"], 1)


def kernel(**inputs):
    import concourse.bacc as bacc
    from concourse.bass_utils import run_bass_kernel_spmd

    I = {k: np.asarray(v) for k, v in inputs.items()}
    L = DEPTH

    def cols(w):
        return w.reshape(KB, P, -1).transpose(1, 0, 2)

    xs = I["x_sample"].reshape(T_S, D)
    x_rows = np.stack([I["x_prompt"][0, :P], I["x_prompt"][0, P:], np.concatenate([xs] * 4)], axis=1)

    sel = np.zeros((P, 3, P), np.float32)
    for t in range(2):
        sel[:, t] = np.eye(P)
    sel[:, 2] = np.tile(np.eye(T_S), (4, 4))
    consts = np.concatenate([sel.reshape(P, -1), np.ones((P, P)), np.tile(np.arange(16), (P, 1))], axis=1).astype(np.float32)

    memT = cols(np.ascontiguousarray(I["mem_prompt"][0].T)).reshape(P, -1)
    ck = I["cache_mem_k"].reshape(L, NSEQ, M, HEADS, 2, P).transpose(0, 1, 5, 3, 4, 2).reshape(L, NSEQ, P, -1)
    cv = I["cache_mem_v"].reshape(L, NSEQ, 2, P, D).transpose(0, 1, 3, 2, 4).reshape(L, NSEQ, P, -1)
    cache = np.concatenate([ck, cv], axis=1)
    st = I["state_conv"].reshape(L, NSEQ, PAST, KB, P).transpose(0, 4, 3, 1, 2)
    state = np.concatenate([st, np.zeros(st.shape[:-1] + (DSEQ,), st.dtype)], axis=-1)

    wl = []
    for l in range(L):
        w = cols(I["w_in"][l])
        part = [w[:, :, D * i:D * (i + 1)] for i in range(8)]

        def blocks(a, b):
            return [np.concatenate([y[:, :, P * c:P * (c + 1)] for c in (2 * i, 2 * i + 1) for y in (a, b)], axis=2) for i in range(4)]

        def halves(a):
            return [a[:, :, :512], a[:, :, 512:]]

        tiles = blocks(part[3], part[2])
        tiles += halves(cols(I["w_mem_k"][l])) + halves(cols(I["w_mem_v"][l])) + halves(part[1]) + halves(part[0]) + halves(part[4])
        for g, name in ((part[5], "w_o_a"), (part[7], "w_o_m"), (part[6], "w_o_b")):
            tiles += blocks(g, cols(I[name][l]))
        tiles += halves(cols(I["w_out"][l])) + halves(cols(I["peer_wq"][l]))
        wl.append(np.stack(tiles))
    wall = np.stack(wl)

    def chan(a):
        return a.reshape(L, KB, P).transpose(0, 2, 1)

    wc = I["b_conv_w"].reshape(L, CONV_W, KB, P).transpose(0, 3, 2, 1).reshape(L, P, -1)
    small = np.concatenate([wc] + [chan(I[n]) for n in ("norm_mix_g", "mem_norm_g", "b_conv_b", "b_ln_g", "b_ln_b")], axis=2)
    rows = np.concatenate([I["a_ln_g"], I["a_ln_b"], I["norm_ffn_g"]], axis=1)
    rows = np.broadcast_to(rows[:, None], (L, P, 3 * D))
    fing = np.broadcast_to(I["final_norm_g"][None], (P, D))
    ws = I["a_ws"].transpose(0, 3, 1, 2)
    wss = np.zeros((L, NSEQ, DSEQ, KB, NSEQ, DSEQ), ws.dtype)
    for n in range(NSEQ):
        wss[:, n, :, :, n, :] = ws[:, :DSEQ, :, :DSEQ]
    bs = np.concatenate([I["a_bs"], np.tile(I["a_bs"][:, :, :DSEQ], (1, 1, NSEQ))], axis=2)
    kt = I["peer_keys"].transpose(0, 2, 4, 1, 3)
    keys = np.zeros((L, 2, 64, PH, 2, NK), kt.dtype)
    for half in range(2):
        keys[:, half, :, :, half, :] = kt[:, half]

    arrays = {
        "x_in": x_rows.reshape(P, TILES, D), "consts_in": consts, "mem_in": memT, "cache_in": cache.reshape(-1, 2 * D),
        "state_in": state.reshape(L * P, -1), "w_in": wall.reshape(L * NW * P, -1), "small_in": small.reshape(L * P, -1),
        "rows_in": rows.reshape(L * P, -1), "fing_in": fing, "ws_in": ws.reshape(L * P, -1), "wss_in": wss.reshape(L * T_S, -1),
        "bs_in": bs.reshape(L, -1), "keys_in": keys.reshape(L * P, -1),
        "u_in": I["peer_u"].reshape(-1, D), "v_in": I["peer_v"].reshape(-1, D),
    }
    arrays = {k: np.ascontiguousarray(a) for k, a in arrays.items()}
    outs = {
        "y_out": (P, 3 * D), "memk_out": (L * P, 2 * D), "memv_out": (L * P, 2 * D), "convp_out": (L * P, KB * PAST),
        "convs_out": (L * P, KB * NSEQ * (PAST + DSEQ)), "vn_out": (L * T_S, D),
    }
    nc = bacc.Bacc("TRN2", target_bir_lowering=False, num_devices=1)
    args = {k: nc.dram_tensor(k, a.shape, mybir.dt.from_np(a.dtype), kind="ExternalInput").ap() for k, a in arrays.items()}
    args.update({k: nc.dram_tensor(k, s, F32, kind="ExternalOutput").ap() for k, s in outs.items()})
    build(nc, **args)
    r = run_bass_kernel_spmd(nc, [arrays], core_ids=[0]).results[0]

    y = r["y_out"].reshape(P, TILES, D)
    y_prompt = np.concatenate([y[:, 0], y[:, 1]])[None]
    y_sample = y[:T_S, 2].reshape(NSEQ, DSEQ, D)
    mk = r["memk_out"].reshape(L, P, KB, M).transpose(0, 3, 2, 1).reshape(L, 1, M, HEADS, HD)
    mvv = r["memv_out"].reshape(L, P, 2, D).transpose(0, 2, 1, 3).reshape(L, 1, M, HEADS, HD)
    cp = r["convp_out"].reshape(L, P, KB, PAST).transpose(0, 3, 2, 1).reshape(L, 1, PAST, D)
    cs = r["convs_out"].reshape(L, P, KB, NSEQ, PAST + DSEQ)[..., DSEQ:].transpose(0, 3, 4, 2, 1).reshape(L, NSEQ, PAST, D)
    vn = r["vn_out"].reshape(L, NSEQ, DSEQ, D)
    return tuple(np.ascontiguousarray(a) for a in (y_prompt, y_sample, mk, mvv, cp, cs, vn))
```

```python
from contextlib import ExitStack

import numpy as np
import concourse.bass as bass
from concourse import mybir

F32 = mybir.dt.float32
U32 = mybir.dt.uint32
ALU = mybir.AluOpType
ACT = mybir.ActivationFunctionType
AX = mybir.AxisListType

P = 128
DEPTH = 2
D = 1024
KB = D // P
T_P, T_S = 256, 32
T = T_P + T_S
NSEQ, DSEQ = 8, 4
TILES = 3
CONV_W = 31
PAST = CONV_W - 1
M = 256
HEADS, HD = 4, 256
EPS = 1e-6
PH, NK, TOPK = 8, 128, 16
NEXP = NK * NK
STEPS = 2 * PH + 2
GROUPS = 4
NEG = -3.0e38

WTILES = [("glu", 4), ("mk", 2), ("mv", 2), ("va", 2), ("ua", 2), ("q", 2), ("merge", 12), ("out", 2), ("wq", 2)]
NW = sum(n for _, n in WTILES)
WFIRST = {}
_n = 0
for _kind, _c in WTILES:
    WFIRST[_kind] = _n
    _n += _c


def wslot(i):
    if i < WFIRST["out"]:
        return i % 4
    return (2, 3, 0, 1)[i - WFIRST["out"]]


def wuse(i):
    return sum(wslot(j) == wslot(i) for j in range(i))


WUSES = [sum(wslot(i) == s for i in range(NW)) for s in range(4)]

PER = dict(
    squares=6, meansq=6, roots=9, rstd=9, xrows=6,
    pe_xt=5, xnt=5, memsq=8, pe_memsq=8, varsum=2, memn=8,
    sig=32, pe_glu=16, glu=16, past_zero=1, ws_masked=2,
    pe_mk=8, pe_mv=4, kv=12, pe_va=6, va=6, lnv_var=1, ln_norm=3, ln_g=3, ln_done=3,
    pe_ua=8, ua=8, pe_q=8, q=8, pe_sgu=8, ya=8,
    pe_s=4, nm=5, pexp=9, p=5, pe_pt=5, pt=5, pe_o=4, o=5, qz=8, pe_sk=8, pz=8, pe_so=8, osel=4, pe_ot=1,
    pad_zero=1, conv=1, pe_csum=1, cd=1, csq=8, pe_csq=8, cn=1, yb=8,
    merged_zero=1, pe_mg=48, mg=24, mrep=1, pe_out=6, x_updated=6 + 2 * STEPS,
    pe_xt2=5, xnt2=5, pe_wq=8, pq=16, qpad_zero=1, pe_sc=STEPS, score=STEPS,
    stage=STEPS, ids=STEPS, cmax=STEPS, gexp=STEPS, xcur=STEPS,
    dots=GROUPS * STEPS, gel=GROUPS * STEPS, diag=GROUPS * STEPS, v_used=GROUPS * STEPS, offset=1,
)
PRIME = dict(x_updated=1, mg=2, dots=GROUPS, v_used=GROUPS, diag=1)


def at(l, name, k):
    return l * PER[name] + (k + PRIME.get(name, 0))


def build(nc, x_in, consts_in, mem_in, cache_in, state_in, w_in, small_in, rows_in, fing_in, ws_in, wss_in, bs_in,
          keys_in, uv_in, y_out, memk_out, memv_out, convp_out, convs_out, vn_out):
    with ExitStack() as ctx:
        def sb(name, shape, dt=F32):
            return ctx.enter_context(nc.sbuf_tensor(name, shape, dt))

        def sem(name):
            return ctx.enter_context(nc.semaphore(name))

        S = {name: sem("s_" + name) for name in PER}
        w_landed = [sem(f"w_landed{i}") for i in range(4)]
        cache_landed = [sem(f"cache_landed{i}") for i in range(3)]
        uv_landed = [sem(f"uv_landed{g}") for g in range(GROUPS)]
        x_landed, consts_landed, small_landed, rows_landed = sem("x_landed"), sem("consts_landed"), sem("small_landed"), sem("rows_landed")
        mem_landed, state_landed, ws_landed, bs_landed = sem("mem_landed"), sem("state_landed"), sem("ws_landed"), sem("bs_landed")
        keys_landed, fing_landed = sem("keys_landed"), sem("fing_landed")
        kv_stored, conv_stored, vn_stored, y_stored = sem("kv_stored"), sem("conv_stored"), sem("vn_stored"), sem("y_stored")
        sp_passed, pool_passed, dve_passed, pe_passed = sem("sp_passed"), sem("pool_passed"), sem("dve_passed"), sem("pe_passed")

        arena = sb("arena", [P, 32 * D])
        wbuf = [arena[:, 4096 * s:4096 * (s + 1)].rearrange("p (k c) -> p k c", k=KB) for s in range(4)]
        uvbuf = [arena[:, 8 * D * place + 2 * D * i:8 * D * place + 2 * D * (i + 1)] for place in (1, 2, 0, 3) for i in range(4)]

        base = [TOPK * D]

        def cut(n):
            base[0] += n
            assert base[0] <= 32 * D
            return arena[:, base[0] - n:base[0]]

        ext_region = cut(KB * (PAST + T_P) + KB * NSEQ * (PAST + DSEQ))
        ext_p = ext_region[:, 0:KB * (PAST + T_P)].rearrange("p (c t) -> p c t", c=KB)
        ext_s_flat = ext_region[:, KB * (PAST + T_P):]
        ext_s = ext_s_flat.rearrange("p (c n t) -> p c n t", c=KB, n=NSEQ)
        merged = ext_region[:, 0:KB * 384].rearrange("p (c t) -> p c t", c=KB)
        qz_flat = [ext_region[:, 1152 * b:1152 * (b + 1)] for b in range(2)]
        pz = [ext_region[:, 2304 + 256 * b:2304 + 256 * (b + 1)] for b in range(2)]
        osel = ext_region[:, 2816:3072]
        y_flat = cut(3 * KB * T)
        Y = [y_flat[:, m * KB * T:(m + 1) * KB * T].rearrange("p (c t) -> p c t", c=KB) for m in range(3)]
        yA, yM, yB = Y
        xnT = cut(KB * T).rearrange("p (c t) -> p c t", c=KB)
        sg = cut(2 * T).rearrange("p (b t) -> p b t", b=2)
        rb = cut(T)
        wsT = cut(KB * P).rearrange("p (g t) -> p g t", g=KB)
        qpad = wsT
        wsS = cut(KB * T_S).rearrange("p (g t) -> p g t", g=KB)

        x = sb("x", [P, TILES, D])
        xn_region = sb("xn", [P, 3 * D])
        xn = xn_region[:, :].rearrange("p (t d) -> p t d", t=TILES)
        a_ln_g, a_ln_b = xn_region[:, 0:D], xn_region[:, D:2 * D]
        bsrow = xn_region[0:1, 0:KB * 160].rearrange("p (g t) -> p g t", g=KB)
        prob = xn_region[:, 2 * D:2 * D + 512]
        probT = xn_region[:, 2 * D + 512:3 * D]
        vn_region = sb("vn", [P, 3 * D])
        vn = vn_region[:, :].rearrange("p (t d) -> p t d", t=TILES)
        memT = vn_region[:, 0:KB * M].rearrange("p (c t) -> p c t", c=KB)
        pqT = vn_region[:, 0:KB * T].rearrange("p (c t) -> p c t", c=KB)
        small_r = [KB * T]

        def cut_small(n):
            small_r[0] += n
            assert small_r[0] <= 3 * D
            return vn_region[:, small_r[0] - n:small_r[0]]

        selcur = cut_small(P)
        top_v = cut_small(32)
        top_if = cut_small(32)
        cand_v = cut_small(16)
        ab_f = cut_small(32)
        pick_k = cut_small(32)
        eid_f = cut_small(16)
        gexp = cut_small(16)
        gsum, grec, ncmax = cut_small(1), cut_small(1), cut_small(1)
        gate = cut_small(32)
        hid = cut_small(32)
        gel = cut_small(32)

        kv_region = sb("kv", [P, 4 * D])
        kT = kv_region[:, 0:KB * M].rearrange("p (c t) -> p c t", c=KB)
        vmem = kv_region[:, KB * M:].rearrange("p (m d) -> p m d", m=2)
        keys = kv_region[:, 0:PH * M].rearrange("p (h n) -> p h n", h=PH)
        ffn_g = kv_region[:, 2 * D:3 * D]
        xcur = ffn_g
        diag = kv_region[:, 3 * D:4 * D].rearrange("p (i c) -> p i c", i=8)

        c_region = sb("cache", [P, 3 * 2 * D])
        cache = [c_region[:, 2 * D * i:2 * D * (i + 1)] for i in range(3)]
        scores = c_region[:, 0:STEPS * 256]
        stg = c_region[:, STEPS * 256:(STEPS + 1) * 256]
        cand = c_region[:, (STEPS + 1) * 256:(STEPS + 2) * 256]
        rest = c_region[:, (STEPS + 2) * 256:(STEPS + 3) * 256]
        onehot = c_region[:, (STEPS + 3) * 256:(STEPS + 5) * 256]

        consts = sb("consts", [P, 3 * P + P + 16])
        ident = consts[:, 0:P]
        ones = consts[:, 3 * P:4 * P]
        iota16 = consts[:, 4 * P:4 * P + 16]
        small = sb("small", [P, KB * CONV_W + 5 * KB])
        wconv = small[:, 0:KB * CONV_W].rearrange("p (c w) -> p c w", c=KB)
        g_mix, g_mem, conv_b, bln_g, bln_b = (small[:, KB * (CONV_W + i):KB * (CONV_W + i + 1)] for i in range(5))
        stat = sb("stat", [P, 40])
        ssq, msq, rt, rstd = (stat[:, 3 * i:3 * i + 3] for i in range(4))
        rsum, rmax, nmax, rinv = (stat[:, 12 + 2 * i:14 + 2 * i] for i in range(4))
        mv = stat[:, 20:26].rearrange("p (t c) -> p t c", t=3)
        bnst = stat[:, 26:38]
        eoff = stat[:, 38:39]
        idx_u = sb("idx_u", [P, 112], U32)
        ids = idx_u[:, 0:32]
        top_i = idx_u[:, 32:64]
        cand_i = idx_u[:, 64:80]
        ab_u = idx_u[:, 80:112]

        bank = [ctx.enter_context(nc.psum_tensor(f"bank{i}", [P, 512], F32)) for i in range(8)]
        block = ctx.enter_context(nc.Block())

        XT = [(0, 0, 4, 0), (0, 4, 4, 1), (1, 0, 4, 2), (1, 4, 4, 3), (2, 0, 8, 0)]
        TOK = [(0, 128), (128, 128), (256, 32)]

        def qz_cols(b, n):
            v = qz_flat[b].rearrange("p (h x) -> p h x", h=HEADS)[:, :, 0:256]
            return v.rearrange("p h (d c) -> p h d c", d=2)[:, :, :, 4 * n:4 * n + 4]

        def pz_cols(ap, n):
            return ap.rearrange("p (b c) -> p b c", b=8)[:, :, 4 * n:4 * n + 4]

        @block.sync
        def _(sp):
            sp.dma_start(x[:, :, :], x_in).then_inc(x_landed, 16)
            sp.dma_start(consts[:, :], consts_in).then_inc(consts_landed, 16)
            with sp.Fori(0, DEPTH) as l:
                def rows(ap, per, off, n=P):
                    return ap[bass.ds(l * per + off, n), :]

                def load_w(i):
                    sp.dma_start(arena[:, 4096 * wslot(i):4096 * (wslot(i) + 1)],
                                 rows(w_in, NW * P, i * P)).then_inc(w_landed[wslot(i)], 16)

                def load_cache(i):
                    sp.dma_start(cache[i % 3], rows(cache_in, 16 * P, i * P)).then_inc(cache_landed[i % 3], 16)

                sp.wait_ge(S["x_updated"], at(l, "x_updated", 0))
                sp.dma_start(small[:, :], rows(small_in, P, 0)).then_inc(small_landed, 16)
                load_w(0)
                sp.dma_start(vn_region[:, 0:KB * M], mem_in).then_inc(mem_landed, 16)
                load_w(1)
                sp.dma_start(ext_s_flat, rows(state_in, P, 0)).then_inc(state_landed, 16)
                load_w(2)
                load_w(3)
                sp.wait_ge(S["pe_xt"], at(l, "pe_xt", 5))
                sp.dma_start(xn_region[:, 0:2 * D], rows(rows_in, P, 0)[:, 0:2 * D]).then_inc(rows_landed, 16)
                sp.dma_start(wsT, rows(ws_in, P, 0).rearrange("p (g t) -> p g t", g=KB)).then_inc(ws_landed, 16)
                sp.dma_start(wsS[0:T_S], rows(wss_in, T_S, 0, T_S).rearrange("p (g t) -> p g t", g=KB)).then_inc(ws_landed, 16)
                for i in range(3):
                    load_cache(i)
                freed = [("pe_glu", 4 * (i + 1)) for i in range(4)] + [("pe_mk", 4), ("pe_mk", 8), ("pe_mv", 2), ("pe_mv", 4),
                         ("pe_va", 3), ("pe_va", 6), ("pe_ua", 4), ("pe_ua", 8), ("pe_q", 4), ("pe_q", 8)]
                freed += [("pe_mg", 4 * (i + 1)) for i in range(12)]
                prev = {i: max((j for j in range(i) if wslot(j) == wslot(i)), default=None) for i in range(NW)}

                def load_next(i):
                    name, k = freed[prev[i]]
                    sp.wait_ge(S[name], at(l, name, k))
                    load_w(i)

                for i in range(4, 8):
                    load_next(i)
                sp.wait_ge(S["glu"], at(l, "glu", 16))
                sp.dma_start(rows(convp_out, P, 0).rearrange("p (c t) -> p c t", c=KB),
                             ext_p[:, :, T_P:T_P + PAST]).then_inc(conv_stored, 16)
                sp.dma_start(rows(convs_out, P, 0), ext_s_flat).then_inc(conv_stored, 16)
                for i in range(8, 14):
                    load_next(i)
                sp.wait_ge(S["kv"], at(l, "kv", 12))
                sp.dma_start(rows(memk_out, P, 0), kv_region[:, 0:2 * D]).then_inc(kv_stored, 16)
                sp.dma_start(rows(memv_out, P, 0), kv_region[:, 2 * D:4 * D]).then_inc(kv_stored, 16)
                for i in range(14, 18):
                    load_next(i)
                for i in range(3, 16):
                    name, k = ("pe_sk", i - 2) if i - 3 < 8 else ("pe_so", i - 10)
                    sp.wait_ge(S[name], at(l, name, k))
                    load_cache(i)
                sp.wait_ge(S["ln_done"], at(l, "ln_done", 3))
                sp.dma_start(rows(vn_out, T_S, 0, T_S), vn[0:T_S, 2, :]).then_inc(vn_stored, 16)
                for i in range(18, NW):
                    load_next(i)
                sp.wait_ge(S["o"], at(l, "o", 5))
                sp.sem_inc(sp_passed, 1)
                sp.wait_ge(kv_stored, l * 32 + 32)
                sp.dma_start(kv_region[:, 0:2 * D], rows(keys_in, P, 0)).then_inc(keys_landed, 16)
                sp.dma_start(ffn_g, rows(rows_in, P, 0)[:, 2 * D:3 * D]).then_inc(keys_landed, 16)
            sp.wait_ge(S["x_updated"], DEPTH * PER["x_updated"] + 1)
            sp.dma_start(ffn_g, fing_in).then_inc(fing_landed, 16)
            sp.wait_ge(S["xrows"], DEPTH * PER["xrows"] + 3)
            sp.dma_start(y_out, xn_region[:, :]).then_inc(y_stored, 16)
            sp.wait_ge(kv_stored, DEPTH * 32)
            sp.wait_ge(conv_stored, DEPTH * 32)
            sp.wait_ge(vn_stored, DEPTH * 16)
            sp.wait_ge(y_stored, 16)

        @block.gpsimd
        def _(pool):
            with pool.Fori(0, DEPTH) as l:
                pool.wait_ge(S["x_updated"], at(l, "x_updated", 0))
                pool.sem_inc(pool_passed, 1)
                nc.gpsimd.memset(ext_p[:, :, 0:PAST], 0.0).then_inc(S["past_zero"], 1)
                pool.wait_ge(ws_landed, l * 32 + 32)
                pool.sem_inc(pool_passed, 1)
                nc.gpsimd.affine_select(out=wsT, in_=wsT, compare_op=ALU.is_ge, fill=0.0, base=0,
                                        pattern=[[0, KB], [1, P]], channel_multiplier=-1).then_inc(S["ws_masked"], 1)
                nc.gpsimd.affine_select(out=wsS[0:T_S], in_=wsS[0:T_S], compare_op=ALU.is_ge, fill=0.0, base=0,
                                        pattern=[[0, KB], [1, T_S]], channel_multiplier=-1).then_inc(S["ws_masked"], 1)
                pool.wait_ge(S["conv"], at(l, "conv", 1))
                pool.wait_ge(conv_stored, l * 32 + 32)
                pool.sem_inc(pool_passed, 1)
                nc.gpsimd.memset(ext_region[:, 0:2816], 0.0).then_inc(S["pad_zero"], 1)
                pool.wait_ge(S["pad_zero"], at(l, "pad_zero", 1))
                pool.wait_ge(S["q"], at(l, "q", 8))
                pool.sem_inc(pool_passed, 1)
                for n in range(NSEQ):
                    if n >= 2:
                        pool.wait_ge(S["pe_sk"], at(l, "pe_sk", n - 1))
                        pool.sem_inc(pool_passed, 1)
                        nc.gpsimd.memset(qz_cols(n % 2, n - 2), 0.0)
                    nc.gpsimd.tensor_copy(qz_cols(n % 2, n), yM[:, :, T_P + 4 * n:T_P + 4 * n + 4].rearrange("p (h d) t -> p h d t", h=HEADS)
                                          ).then_inc(S["qz"], 1)
                    if 1 <= n <= 3:
                        t = n - 1
                        r = TOK[t][1]
                        if t == 0:
                            pool.wait_ge(rows_landed, l * 16 + 16)
                        pool.wait_ge(S["ln_norm"], at(l, "ln_norm", t + 1))
                        nc.gpsimd.tensor_tensor(vn[0:r, t], vn[0:r, t], a_ln_g[0:r], ALU.mult).then_inc(S["ln_g"], 1)
                        pool.wait_ge(S["ln_g"], at(l, "ln_g", t + 1))
                        nc.gpsimd.tensor_tensor(vn[0:r, t], vn[0:r, t], a_ln_b[0:r], ALU.add).then_inc(S["ln_done"], 1)
                pool.wait_ge(S["ln_done"], at(l, "ln_done", 3))
                pool.dma_start(xn_region[0:1, 0:KB * 160], bs_in[bass.ds(l, 1), :]).then_inc(bs_landed, 16)
                pool.wait_ge(S["pe_sgu"], at(l, "pe_sgu", 8))
                pool.sem_inc(pool_passed, 1)
                nc.gpsimd.memset(qpad, 0.0).then_inc(S["qpad_zero"], 1)
                pool.wait_ge(S["pt"], at(l, "pt", 5))
                pool.sem_inc(pool_passed, 1)
                for n in range(NSEQ):
                    if n >= 2:
                        pool.wait_ge(S["pe_so"], at(l, "pe_so", n - 1))
                        pool.sem_inc(pool_passed, 1)
                        nc.gpsimd.memset(pz_cols(pz[n % 2], n - 2), 0.0)
                    nc.gpsimd.tensor_copy(pz_cols(pz[n % 2], n), pz_cols(probT[:, 0:256], n)).then_inc(S["pz"], 1)
                pool.wait_ge(S["pe_ot"], at(l, "pe_ot", 1))
                pool.sem_inc(pool_passed, 1)
                nc.gpsimd.memset(merged, 0.0).then_inc(S["merged_zero"], 1)

                def gathers(s, q):
                    for g in range(GROUPS):
                        pool.wait_ge(S["ids"], at(l, "ids", s + 1))
                        pool.wait_ge(S["v_used"], at(l, "v_used", GROUPS * (s - 1) + g + 1))
                        if g == 2:
                            pool.wait_ge(S["pe_wq"], at(l, "pe_wq", 8))
                        if g == 3:
                            pool.wait_ge(S["pe_sc"], at(l, "pe_sc", STEPS))
                        pool.sem_inc(pool_passed, 1)
                        for i in range(4 * g, 4 * g + 4):
                            nc.gpsimd.indirect_dma_start(
                                out=uvbuf[i], out_offset=None, in_=uv_in,
                                in_offset=bass.IndirectOffsetOnAxis(ap=ids[:, 16 * q + i:16 * q + i + 1], axis=0),
                            ).then_inc(uv_landed[g], 16)

                with pool.Fori(0, STEPS // 2) as j:
                    for q in range(2):
                        gathers(j * 2 + q, q)

        @block.scalar
        def _(act):
            def A(out, in_, func, name, bias=0.0, scale=1.0, accum=None):
                ins = nc.scalar.activation(out, in_, func, bias=bias, scale=scale, **({} if accum is None else {"accum_out": accum}))
                return ins.then_inc(S[name], 1)

            act.wait_ge(x_landed, 16)
            act.wait_ge(consts_landed, 16)

            def norm_rows(l, updated, done):
                for t in range(TILES):
                    act.wait_ge(S["x_updated"], at(l, "x_updated", updated(t)))
                    A(xn[:, t], x[:, t], ACT.Square, "squares", accum=ssq[:, t:t + 1])
                for t in range(TILES):
                    act.wait_ge(S["meansq"], at(l, "meansq", done + t + 1))
                    A(rt[:, t:t + 1], msq[:, t:t + 1], ACT.Sqrt, "roots")

            def root(l, out, in_):
                A(out, in_, ACT.Sqrt, "roots")

            with act.Fori(0, DEPTH) as l:
                norm_rows(l, lambda t: 0, 0)
                act.wait_ge(mem_landed, l * 16 + 16)
                for k in range(KB):
                    if k >= 2:
                        act.wait_ge(S["pe_memsq"], at(l, "pe_memsq", k - 1))
                    A(sg[:, k % 2, 0:M], memT[:, k], ACT.Square, "memsq")
                act.wait_ge(S["varsum"], at(l, "varsum", 1))
                root(l, rb[:, 0:M], rb[:, 0:M])
                for c in range(KB):
                    act.wait_ge(S["pe_glu"], at(l, "pe_glu", 2 * c + 1))
                    if c < 2:
                        act.wait_ge(S["pe_memsq"], at(l, "pe_memsq", 8))
                    else:
                        act.wait_ge(S["glu"], at(l, "glu", 2 * (c - 1)))
                    A(sg[:, c % 2], bank[2 * (c % 2)][:, 0:T], ACT.Sigmoid, "sig")
                for b in range(KB):
                    act.wait_ge(S["pe_mk"], at(l, "pe_mk", b + 1))
                    A(kT[:, b], bank[4 + b % 4][:, 0:M], ACT.Copy, "kv")
                for r in range(4):
                    act.wait_ge(S["pe_mv"], at(l, "pe_mv", r + 1))
                    A(vmem[:, r % 2, 512 * (r // 2):512 * (r // 2 + 1)], bank[r][:, :], ACT.Copy, "kv")
                for r in range(6):
                    n = (P, P, T_S)[r % 3]
                    act.wait_ge(S["pe_va"], at(l, "pe_va", r + 1))
                    A(vn[0:n, r % 3, 512 * (r // 3):512 * (r // 3 + 1)], bank[4 + r % 4][0:n, :], ACT.Gelu, "va")
                for b in range(KB):
                    act.wait_ge(S["pe_ua"], at(l, "pe_ua", b + 1))
                    A(yA[:, b], bank[b % 4][:, 0:T], ACT.Gelu, "ua")
                for b in range(KB):
                    act.wait_ge(S["pe_q"], at(l, "pe_q", b + 1))
                    A(yM[:, b], bank[4 + b % 4][:, 0:T], ACT.Copy, "q")
                act.wait_ge(S["lnv_var"], at(l, "lnv_var", 1))
                root(l, rt, msq)
                for h in range(HEADS):
                    act.wait_ge(S["nm"], at(l, "nm", h + 1))
                    if h:
                        act.wait_ge(S["pe_pt"], at(l, "pe_pt", h))
                    for t in range(2):
                        A(prob[:, M * t:M * (t + 1)], bank[4 + h % 2][:, M * t:M * (t + 1)], ACT.Exp, "pexp",
                          bias=nmax[:, t:t + 1], scale=HD ** -0.5, accum=rsum[:, t:t + 1])
                    act.wait_ge(S["pe_pt"], at(l, "pe_pt", h + 1))
                    if h:
                        act.wait_ge(S["pe_o"], at(l, "pe_o", h))
                    A(probT, bank[6][:, :], ACT.Copy, "pt")
                    act.wait_ge(S["pe_o"], at(l, "pe_o", h + 1))
                    A(yM[:, 2 * h:2 * h + 2, 0:T_P], bank[7][:, :].rearrange("p (c t) -> p c t", c=2), ACT.Copy, "o")
                    if h == 2:
                        act.wait_ge(S["cd"], at(l, "cd", 1))
                        for c in range(KB):
                            if c >= 2:
                                act.wait_ge(S["pe_csq"], at(l, "pe_csq", c - 1))
                            A(sg[:, c % 2], yB[:, c], ACT.Square, "csq")
                        act.wait_ge(S["varsum"], at(l, "varsum", 2))
                        root(l, rb, rb)
                act.wait_ge(S["nm"], at(l, "nm", 5))
                A(prob[:, 256:512], bank[3][:, 0:256], ACT.Exp, "pexp", bias=nmax[:, 0:1], scale=HD ** -0.5, accum=rsum[:, 0:1])
                act.wait_ge(S["cn"], at(l, "cn", 1))
                for c in range(KB):
                    A(yB[:, c], yB[:, c], ACT.Silu, "yb", bias=bln_b[:, c:c + 1], scale=bln_g[:, c:c + 1])
                act.wait_ge(S["pe_pt"], at(l, "pe_pt", 5))
                A(probT[:, 0:256], bank[6][:, 0:256], ACT.Copy, "pt")
                act.wait_ge(S["pe_so"], at(l, "pe_so", 8))
                for h in range(HEADS):
                    r = slice(T_S * h, T_S * (h + 1))
                    A(osel[r], bank[4 + h // 2][r, 256 * (h % 2):256 * (h % 2 + 1)], ACT.Copy, "osel")
                act.wait_ge(S["pe_ot"], at(l, "pe_ot", 1))
                A(yM[:, :, T_P:T].rearrange("p (h d) t -> p h d t", h=HEADS),
                  bank[7][:, 0:256].rearrange("p (d h t) -> p h d t", d=2, h=HEADS), ACT.Copy, "o")
                act.wait_ge(S["pe_csq"], at(l, "pe_csq", 8))
                with act.Fori(0, 3) as m:
                    for c in range(KB):
                        act.wait_ge(S["pe_mg"], at(l, "pe_mg", m * 16 + 2 * c + 1))
                        act.wait_ge(S["mg"], at(l, "mg", m * 8 + c - 1))
                        A(sg[:, c % 2], bank[2 * (c % 2)][:, 0:T], ACT.Sigmoid, "sig")
                norm_rows(l, lambda t: 2 * (t + 1), 3)
                for i, (t, k0, nk, b) in enumerate(XT):
                    a, n = TOK[t]
                    act.wait_ge(S["pe_xt2"], at(l, "pe_xt2", i + 1))
                    A(xnT[:, k0:k0 + nk, a:a + n], bank[b][:, 0:nk * n].rearrange("p (k t) -> p k t", k=nk), ACT.Copy, "xnt2")
                def stage(s):
                    act.wait_ge(S["ids"], at(l, "ids", s))
                    A(stg, scores[:, bass.ds(s * 256, 256)] if not isinstance(s, int) else scores[:, 256 * s:256 * (s + 1)], ACT.Copy, "stage")

                def gate_exp(s):
                    act.wait_ge(S["cmax"], at(l, "cmax", s + 1))
                    A(gexp, cand_v, ACT.Exp, "gexp", bias=ncmax, accum=gsum)

                def step(s, q, last):
                    if not last:
                        stage(s + 1)
                    for g in range(GROUPS):
                        act.wait_ge(S["dots"], at(l, "dots", GROUPS * s + g + 1))
                        a = 16 * q + 4 * g
                        A(gel[:, a:a + 4], hid[:, a:a + 4], ACT.Gelu, "gel")
                        if g == 1 and not last:
                            gate_exp(s + 1)

                def tile_of(j):
                    act.wait_ge(S["dots"], at(l, "dots", j * 8))
                    t = j // 4
                    A(xcur, xn_region[:, bass.ds(t * D, D)] if not isinstance(t, int) else xn[:, t], ACT.Copy, "xcur")
                    act.wait_ge(S["diag"], at(l, "diag", j * 8))
                    A(selcur, consts[:, bass.ds(t * P, P)] if not isinstance(t, int) else consts[:, P * t:P * (t + 1)], ACT.Copy, "xcur")

                act.wait_ge(S["qpad_zero"], at(l, "qpad_zero", 1))
                act.wait_ge(vn_stored, l * 16 + 16)
                for h in range(PH):
                    act.wait_ge(S["pe_wq"], at(l, "pe_wq", h + 1))
                    A(pqT[:, h], bank[4 + h % 2][:, 0:T], ACT.Copy, "pq")
                    j0 = T_S * (h // 2)
                    A(qpad[:, h, j0:j0 + T_S], bank[4 + h % 2][:, T_P:T], ACT.Copy, "pq")
                    for t in range(2):
                        s = PH * t + h
                        act.wait_ge(S["pe_sc"], at(l, "pe_sc", 2 * h + t + 1))
                        A(scores[:, 256 * s:256 * (s + 1)], bank[6 + t][:, 0:256], ACT.Copy, "score")
                        if s == 0:
                            act.wait_ge(S["score"], at(l, "score", 1))
                            A(stg, scores[:, 0:256], ACT.Copy, "stage")
                    if h == 1:
                        tile_of(0)
                    if h == 3:
                        gate_exp(0)
                for r in range(2):
                    s = 2 * PH + r
                    act.wait_ge(S["pe_sc"], at(l, "pe_sc", s + 1))
                    A(scores[:, 256 * s:256 * (s + 1)], bank[6 + r][:, 0:256], ACT.Copy, "score")

                act.wait_ge(S["score"], at(l, "score", STEPS))
                with act.Fori(0, STEPS // 2 - 1) as j:
                    step(j * 2, 0, False)
                    step(j * 2 + 1, 1, False)
                    tile_of(j + 1)
                step(STEPS - 2, 0, False)
                step(STEPS - 1, 1, True)
            norm_rows(DEPTH, lambda t: 0, 0)

        @block.vector
        def _(dve):
            V = nc.vector
            for name in ("x_updated", "mg", "dots", "diag"):
                dve.sem_inc(S[name], PRIME[name])
            V.memset(eoff, 0.0)
            dve.wait_ge(x_landed, 16)
            dve.wait_ge(consts_landed, 16)

            def inv_norm(l, k, roots_before):
                for t in range(TILES):
                    dve.wait_ge(S["squares"], at(l, "squares", k + t + 1))
                    V.tensor_scalar(msq[:, t:t + 1], ssq[:, t:t + 1], 1.0 / D, EPS, ALU.mult, ALU.add).then_inc(S["meansq"], 1)
                for t in range(TILES):
                    dve.wait_ge(S["roots"], at(l, "roots", roots_before + t + 1))
                    V.reciprocal(rstd[:, t:t + 1], rt[:, t:t + 1]).then_inc(S["rstd"], 1)
                    dve.drain()
                    yield t

            def one_over_root(l, k):
                dve.wait_ge(S["roots"], at(l, "roots", k))
                V.reciprocal(rstd, rt).then_inc(S["rstd"], 1)
                dve.drain()

            with dve.Fori(0, DEPTH) as l:
                for t in inv_norm(l, 0, 0):
                    V.tensor_scalar(xn[:, t], x[:, t], rstd[:, t:t + 1], None, ALU.mult).then_inc(S["xrows"], 1)
                dve.wait_ge(small_landed, l * 16 + 16)
                for i, (t, k0, nk, b) in enumerate(XT):
                    a, n = TOK[t]
                    dve.wait_ge(S["pe_xt"], at(l, "pe_xt", i + 1))
                    V.tensor_tensor(xnT[:, k0:k0 + nk, a:a + n], bank[b][:, 0:nk * n].rearrange("p (k t) -> p k t", k=nk),
                                    g_mix[:, k0:k0 + nk].unsqueeze(2).to_broadcast([P, nk, n]), ALU.mult).then_inc(S["xnt"], 1)
                dve.wait_ge(S["pe_memsq"], at(l, "pe_memsq", 8))
                V.tensor_scalar(rb[:, 0:M], bank[4][:, 0:M], 1.0 / D, EPS, ALU.mult, ALU.add).then_inc(S["varsum"], 1)
                dve.wait_ge(S["roots"], at(l, "roots", 4))
                V.reciprocal(rb[:, 0:M], rb[:, 0:M]).then_inc(S["rstd"], 1)
                dve.drain()
                for k in range(KB):
                    V.scalar_tensor_tensor(out=memT[:, k], in0=memT[:, k], scalar=g_mem[:, k:k + 1], in1=rb[:, 0:M],
                                           op0=ALU.mult, op1=ALU.mult).then_inc(S["memn"], 1)
                dve.wait_ge(state_landed, l * 16 + 16)
                for c in range(KB):
                    dve.wait_ge(S["pe_glu"], at(l, "pe_glu", 2 * c + 2))
                    dve.wait_ge(S["sig"], at(l, "sig", c + 1))
                    val = bank[2 * (c % 2) + 1]
                    V.tensor_tensor(ext_p[:, c, PAST:], val[:, 0:T_P], sg[:, c % 2, 0:T_P], ALU.mult).then_inc(S["glu"], 1)
                    V.tensor_tensor(ext_s[:, c, :, PAST:], val[:, T_P:T].rearrange("p (n t) -> p n t", n=NSEQ),
                                    sg[:, c % 2, T_P:T].rearrange("p (n t) -> p n t", n=NSEQ), ALU.mult).then_inc(S["glu"], 1)
                dve.wait_ge(S["past_zero"], at(l, "past_zero", 1))
                dve.sem_inc(dve_passed, 1)
                dve.drain()
                for c0 in (0, 4):
                    for c in range(c0, c0 + 4):
                        V.tensor_scalar(yB[:, c, 0:T_P], ext_p[:, c, 0:T_P], wconv[:, c, 0:1], conv_b[:, c:c + 1], ALU.mult, ALU.add)
                        V.tensor_scalar(yB[:, c, T_P:T].rearrange("p (n t) -> p n t", n=NSEQ), ext_s[:, c, :, 0:DSEQ],
                                        wconv[:, c, 0:1], conv_b[:, c:c + 1], ALU.mult, ALU.add)
                    for w in range(1, CONV_W):
                        dve.drain()
                        for c in range(c0, c0 + 4):
                            V.scalar_tensor_tensor(out=yB[:, c, 0:T_P], in0=ext_p[:, c, w:w + T_P], scalar=wconv[:, c, w:w + 1],
                                                   in1=yB[:, c, 0:T_P], op0=ALU.mult, op1=ALU.add)
                            ys = yB[:, c, T_P:T].rearrange("p (n t) -> p n t", n=NSEQ)
                            ins = V.scalar_tensor_tensor(out=ys, in0=ext_s[:, c, :, w:w + DSEQ], scalar=wconv[:, c, w:w + 1],
                                                         in1=ys, op0=ALU.mult, op1=ALU.add)
                ins.then_inc(S["conv"], 1)
                dve.wait_ge(S["va"], at(l, "va", 6))
                for t, n in enumerate((P, P, T_S)):
                    for i in range(2):
                        V.bn_stats(bnst[0:n, 6 * i:6 * i + 6], vn[0:n, t, 512 * i:512 * (i + 1)])
                    dve.drain()
                    V.bn_aggr(mv[0:n, t], bnst[0:n, :])
                    dve.drain()
                V.memset(msq, 1.0)
                dve.drain()
                for t, n in enumerate((P, P, T_S)):
                    ins = V.tensor_scalar(msq[0:n, t:t + 1], mv[0:n, t, 1:2], 1.0, EPS, ALU.mult, ALU.add)
                ins.then_inc(S["lnv_var"], 1)
                one_over_root(l, 5)
                for t, n in enumerate((P, P, T_S)):
                    V.tensor_scalar(vn[0:n, t], vn[0:n, t], mv[0:n, t, 0:1], rstd[0:n, t:t + 1], ALU.subtract, ALU.mult).then_inc(S["ln_norm"], 1)
                def att_max(h):
                    dve.wait_ge(S["pe_s"], at(l, "pe_s", h + 1))
                    V.tensor_reduce(rmax, bank[4 + h % 2][:, :].rearrange("p (t m) -> p t m", t=2), AX.X, ALU.max)
                    dve.drain()
                    V.tensor_scalar(nmax, rmax, -HD ** -0.5, None, ALU.mult).then_inc(S["nm"], 1)

                def att_norm(h):
                    dve.wait_ge(S["pexp"], at(l, "pexp", 2 * h + 2))
                    V.reciprocal(rinv, rsum)
                    dve.drain()
                    pr = prob.rearrange("p (t m) -> p t m", t=2)
                    V.tensor_tensor(pr, pr, rinv.unsqueeze(2).to_broadcast([P, 2, M]), ALU.mult).then_inc(S["p"], 1)

                att_max(0)
                att_norm(0)
                dve.wait_ge(S["pe_csum"], at(l, "pe_csum", 1))
                for c in range(KB):
                    ins = V.scalar_tensor_tensor(out=yB[:, c], in0=bank[0][:, 0:T], scalar=-1.0 / D, in1=yB[:, c], op0=ALU.mult, op1=ALU.add)
                ins.then_inc(S["cd"], 1)
                for h in (1, 2):
                    att_max(h)
                    att_norm(h)
                dve.wait_ge(S["pe_csq"], at(l, "pe_csq", 8))
                V.tensor_scalar(rb, bank[1][:, 0:T], 1.0 / D, EPS, ALU.mult, ALU.add).then_inc(S["varsum"], 1)
                att_max(3)
                att_norm(3)
                dve.wait_ge(S["roots"], at(l, "roots", 6))
                V.reciprocal(rb, rb).then_inc(S["rstd"], 1)
                dve.drain()
                V.tensor_tensor(yB, yB, rb.unsqueeze(1).to_broadcast([P, KB, T]), ALU.mult).then_inc(S["cn"], 1)
                dve.wait_ge(S["pe_sk"], at(l, "pe_sk", 8))
                V.tensor_reduce(rmax[:, 0:1], bank[3][:, 0:256], AX.X, ALU.max)
                dve.drain()
                V.tensor_scalar(nmax[:, 0:1], rmax[:, 0:1], -HD ** -0.5, None, ALU.mult).then_inc(S["nm"], 1)
                dve.wait_ge(S["pexp"], at(l, "pexp", 9))
                V.reciprocal(rinv[:, 0:1], rsum[:, 0:1])
                dve.drain()
                V.tensor_scalar(prob[:, 256:512], prob[:, 256:512], rinv[:, 0:1], None, ALU.mult).then_inc(S["p"], 1)
                for g in range(KB):
                    dve.wait_ge(S["pe_sgu"], at(l, "pe_sgu", g + 1))
                    V.tensor_tensor(yA[:, g], yA[:, g], bank[g % 3][:, 0:T], ALU.mult).then_inc(S["ya"], 1)
                dve.wait_ge(S["merged_zero"], at(l, "merged_zero", 1))
                dve.sem_inc(dve_passed, 1)
                with dve.Fori(0, 3) as m:
                    for c in range(KB):
                        dve.wait_ge(S["pe_mg"], at(l, "pe_mg", m * 16 + 2 * c + 2))
                        dve.wait_ge(S["sig"], at(l, "sig", m * 8 + 8 + c + 1))
                        V.tensor_tensor(sg[:, c % 2], sg[:, c % 2], bank[2 * (c % 2) + 1][:, 0:T], ALU.mult)
                        dve.drain()
                        V.tensor_tensor(merged[:, c, 0:T], merged[:, c, 0:T], sg[:, c % 2], ALU.add).then_inc(S["mg"], 1)
                dve.drain()
                src = merged[:, :, T_P:T].unsqueeze(2).to_broadcast([P, KB, 3, T_S])
                V.tensor_copy(merged[:, :, T:384].rearrange("p c (j t) -> p c j t", j=3), src).then_inc(S["mrep"], 1)
                for r in range(6):
                    dve.wait_ge(S["pe_out"], at(l, "pe_out", r + 1))
                    xs = x[:, r // 2, 512 * (r % 2):512 * (r % 2 + 1)]
                    V.tensor_tensor(xs, xs, bank[4 + r % 4][:, :], ALU.add).then_inc(S["x_updated"], 1)
                dve.wait_ge(keys_landed, l * 32 + 32)
                for t in inv_norm(l, 3, 6):
                    V.scalar_tensor_tensor(out=xn[:, t], in0=x[:, t], scalar=rstd[:, t:t + 1], in1=ffn_g,
                                           op0=ALU.mult, op1=ALU.mult).then_inc(S["xrows"], 1)

                def top16(vals, idx, src, scratch):
                    V.max(vals[:, 0:8], src)
                    dve.drain()
                    V.max_index(idx[:, 0:8], vals[:, 0:8], src)
                    V.match_replace(scratch, vals[:, 0:8], src, NEG)
                    dve.drain()
                    V.max(vals[:, 8:16], scratch)
                    dve.drain()
                    V.max_index(idx[:, 8:16], vals[:, 8:16], scratch)

                def pick_halves(s):
                    dve.wait_ge(S["stage"], at(l, "stage", s + 1))
                    dve.sem_inc(dve_passed, 1)
                    dve.drain()
                    for half in range(2):
                        top16(top_v[:, 16 * half:16 * half + 16], top_i[:, 16 * half:16 * half + 16],
                              stg[:, NK * half:NK * (half + 1)], rest[:, NK * half:NK * (half + 1)])
                    dve.drain()
                    V.tensor_tensor(cand.rearrange("p (a b) -> p a b", a=16), top_v[:, 0:16].unsqueeze(2).to_broadcast([P, 16, 16]),
                                    top_v[:, 16:32].unsqueeze(1).to_broadcast([P, 16, 16]), ALU.add)
                    V.tensor_copy(top_if, top_i)
                    dve.drain()

                def pick_experts(q):
                    top16(cand_v, cand_i, cand, rest)
                    dve.drain()
                    V.tensor_scalar(ncmax, cand_v[:, 0:1], -1.0, None, ALU.mult).then_inc(S["cmax"], 1)
                    V.tensor_scalar(ab_u[:, 0:16], cand_i, 4, None, ALU.logical_shift_right)
                    V.tensor_scalar(ab_u[:, 16:32], cand_i, 15, None, ALU.bitwise_and)
                    dve.drain()
                    V.tensor_copy(ab_f, ab_u)
                    dve.drain()
                    oh3 = onehot.rearrange("p (k a) -> p k a", a=16)
                    V.tensor_tensor(oh3, ab_f.unsqueeze(2).to_broadcast([P, 32, 16]),
                                    iota16.unsqueeze(1).to_broadcast([P, 32, 16]), ALU.is_equal)
                    dve.drain()
                    for half in range(2):
                        part = oh3[:, 16 * half:16 * half + 16]
                        V.tensor_tensor(part, part, top_if[:, 16 * half:16 * half + 16].unsqueeze(1).to_broadcast([P, 16, 16]), ALU.mult)
                    dve.drain()
                    V.tensor_reduce(pick_k, oh3, AX.X, ALU.add)
                    dve.drain()
                    V.scalar_tensor_tensor(out=eid_f, in0=pick_k[:, 0:16], scalar=float(NK), in1=pick_k[:, 16:32], op0=ALU.mult, op1=ALU.add)
                    dve.drain()
                    V.tensor_scalar(ids[:, 16 * q:16 * q + 16], eid_f, eoff, None, ALU.add).then_inc(S["ids"], 1)

                def diags(s, q, g):
                    dve.wait_ge(S["gel"], at(l, "gel", GROUPS * s + g + 1))
                    dve.wait_ge(S["v_used"], at(l, "v_used", GROUPS * s + g - 1))
                    for i in range(4):
                        a = 16 * q + 4 * g + i
                        ins = V.tensor_scalar(diag[:, 4 * (g % 2) + i], selcur, gel[:, a:a + 1], gate[:, a:a + 1], ALU.mult, ALU.mult)
                    ins.then_inc(S["diag"], 1)

                def gates(s, q):
                    dve.wait_ge(S["gexp"], at(l, "gexp", s + 1))
                    V.reciprocal(grec, gsum)
                    dve.drain()
                    V.tensor_scalar(gate[:, 16 * q:16 * q + 16], gexp, grec, None, ALU.mult)
                    dve.drain()

                def dots(s, q, g):
                    dve.wait_ge(uv_landed[g], l * (64 * STEPS) + (s * 64 + 64))
                    for i in range(4 * g, 4 * g + 4):
                        ins = V.tensor_tensor_reduce(out=uvbuf[i][:, 0:D], in0=uvbuf[i][:, 0:D], in1=xcur, scale=1.0, scalar=0.0,
                                                     op0=ALU.mult, op1=ALU.add, accum_out=hid[:, 16 * q + i:16 * q + i + 1])
                    ins.then_inc(S["dots"], 1)

                def add_share(s, q, tile):
                    dve.wait_ge(S["v_used"], at(l, "v_used", GROUPS * s + GROUPS))
                    for n in range(2):
                        if isinstance(tile, int):
                            xs = x[:, tile, 512 * n:512 * (n + 1)]
                        else:
                            xs = x[:, :, :].rearrange("p t d -> p (t d)")[:, bass.ds(tile * D + 512 * n, 512)]
                        V.tensor_tensor(xs, xs, bank[2 * q + n][:, :], ALU.add).then_inc(S["x_updated"], 1)
                    dve.drain()

                def step(s, q, last, before=None):
                    dots(s, q, 0)
                    if not last:
                        pick_halves(s + 1)
                    diags(s, q, 0)
                    dots(s, q, 1)
                    if not last:
                        pick_experts(1 - q)
                    diags(s, q, 1)
                    dots(s, q, 2)
                    if before is not None:
                        add_share(*before)
                    diags(s, q, 2)
                    dots(s, q, 3)
                    if not last:
                        gates(s + 1, 1 - q)
                    diags(s, q, 3)

                def pair(j, last):
                    s = j * 2
                    tile = j // 4
                    dve.wait_ge(S["xcur"], at(l, "xcur", j * 2 + 2))
                    step(s, 0, False)
                    step(s + 1, 1, last, (s, 0, tile))
                    add_share(s + 1, 1, tile)

                pick_halves(0)
                pick_experts(0)
                gates(0, 0)
                with dve.Fori(0, STEPS // 2 - 1) as j:
                    pair(j, False)
                pair(STEPS // 2 - 1, True)
                V.tensor_scalar(eoff, eoff, float(NEXP), None, ALU.add).then_inc(S["offset"], 1)
                dve.drain()
            dve.wait_ge(fing_landed, 16)
            for t in inv_norm(DEPTH, 0, 0):
                V.scalar_tensor_tensor(out=xn[:, t], in0=x[:, t], scalar=rstd[:, t:t + 1], in1=ffn_g,
                                       op0=ALU.mult, op1=ALU.mult).then_inc(S["xrows"], 1)

        @block.tensor
        def _(pe):
            MM = nc.tensor.matmul
            pe.sem_inc(S["v_used"], PRIME["v_used"])
            pe.wait_ge(consts_landed, 16)

            with pe.Fori(0, DEPTH) as l:
                def tile_in(i):
                    pe.wait_ge(w_landed[wslot(i)], l * (16 * WUSES[wslot(i)]) + 16 * (wuse(i) + 1))
                    return wbuf[wslot(i)]

                def down(out, w, b, rhs):
                    for k in range(KB):
                        ins = MM(out, w[:, k, P * b:P * (b + 1)], rhs[:, k], start=k == 0, stop=k == KB - 1)
                    return ins

                def transposes(rows_before, name, free):
                    for i, (t, k0, nk, b) in enumerate(XT):
                        n = TOK[t][1]
                        pe.wait_ge(S["xrows"], at(l, "xrows", rows_before + t + 1))
                        if i == 4:
                            pe.wait_ge(S[free], at(l, free, 1))
                            pe.sem_inc(pe_passed, 1)
                        for k in range(nk):
                            ins = nc.tensor.transpose(bank[b][:, n * k:n * (k + 1)], xn[0:n, t, P * (k0 + k):P * (k0 + k + 1)], ident[0:n, 0:n])
                        ins.then_inc(S[name], 1)

                pe.wait_ge(S["x_updated"], at(l, "x_updated", 0))
                transposes(0, "pe_xt", "xnt")
                for k in range(KB):
                    pe.wait_ge(S["memsq"], at(l, "memsq", k + 1))
                    MM(bank[4][:, 0:M], ones, sg[:, k % 2, 0:M], start=k == 0, stop=k == KB - 1).then_inc(S["pe_memsq"], 1)
                pe.wait_ge(S["xnt"], at(l, "xnt", 5))
                for c in range(KB):
                    if c % 2 == 0:
                        w = tile_in(WFIRST["glu"] + c // 2)
                    if c >= 2:
                        pe.wait_ge(S["glu"], at(l, "glu", 2 * (c - 1)))
                    for v in range(2):
                        down(bank[2 * (c % 2) + v][:, 0:T], w, 2 * (c % 2) + v, xnT).then_inc(S["pe_glu"], 1)
                pe.wait_ge(S["memn"], at(l, "memn", 8))
                for b in range(KB):
                    if b % 4 == 0:
                        w = tile_in(WFIRST["mk"] + b // 4)
                    else:
                        pass
                    if b >= 4:
                        pe.wait_ge(S["kv"], at(l, "kv", b - 3))
                    down(bank[4 + b % 4][:, 0:M], w, b % 4, memT).then_inc(S["pe_mk"], 1)
                pe.wait_ge(S["glu"], at(l, "glu", 16))
                for r in range(4):
                    if r % 2 == 0:
                        w = tile_in(WFIRST["mv"] + r // 2)
                    for k in range(KB):
                        ins = MM(bank[r][:, :], memT[:, k, P * (r % 2):P * (r % 2 + 1)], w[:, k, :], start=k == 0, stop=k == KB - 1)
                    ins.then_inc(S["pe_mv"], 1)
                for r in range(6):
                    if r % 3 == 0:
                        w = tile_in(WFIRST["va"] + r // 3)
                    if r < 4:
                        pe.wait_ge(S["kv"], at(l, "kv", 5 + r))
                    else:
                        pe.wait_ge(S["va"], at(l, "va", r - 3))
                    a, n = TOK[r % 3]
                    for k in range(KB):
                        ins = MM(bank[4 + r % 4][0:n, :], xnT[:, k, a:a + n], w[:, k, :], start=k == 0, stop=k == KB - 1)
                    ins.then_inc(S["pe_va"], 1)
                for b in range(KB):
                    if b % 4 == 0:
                        w = tile_in(WFIRST["ua"] + b // 4)
                    if b < 4:
                        pe.wait_ge(S["kv"], at(l, "kv", 9 + b))
                    else:
                        pe.wait_ge(S["ua"], at(l, "ua", b - 3))
                    down(bank[b % 4][:, 0:T], w, b % 4, xnT).then_inc(S["pe_ua"], 1)
                for b in range(KB):
                    if b % 4 == 0:
                        w = tile_in(WFIRST["q"] + b // 4)
                    if b < 4:
                        pe.wait_ge(S["va"], at(l, "va", 6))
                    else:
                        pe.wait_ge(S["q"], at(l, "q", b - 3))
                    down(bank[4 + b % 4][:, 0:T], w, b % 4, xnT).then_inc(S["pe_q"], 1)
                pe.wait_ge(S["q"], at(l, "q", 8))

                def att_scores(h):
                    if h >= 2:
                        pe.wait_ge(S["pexp"], at(l, "pexp", 2 * (h - 1)))
                    for t in range(2):
                        for d in range(2):
                            ins = MM(bank[4 + h % 2][:, M * t:M * (t + 1)], yM[:, 2 * h + d, P * t:P * (t + 1)], kT[:, 2 * h + d],
                                     start=d == 0, stop=d == 1)
                    ins.then_inc(S["pe_s"], 1)

                def att_out(h):
                    pe.wait_ge(S["p"], at(l, "p", h + 1))
                    if h:
                        pe.wait_ge(S["pt"], at(l, "pt", h))
                    for m in range(2):
                        for t in range(2):
                            ins = nc.tensor.transpose(bank[6][:, 256 * m + P * t:256 * m + P * (t + 1)],
                                                      prob[:, M * t + P * m:M * t + P * (m + 1)], ident)
                    ins.then_inc(S["pe_pt"], 1)

                def att_out2(h):
                    pe.wait_ge(S["pt"], at(l, "pt", h + 1))
                    if h:
                        pe.wait_ge(S["o"], at(l, "o", h))
                    for d in range(2):
                        for m in range(2):
                            ins = MM(bank[7][:, T_P * d:T_P * (d + 1)], vmem[:, m, HD * h + P * d:HD * h + P * (d + 1)],
                                     probT[:, 256 * m:256 * (m + 1)], start=m == 0, stop=m == 1)
                    ins.then_inc(S["pe_o"], 1)

                def sample_scores(n):
                    pe.wait_ge(S["qz"], at(l, "qz", n + 1))
                    pe.wait_ge(cache_landed[n % 3], l * (16 * (6 if n % 3 == 0 else 5)) + 16 * (n // 3 + 1))
                    kc = cache[n % 3].rearrange("p (c t) -> p c t", c=KB)
                    for c in range(KB):
                        ins = MM(bank[3][:, 0:M], qz_flat[n % 2][:, P * c:P * (c + 1)], kc[:, c],
                                 start=n == 0 and c == 0, stop=n == NSEQ - 1 and c == KB - 1)
                    ins.then_inc(S["pe_sk"], 1)

                pe.wait_ge(S["ua"], at(l, "ua", 8))
                att_scores(0)
                att_scores(1)
                sample_scores(0)
                sample_scores(1)
                att_out(0)
                pe.wait_ge(S["conv"], at(l, "conv", 1))
                for c in range(KB):
                    ins = MM(bank[0][:, 0:T], ones, yB[:, c], start=c == 0, stop=c == KB - 1)
                ins.then_inc(S["pe_csum"], 1)
                att_out2(0)
                att_scores(2)
                sample_scores(2)
                att_out(1)
                sample_scores(3)
                att_out2(1)
                att_scores(3)
                sample_scores(4)
                att_out(2)
                sample_scores(5)
                att_out2(2)
                for c in range(KB):
                    pe.wait_ge(S["csq"], at(l, "csq", c + 1))
                    MM(bank[1][:, 0:T], ones, sg[:, c % 2], start=c == 0, stop=c == KB - 1).then_inc(S["pe_csq"], 1)
                sample_scores(6)
                att_out(3)
                sample_scores(7)
                att_out2(3)
                pe.wait_ge(S["ln_done"], at(l, "ln_done", 3))
                pe.wait_ge(S["ws_masked"], at(l, "ws_masked", 2))
                pe.wait_ge(bs_landed, l * 16 + 16)
                pe.wait_ge(S["varsum"], at(l, "varsum", 2))
                for g in range(KB):
                    if g >= 3:
                        pe.wait_ge(S["ya"], at(l, "ya", g - 2))
                    ch = slice(P * g, P * (g + 1))
                    out = bank[g % 3]
                    for t in range(2):
                        MM(out[:, P * t:P * (t + 1)], vn[:, t, ch], wsT[:, g], start=True, stop=False)
                        MM(out[:, P * t:P * (t + 1)], ones[0:1, :], bsrow[:, g, 0:P], start=False, stop=True)
                    MM(out[:, T_P:T], vn[0:T_S, 2, ch], wsS[0:T_S, g], start=True, stop=False)
                    MM(out[:, T_P:T], ones[0:1, :], bsrow[:, g, P:160], start=False, stop=True).then_inc(S["pe_sgu"], 1)
                pe.wait_ge(S["p"], at(l, "p", 5))
                pe.wait_ge(S["pt"], at(l, "pt", 4))
                for m in range(2):
                    ins = nc.tensor.transpose(bank[6][:, P * m:P * (m + 1)], prob[:, 256 + P * m:256 + P * (m + 1)], ident)
                ins.then_inc(S["pe_pt"], 1)
                for n in range(NSEQ):
                    i = 8 + n
                    pe.wait_ge(S["pz"], at(l, "pz", n + 1))
                    pe.wait_ge(cache_landed[i % 3], l * (16 * (6 if i % 3 == 0 else 5)) + 16 * (i // 3 + 1))
                    vc = cache[i % 3].rearrange("p (m d) -> p m d", m=2)
                    for m in range(2):
                        for f in range(2):
                            ins = MM(bank[4 + f][:, :], pz[n % 2][:, P * m:P * (m + 1)], vc[:, m, 512 * f:512 * (f + 1)],
                                     start=n == 0 and m == 0, stop=n == NSEQ - 1 and m == 1)
                    ins.then_inc(S["pe_so"], 1)
                pe.wait_ge(S["osel"], at(l, "osel", 4))
                pe.wait_ge(S["o"], at(l, "o", 4))
                for d in range(2):
                    ins = nc.tensor.transpose(bank[7][:, P * d:P * (d + 1)], osel[:, P * d:P * (d + 1)], ident)
                ins.then_inc(S["pe_ot"], 1)
                pe.wait_ge(S["o"], at(l, "o", 5))
                pe.wait_ge(S["ya"], at(l, "ya", 8))
                pe.wait_ge(S["yb"], at(l, "yb", 8))
                pe.sem_inc(pe_passed, 1)
                with pe.Fori(0, 3) as m:
                    for c in range(KB):
                        i = WFIRST["merge"] + c // 2
                        if c % 2 == 0:
                            s = wslot(i)
                            pe.wait_ge(w_landed[s], l * (16 * WUSES[s]) + (m * 16 + 16 * (wuse(i) + 1)))
                        pe.wait_ge(S["mg"], at(l, "mg", m * 8 + c - 1))
                        for k in range(KB):
                            ins = MM(bank[2 * (c % 2)][:, 0:T], wbuf[wslot(i)][:, k, 256 * (c % 2):256 * (c % 2) + P], xnT[:, k],
                                     start=k == 0, stop=k == KB - 1)
                        ins.then_inc(S["pe_mg"], 1)
                        for k in range(KB):
                            ins = MM(bank[2 * (c % 2) + 1][:, 0:T], wbuf[wslot(i)][:, k, 256 * (c % 2) + P:256 * (c % 2) + 2 * P],
                                     y_flat[:, bass.ds(m * (KB * T) + k * T, T)], start=k == 0, stop=k == KB - 1)
                        ins.then_inc(S["pe_mg"], 1)
                pe.wait_ge(S["mrep"], at(l, "mrep", 1))
                w = [tile_in(WFIRST["out"] + i) for i in range(2)]
                for r in range(6):
                    if r >= 4:
                        pe.wait_ge(S["x_updated"], at(l, "x_updated", r - 3))
                    for k in range(KB):
                        ins = MM(bank[4 + r % 4][:, :], merged[:, k, P * (r // 2):P * (r // 2 + 1)], w[r % 2][:, k, :], start=k == 0, stop=k == KB - 1)
                    ins.then_inc(S["pe_out"], 1)
                transposes(3, "pe_xt2", "xnt2")
                pe.wait_ge(S["xnt2"], at(l, "xnt2", 5))
                pe.wait_ge(S["x_updated"], at(l, "x_updated", 6))
                pe.wait_ge(keys_landed, l * 32 + 32)

                def queries(h):
                    w = tile_in(WFIRST["wq"] + h // 4)
                    if h >= 2:
                        pe.wait_ge(S["pq"], at(l, "pq", 2 * (h - 1)))
                    down(bank[4 + h % 2][:, 0:T], w, h % 4, xnT).then_inc(S["pe_wq"], 1)

                queries(0)
                for h in range(PH):
                    if h + 1 < PH:
                        queries(h + 1)
                    pe.wait_ge(S["pq"], at(l, "pq", 2 * h + 2))
                    for t in range(2):
                        if h:
                            pe.wait_ge(S["score"], at(l, "score", 2 * (h - 1) + t + 1))
                        MM(bank[6 + t][:, 0:256], pqT[:, h, P * t:P * (t + 1)], keys[:, h], start=True, stop=True).then_inc(S["pe_sc"], 1)
                for r in range(2):
                    pe.wait_ge(S["score"], at(l, "score", 2 * (PH - 1) + r + 1))
                    for j in range(4):
                        h = 2 * j + r
                        ins = MM(bank[6 + r][:, 0:256], qpad[:, h], keys[:, h], start=j == 0, stop=j == 3)
                    ins.then_inc(S["pe_sc"], 1)

                with pe.Fori(0, STEPS // 2) as j:
                    for q in range(2):
                        s = j * 2 + q
                        pe.wait_ge(S["x_updated"], at(l, "x_updated", s * 2 + 4))
                        for g in range(GROUPS):
                            pe.wait_ge(S["diag"], at(l, "diag", GROUPS * s + g + 1))
                            pe.wait_ge(uv_landed[g], l * (64 * STEPS) + (s * 64 + 64))
                            for i in range(4):
                                for n in range(2):
                                    ins = MM(bank[2 * q + n][:, :], diag[:, 4 * (g % 2) + i], uvbuf[4 * g + i][:, D + 512 * n:D + 512 * (n + 1)],
                                             start=g == 0 and i == 0, stop=g == GROUPS - 1 and i == 3)
                            ins.then_inc(S["v_used"], 1)


def kernel(**inputs):
    import concourse.bacc as bacc
    from concourse.bass_utils import run_bass_kernel_spmd

    I = {k: np.asarray(v) for k, v in inputs.items()}
    L = DEPTH

    def cols(w):
        return w.reshape(KB, P, -1).transpose(1, 0, 2)

    xs = I["x_sample"].reshape(T_S, D)
    x_rows = np.stack([I["x_prompt"][0, :P], I["x_prompt"][0, P:], np.concatenate([xs] * 4)], axis=1)

    sel = np.zeros((P, 3, P), np.float32)
    for t in range(2):
        sel[:, t] = np.eye(P)
    sel[:, 2] = np.tile(np.eye(T_S), (4, 4))
    consts = np.concatenate([sel.reshape(P, -1), np.ones((P, P)), np.tile(np.arange(16), (P, 1))], axis=1).astype(np.float32)

    memT = cols(np.ascontiguousarray(I["mem_prompt"][0].T)).reshape(P, -1)
    ck = I["cache_mem_k"].reshape(L, NSEQ, M, HEADS, 2, P).transpose(0, 1, 5, 3, 4, 2).reshape(L, NSEQ, P, -1)
    cv = I["cache_mem_v"].reshape(L, NSEQ, 2, P, D).transpose(0, 1, 3, 2, 4).reshape(L, NSEQ, P, -1)
    cache = np.concatenate([ck, cv], axis=1)
    st = I["state_conv"].reshape(L, NSEQ, PAST, KB, P).transpose(0, 4, 3, 1, 2)
    state = np.concatenate([st, np.zeros(st.shape[:-1] + (DSEQ,), st.dtype)], axis=-1)

    wl = []
    for l in range(L):
        w = cols(I["w_in"][l])
        part = [w[:, :, D * i:D * (i + 1)] for i in range(8)]

        def blocks(a, b):
            return [np.concatenate([y[:, :, P * c:P * (c + 1)] for c in (2 * i, 2 * i + 1) for y in (a, b)], axis=2) for i in range(4)]

        def halves(a):
            return [a[:, :, :512], a[:, :, 512:]]

        tiles = blocks(part[3], part[2])
        tiles += halves(cols(I["w_mem_k"][l])) + halves(cols(I["w_mem_v"][l])) + halves(part[1]) + halves(part[0]) + halves(part[4])
        for g, name in ((part[5], "w_o_a"), (part[7], "w_o_m"), (part[6], "w_o_b")):
            tiles += blocks(g, cols(I[name][l]))
        tiles += halves(cols(I["w_out"][l])) + halves(cols(I["peer_wq"][l]))
        wl.append(np.stack(tiles))
    wall = np.stack(wl)

    def chan(a):
        return a.reshape(L, KB, P).transpose(0, 2, 1)

    wc = I["b_conv_w"].reshape(L, CONV_W, KB, P).transpose(0, 3, 2, 1).reshape(L, P, -1)
    small = np.concatenate([wc] + [chan(I[n]) for n in ("norm_mix_g", "mem_norm_g", "b_conv_b", "b_ln_g", "b_ln_b")], axis=2)
    rows = np.concatenate([I["a_ln_g"], I["a_ln_b"], I["norm_ffn_g"]], axis=1)
    rows = np.broadcast_to(rows[:, None], (L, P, 3 * D))
    fing = np.broadcast_to(I["final_norm_g"][None], (P, D))
    ws = I["a_ws"].transpose(0, 3, 1, 2)
    wss = np.zeros((L, NSEQ, DSEQ, KB, NSEQ, DSEQ), ws.dtype)
    for n in range(NSEQ):
        wss[:, n, :, :, n, :] = ws[:, :DSEQ, :, :DSEQ]
    bs = np.concatenate([I["a_bs"], np.tile(I["a_bs"][:, :, :DSEQ], (1, 1, NSEQ))], axis=2)
    kt = I["peer_keys"].transpose(0, 2, 4, 1, 3)
    keys = np.zeros((L, 2, 64, PH, 2, NK), kt.dtype)
    for half in range(2):
        keys[:, half, :, :, half, :] = kt[:, half]

    arrays = {
        "x_in": x_rows.reshape(P, TILES, D), "consts_in": consts, "mem_in": memT, "cache_in": cache.reshape(-1, 2 * D),
        "state_in": state.reshape(L * P, -1), "w_in": wall.reshape(L * NW * P, -1), "small_in": small.reshape(L * P, -1),
        "rows_in": rows.reshape(L * P, -1), "fing_in": fing, "ws_in": ws.reshape(L * P, -1), "wss_in": wss.reshape(L * T_S, -1),
        "bs_in": bs.reshape(L, -1), "keys_in": keys.reshape(L * P, -1),
        "uv_in": np.concatenate([I["peer_u"], I["peer_v"]], axis=2).reshape(-1, 2 * D),
    }
    arrays = {k: np.ascontiguousarray(a) for k, a in arrays.items()}
    outs = {
        "y_out": (P, 3 * D), "memk_out": (L * P, 2 * D), "memv_out": (L * P, 2 * D), "convp_out": (L * P, KB * PAST),
        "convs_out": (L * P, KB * NSEQ * (PAST + DSEQ)), "vn_out": (L * T_S, D),
    }
    nc = bacc.Bacc("TRN2", target_bir_lowering=False, num_devices=1)
    args = {k: nc.dram_tensor(k, a.shape, mybir.dt.from_np(a.dtype), kind="ExternalInput").ap() for k, a in arrays.items()}
    args.update({k: nc.dram_tensor(k, s, F32, kind="ExternalOutput").ap() for k, s in outs.items()})
    build(nc, **args)
    r = run_bass_kernel_spmd(nc, [arrays], core_ids=[0]).results[0]

    y = r["y_out"].reshape(P, TILES, D)
    y_prompt = np.concatenate([y[:, 0], y[:, 1]])[None]
    y_sample = y[:T_S, 2].reshape(NSEQ, DSEQ, D)
    mk = r["memk_out"].reshape(L, P, KB, M).transpose(0, 3, 2, 1).reshape(L, 1, M, HEADS, HD)
    mvv = r["memv_out"].reshape(L, P, 2, D).transpose(0, 2, 1, 3).reshape(L, 1, M, HEADS, HD)
    cp = r["convp_out"].reshape(L, P, KB, PAST).transpose(0, 3, 2, 1).reshape(L, 1, PAST, D)
    cs = r["convs_out"].reshape(L, P, KB, NSEQ, PAST + DSEQ)[..., DSEQ:].transpose(0, 3, 4, 2, 1).reshape(L, NSEQ, PAST, D)
    vn = r["vn_out"].reshape(L, NSEQ, DSEQ, D)
    return tuple(np.ascontiguousarray(a) for a in (y_prompt, y_sample, mk, mvv, cp, cs, vn))
```

```python
from contextlib import ExitStack

import numpy as np
import concourse.bass as bass
from concourse import mybir

F32 = mybir.dt.float32
U32 = mybir.dt.uint32
ALU = mybir.AluOpType
ACT = mybir.ActivationFunctionType
AX = mybir.AxisListType

P = 128
DEPTH = 2
D = 1024
KB = D // P
T_P, T_S = 256, 32
T = T_P + T_S
NSEQ, DSEQ = 8, 4
TILES = 3
CONV_W = 31
PAST = CONV_W - 1
M = 256
HEADS, HD = 4, 256
EPS = 1e-6
PH, NK, TOPK = 8, 128, 16
NEXP = NK * NK
STEPS = 2 * PH + 2
GROUPS = 4
NEG = -3.0e38
SCORES = [(0, 0), (1, 0), (0, 1), (1, 1)] + [(h, t) for h in range(2, PH) for t in range(2)] + [(r, 2) for r in range(2)]

WTILES = [("glu", 4), ("mk", 2), ("mv", 2), ("va", 2), ("ua", 2), ("q", 2), ("merge", 12), ("out", 2), ("wq", 2)]
NW = sum(n for _, n in WTILES)
WFIRST = {}
_n = 0
for _kind, _c in WTILES:
    WFIRST[_kind] = _n
    _n += _c


def wslot(i):
    if i < WFIRST["out"]:
        return i % 4
    return (2, 3, 0, 1)[i - WFIRST["out"]]


def wuse(i):
    return sum(wslot(j) == wslot(i) for j in range(i))


WUSES = [sum(wslot(i) == s for i in range(NW)) for s in range(4)]

PER = dict(
    squares=6, meansq=6, roots=9, rstd=9, xrows=6,
    pe_xt=5, xnt=5, memsq=1, pe_memsq=1, varsum=2, memn=8,
    sig=32, pe_glu=16, glu=16, past_zero=1, ws_masked=2,
    pe_mk=8, pe_mv=4, kv=12, pe_va=6, va=6, lnv_var=1, ln_norm=3, ln_g=3, ln_done=3,
    pe_ua=8, ua=8, pe_q=8, q=8, pe_sgu=8, ya=8,
    pe_s=4, nm=5, pexp=9, p=5, pe_pt=5, pt=5, pe_o=4, o=5, qz=8, pe_sk=8, pz=8, pe_so=8, osel=4, pe_ot=1,
    pad_zero=1, conv=1, pe_csum=1, cd=1, csq=8, pe_csq=8, cn=1, yb=8,
    merged_zero=1, pe_mg=48, mg=24, mrep=1, pe_out=6, x_updated=6 + 2 * STEPS,
    pe_xt2=5, xnt2=5, pe_wq=PH + 1, pq=2 * PH + 1, qpad_zero=1, pe_sc=STEPS, score=STEPS,
    stage=STEPS, ids=STEPS, cmax=STEPS, gexp=STEPS, xcur=STEPS,
    dots=GROUPS * STEPS, gel=GROUPS * STEPS, diag=GROUPS * STEPS, v_used=GROUPS * STEPS, offset=1,
)
PRIME = dict(x_updated=5, mg=2, dots=GROUPS, v_used=GROUPS, diag=1)


def at(l, name, k):
    return l * PER[name] + (k + PRIME.get(name, 0))


def build(nc, x_in, consts_in, mem_in, cache_in, state_in, w_in, small_in, rows_in, fing_in, ws_in, wss_in, bs_in,
          keys_in, uv_in, y_out, memk_out, memv_out, convp_out, convs_out, vn_out):
    with ExitStack() as ctx:
        def sb(name, shape, dt=F32):
            return ctx.enter_context(nc.sbuf_tensor(name, shape, dt))

        def sem(name):
            return ctx.enter_context(nc.semaphore(name))

        S = {name: sem("s_" + name) for name in PER}
        w_landed = [sem(f"w_landed{i}") for i in range(4)]
        cache_landed = [sem(f"cache_landed{i}") for i in range(3)]
        uv_landed = [sem(f"uv_landed{g}") for g in range(GROUPS)]
        x_landed = [sem(f"x_landed{t}") for t in range(TILES)]
        consts_landed, small_landed, rows_landed = sem("consts_landed"), sem("small_landed"), sem("rows_landed")
        mem_landed, state_landed, ws_landed, bs_landed = sem("mem_landed"), sem("state_landed"), sem("ws_landed"), sem("bs_landed")
        keys_landed, fing_landed, y_rows = sem("keys_landed"), sem("fing_landed"), sem("y_rows")
        kv_stored, conv_stored, vn_stored, y_stored = sem("kv_stored"), sem("conv_stored"), sem("vn_stored"), sem("y_stored")
        sp_passed, pool_passed, dve_passed, pe_passed = sem("sp_passed"), sem("pool_passed"), sem("dve_passed"), sem("pe_passed")

        arena = sb("arena", [P, 32 * D])
        wbuf = [arena[:, 4096 * s:4096 * (s + 1)].rearrange("p (k c) -> p k c", k=KB) for s in range(4)]
        uvbuf = [arena[:, 2 * D * i:2 * D * (i + 1)] for i in (4, 5, 6, 7, 8, 9, 10, 11, 12, 0, 1, 2, 3, 13, 14, 15)]

        base = [TOPK * D]

        def cut(n):
            base[0] += n
            assert base[0] <= 32 * D
            return arena[:, base[0] - n:base[0]]

        ext_region = cut(KB * (PAST + T_P) + KB * NSEQ * (PAST + DSEQ))
        ext_p = ext_region[:, 0:KB * (PAST + T_P)].rearrange("p (c t) -> p c t", c=KB)
        ext_s_flat = ext_region[:, KB * (PAST + T_P):]
        ext_s = ext_s_flat.rearrange("p (c n t) -> p c n t", c=KB, n=NSEQ)
        merged = ext_region[:, 0:KB * 384].rearrange("p (c t) -> p c t", c=KB)
        qz_flat = [ext_region[:, 1152 * b:1152 * (b + 1)] for b in range(2)]
        pz = [ext_region[:, 2304 + 256 * b:2304 + 256 * (b + 1)] for b in range(2)]
        osel = ext_region[:, 2816:3072]
        y_flat = cut(3 * KB * T)
        Y = [y_flat[:, m * KB * T:(m + 1) * KB * T].rearrange("p (c t) -> p c t", c=KB) for m in range(3)]
        yA, yM, yB = Y
        xnT = cut(KB * T).rearrange("p (c t) -> p c t", c=KB)
        sg = cut(2 * T).rearrange("p (b t) -> p b t", b=2)
        rb = cut(T)
        wsT = cut(KB * P).rearrange("p (g t) -> p g t", g=KB)
        qpad = wsT
        wsS = cut(KB * T_S).rearrange("p (g t) -> p g t", g=KB)

        x = sb("x", [P, TILES, D])
        xn_region = sb("xn", [P, 3 * D])
        xn = xn_region[:, :].rearrange("p (t d) -> p t d", t=TILES)
        a_ln_g, a_ln_b = xn_region[:, 0:D], xn_region[:, D:2 * D]
        bsrow = xn_region[0:1, 0:KB * 160].rearrange("p (g t) -> p g t", g=KB)
        prob = xn_region[:, 2 * D:2 * D + 512]
        probT = xn_region[:, 2 * D + 512:3 * D]
        vn_region = sb("vn", [P, 3 * D])
        vn = vn_region[:, :].rearrange("p (t d) -> p t d", t=TILES)
        memT = vn_region[:, 0:KB * M].rearrange("p (c t) -> p c t", c=KB)
        pqT = vn_region[:, 0:KB * T].rearrange("p (c t) -> p c t", c=KB)
        small_r = [KB * T]

        def cut_small(n):
            small_r[0] += n
            assert small_r[0] <= 3 * D
            return vn_region[:, small_r[0] - n:small_r[0]]

        selcur = cut_small(P)
        top_v = cut_small(32)
        top_if = cut_small(32)
        cand_v = cut_small(16)
        ab_f = cut_small(32)
        pick_k = cut_small(32)
        eid_f = cut_small(16)
        gexp = cut_small(16)
        gsum, grec, ncmax = cut_small(1), cut_small(1), cut_small(1)
        gate = cut_small(32)
        hid = cut_small(32)
        gel = cut_small(32)

        kv_region = sb("kv", [P, 4 * D])
        kT = kv_region[:, 0:KB * M].rearrange("p (c t) -> p c t", c=KB)
        vmem = kv_region[:, KB * M:].rearrange("p (m d) -> p m d", m=2)
        keys = kv_region[:, 0:PH * M].rearrange("p (h n) -> p h n", h=PH)
        ffn_g = kv_region[:, 2 * D:3 * D]
        fing = kv_region[:, 0:D]
        xcur = ffn_g
        diag = kv_region[:, 3 * D:4 * D].rearrange("p (i c) -> p i c", i=8)

        c_region = sb("cache", [P, 3 * 2 * D])
        cache = [c_region[:, 2 * D * i:2 * D * (i + 1)] for i in range(3)]
        scores = c_region[:, 0:STEPS * 256]
        stg = c_region[:, STEPS * 256:(STEPS + 1) * 256]
        cand = c_region[:, (STEPS + 1) * 256:(STEPS + 2) * 256]
        rest = c_region[:, (STEPS + 2) * 256:(STEPS + 3) * 256]
        onehot = c_region[:, (STEPS + 3) * 256:(STEPS + 5) * 256]

        consts = sb("consts", [P, 3 * P + P + 16])
        ident = consts[:, 0:P]
        ones = consts[:, 3 * P:4 * P]
        iota16 = consts[:, 4 * P:4 * P + 16]
        small = sb("small", [P, KB * CONV_W + 5 * KB])
        wconv = small[:, 0:KB * CONV_W].rearrange("p (c w) -> p c w", c=KB)
        g_mix, g_mem, conv_b, bln_g, bln_b = (small[:, KB * (CONV_W + i):KB * (CONV_W + i + 1)] for i in range(5))
        stat = sb("stat", [P, 40])
        ssq, msq, rt, rstd = (stat[:, 3 * i:3 * i + 3] for i in range(4))
        rsum, rmax, nmax, rinv = (stat[:, 12 + 2 * i:14 + 2 * i] for i in range(4))
        mv = stat[:, 20:26].rearrange("p (t c) -> p t c", t=3)
        bnst = stat[:, 26:38]
        eoff = stat[:, 38:39]
        idx_u = sb("idx_u", [P, 112], U32)
        ids = idx_u[:, 0:32]
        top_i = idx_u[:, 32:64]
        cand_i = idx_u[:, 64:80]
        ab_u = idx_u[:, 80:112]

        bank = [ctx.enter_context(nc.psum_tensor(f"bank{i}", [P, 512], F32)) for i in range(8)]
        block = ctx.enter_context(nc.Block())

        XT = [(0, 0, 4, 0), (0, 4, 4, 1), (1, 0, 4, 2), (1, 4, 4, 3), (2, 0, 8, 0)]
        XT_BANK = (0, 1, 4, 5, 6)
        XT2_BANK = [b for _, _, _, b in XT]
        TOK = [(0, 128), (128, 128), (256, 32)]

        def qz_cols(b, n):
            v = qz_flat[b].rearrange("p (h x) -> p h x", h=HEADS)[:, :, 0:256]
            return v.rearrange("p h (d c) -> p h d c", d=2)[:, :, :, 4 * n:4 * n + 4]

        def pz_cols(ap, n):
            return ap.rearrange("p (b c) -> p b c", b=8)[:, :, 4 * n:4 * n + 4]

        @block.sync
        def _(sp):
            sp.dma_start(x[:, 0], x_in[:, 0]).then_inc(x_landed[0], 16)
            sp.dma_start(consts[:, :], consts_in).then_inc(consts_landed, 16)
            for t in range(1, TILES):
                sp.dma_start(x[:, t], x_in[:, t]).then_inc(x_landed[t], 16)
            with sp.Fori(0, DEPTH) as l:
                def rows(ap, per, off, n=P):
                    return ap[bass.ds(l * per + off, n), :]

                def load_w(i):
                    sp.dma_start(arena[:, 4096 * wslot(i):4096 * (wslot(i) + 1)],
                                 rows(w_in, NW * P, i * P)).then_inc(w_landed[wslot(i)], 16)

                def load_cache(i):
                    sp.dma_start(cache[i % 3], rows(cache_in, 16 * P, i * P)).then_inc(cache_landed[i % 3], 16)

                sp.wait_ge(S["v_used"], at(l, "v_used", -1))
                sp.dma_start(small[:, :], rows(small_in, P, 0)).then_inc(small_landed, 16)
                load_w(0)
                sp.wait_ge(S["x_updated"], at(l, "x_updated", 0))
                sp.dma_start(vn_region[:, 0:KB * M], mem_in).then_inc(mem_landed, 16)
                load_w(1)
                sp.dma_start(ext_s_flat, rows(state_in, P, 0)).then_inc(state_landed, 16)
                load_w(2)
                load_w(3)
                sp.wait_ge(S["pe_xt"], at(l, "pe_xt", 5))
                sp.dma_start(xn_region[:, 0:2 * D], rows(rows_in, P, 0)[:, 0:2 * D]).then_inc(rows_landed, 16)
                sp.dma_start(wsT, rows(ws_in, P, 0).rearrange("p (g t) -> p g t", g=KB)).then_inc(ws_landed, 16)
                sp.dma_start(wsS[0:T_S], rows(wss_in, T_S, 0, T_S).rearrange("p (g t) -> p g t", g=KB)).then_inc(ws_landed, 16)
                for i in range(3):
                    load_cache(i)
                freed = [("pe_glu", 4 * (i + 1)) for i in range(4)] + [("pe_mk", 4), ("pe_mk", 8), ("pe_mv", 2), ("pe_mv", 4),
                         ("pe_va", 3), ("pe_va", 6), ("pe_ua", 4), ("pe_ua", 8), ("pe_q", 4), ("pe_q", 8)]
                freed += [("pe_mg", 4 * (i + 1)) for i in range(12)]
                prev = {i: max((j for j in range(i) if wslot(j) == wslot(i)), default=None) for i in range(NW)}

                def load_next(i):
                    name, k = freed[prev[i]]
                    sp.wait_ge(S[name], at(l, name, k))
                    load_w(i)

                for i in range(4, 8):
                    load_next(i)
                sp.wait_ge(S["glu"], at(l, "glu", 16))
                sp.dma_start(rows(convp_out, P, 0).rearrange("p (c t) -> p c t", c=KB),
                             ext_p[:, :, T_P:T_P + PAST]).then_inc(conv_stored, 16)
                sp.dma_start(rows(convs_out, P, 0), ext_s_flat).then_inc(conv_stored, 16)
                for i in range(8, 14):
                    load_next(i)
                sp.wait_ge(S["kv"], at(l, "kv", 12))
                sp.dma_start(rows(memk_out, P, 0), kv_region[:, 0:2 * D]).then_inc(kv_stored, 16)
                sp.dma_start(rows(memv_out, P, 0), kv_region[:, 2 * D:4 * D]).then_inc(kv_stored, 16)
                for i in range(14, 18):
                    load_next(i)
                for i in range(3, 16):
                    name, k = ("pe_sk", i - 2) if i - 3 < 8 else ("pe_so", i - 10)
                    sp.wait_ge(S[name], at(l, name, k))
                    load_cache(i)
                sp.wait_ge(S["ln_done"], at(l, "ln_done", 3))
                sp.dma_start(rows(vn_out, T_S, 0, T_S), vn[0:T_S, 2, :]).then_inc(vn_stored, 16)
                for i in range(18, NW):
                    load_next(i)
                sp.wait_ge(S["o"], at(l, "o", 5))
                sp.sem_inc(sp_passed, 1)
                sp.wait_ge(kv_stored, l * 32 + 32)
                sp.dma_start(kv_region[:, 0:2 * D], rows(keys_in, P, 0)).then_inc(keys_landed, 16)
                sp.dma_start(ffn_g, rows(rows_in, P, 0)[:, 2 * D:3 * D]).then_inc(keys_landed, 16)
            sp.wait_ge(S["pe_sc"], DEPTH * PER["pe_sc"])
            sp.dma_start(fing, fing_in).then_inc(fing_landed, 16)
            for t in range(TILES):
                sp.wait_ge(y_rows, t + 1)
                sp.dma_start(y_out[:, D * t:D * (t + 1)], xn[:, t]).then_inc(y_stored, 16)
            sp.wait_ge(kv_stored, DEPTH * 32)
            sp.wait_ge(conv_stored, DEPTH * 32)
            sp.wait_ge(vn_stored, DEPTH * 16)
            sp.wait_ge(y_stored, 16 * TILES)

        @block.gpsimd
        def _(pool):
            with pool.Fori(0, DEPTH) as l:
                pool.wait_ge(S["x_updated"], at(l, "x_updated", 0))
                pool.sem_inc(pool_passed, 1)
                nc.gpsimd.memset(ext_p[:, :, 0:PAST], 0.0).then_inc(S["past_zero"], 1)
                pool.wait_ge(ws_landed, l * 32 + 32)
                pool.sem_inc(pool_passed, 1)
                nc.gpsimd.affine_select(out=wsT, in_=wsT, compare_op=ALU.is_ge, fill=0.0, base=0,
                                        pattern=[[0, KB], [1, P]], channel_multiplier=-1).then_inc(S["ws_masked"], 1)
                nc.gpsimd.affine_select(out=wsS[0:T_S], in_=wsS[0:T_S], compare_op=ALU.is_ge, fill=0.0, base=0,
                                        pattern=[[0, KB], [1, T_S]], channel_multiplier=-1).then_inc(S["ws_masked"], 1)
                pool.wait_ge(S["conv"], at(l, "conv", 1))
                pool.wait_ge(conv_stored, l * 32 + 32)
                pool.sem_inc(pool_passed, 1)
                nc.gpsimd.memset(ext_region[:, 0:2816], 0.0).then_inc(S["pad_zero"], 1)
                pool.wait_ge(S["pad_zero"], at(l, "pad_zero", 1))
                pool.wait_ge(S["q"], at(l, "q", 8))
                pool.sem_inc(pool_passed, 1)
                for n in range(NSEQ):
                    if n >= 2:
                        pool.wait_ge(S["pe_sk"], at(l, "pe_sk", n - 1))
                        pool.sem_inc(pool_passed, 1)
                        nc.gpsimd.memset(qz_cols(n % 2, n - 2), 0.0)
                    nc.gpsimd.tensor_copy(qz_cols(n % 2, n), yM[:, :, T_P + 4 * n:T_P + 4 * n + 4].rearrange("p (h d) t -> p h d t", h=HEADS)
                                          ).then_inc(S["qz"], 1)
                    if 1 <= n <= 3:
                        t = n - 1
                        r = TOK[t][1]
                        if t == 0:
                            pool.wait_ge(rows_landed, l * 16 + 16)
                        pool.wait_ge(S["ln_norm"], at(l, "ln_norm", t + 1))
                        nc.gpsimd.tensor_tensor(vn[0:r, t], vn[0:r, t], a_ln_g[0:r], ALU.mult).then_inc(S["ln_g"], 1)
                        pool.wait_ge(S["ln_g"], at(l, "ln_g", t + 1))
                        nc.gpsimd.tensor_tensor(vn[0:r, t], vn[0:r, t], a_ln_b[0:r], ALU.add).then_inc(S["ln_done"], 1)
                pool.wait_ge(S["ln_done"], at(l, "ln_done", 3))
                pool.dma_start(xn_region[0:1, 0:KB * 160], bs_in[bass.ds(l, 1), :]).then_inc(bs_landed, 16)
                pool.wait_ge(S["pt"], at(l, "pt", 5))
                pool.sem_inc(pool_passed, 1)
                for n in range(NSEQ):
                    if n >= 2:
                        pool.wait_ge(S["pe_so"], at(l, "pe_so", n - 1))
                        pool.sem_inc(pool_passed, 1)
                        nc.gpsimd.memset(pz_cols(pz[n % 2], n - 2), 0.0)
                    nc.gpsimd.tensor_copy(pz_cols(pz[n % 2], n), pz_cols(probT[:, 0:256], n)).then_inc(S["pz"], 1)
                pool.wait_ge(S["pe_sgu"], at(l, "pe_sgu", 8))
                pool.sem_inc(pool_passed, 1)
                nc.gpsimd.memset(qpad, 0.0).then_inc(S["qpad_zero"], 1)
                pool.wait_ge(S["pe_ot"], at(l, "pe_ot", 1))
                pool.sem_inc(pool_passed, 1)
                nc.gpsimd.memset(merged, 0.0).then_inc(S["merged_zero"], 1)

                def gathers(s, q):
                    for g in range(GROUPS):
                        pool.wait_ge(S["ids"], at(l, "ids", s + 1))
                        pool.wait_ge(S["v_used"], at(l, "v_used", GROUPS * (s - 1) + g + 1))
                        if g == 0:
                            pool.wait_ge(S["pe_out"], at(l, "pe_out", 6))
                        pool.sem_inc(pool_passed, 1)
                        for i in range(4 * g, 4 * g + 4):
                            used = {9: ("pe_wq", 5), 11: ("pe_wq", PH + 1), 15: ("pe_sc", STEPS)}.get(i)
                            if used is not None:
                                pool.wait_ge(S[used[0]], at(l, *used))
                                pool.sem_inc(pool_passed, 1)
                            nc.gpsimd.indirect_dma_start(
                                out=uvbuf[i], out_offset=None, in_=uv_in,
                                in_offset=bass.IndirectOffsetOnAxis(ap=ids[:, 16 * q + i:16 * q + i + 1], axis=0),
                            ).then_inc(uv_landed[g], 16)

                with pool.Fori(0, STEPS // 2) as j:
                    for q in range(2):
                        gathers(j * 2 + q, q)

        @block.scalar
        def _(act):
            def A(out, in_, func, name, bias=0.0, scale=1.0, accum=None):
                ins = nc.scalar.activation(out, in_, func, bias=bias, scale=scale, **({} if accum is None else {"accum_out": accum}))
                return ins.then_inc(S[name], 1)

            act.wait_ge(consts_landed, 16)

            def row_squares(l, t, updated):
                act.wait_ge(x_landed[t], 16)
                act.wait_ge(S["x_updated"], at(l, "x_updated", updated))
                A(xn[:, t], x[:, t], ACT.Square, "squares", accum=ssq[:, t:t + 1])

            def row_root(l, t, done):
                act.wait_ge(S["meansq"], at(l, "meansq", done + t + 1))
                A(rt[:, t:t + 1], msq[:, t:t + 1], ACT.Sqrt, "roots")

            def norm_rows(l, tiles, updated):
                for t in tiles:
                    row_squares(l, t, updated)
                    row_root(l, t, 0)

            def root(l, out, in_):
                A(out, in_, ACT.Sqrt, "roots")

            norm_rows(0, (0, 1), 0)
            with act.Fori(0, DEPTH) as l:
                norm_rows(l, (2,), 0)
                for c in range(KB):
                    act.wait_ge(S["pe_glu"], at(l, "pe_glu", 2 * c + 1))
                    if c >= 2:
                        act.wait_ge(S["glu"], at(l, "glu", 2 * (c - 1)))
                    A(sg[:, c % 2], bank[2 * (c % 2)][:, 0:T], ACT.Sigmoid, "sig")
                    if c == 0:
                        act.wait_ge(mem_landed, l * 16 + 16)
                        A(kT, memT, ACT.Square, "memsq")
                    if c == 2:
                        act.wait_ge(S["varsum"], at(l, "varsum", 1))
                        root(l, rb[:, 0:M], rb[:, 0:M])
                for b in range(KB):
                    act.wait_ge(S["pe_mk"], at(l, "pe_mk", b + 1))
                    A(kT[:, b], bank[4 + b % 4][:, 0:M], ACT.Copy, "kv")
                for r in range(4):
                    act.wait_ge(S["pe_mv"], at(l, "pe_mv", r + 1))
                    A(vmem[:, r % 2, 512 * (r // 2):512 * (r // 2 + 1)], bank[r][:, :], ACT.Copy, "kv")
                for r in range(6):
                    n = (P, P, T_S)[r % 3]
                    act.wait_ge(S["pe_va"], at(l, "pe_va", r + 1))
                    A(vn[0:n, r % 3, 512 * (r // 3):512 * (r // 3 + 1)], bank[4 + r % 4][0:n, :], ACT.Gelu, "va")
                for b in range(KB):
                    act.wait_ge(S["pe_ua"], at(l, "pe_ua", b + 1))
                    A(yA[:, b], bank[b % 4][:, 0:T], ACT.Gelu, "ua")
                for b in range(KB):
                    act.wait_ge(S["pe_q"], at(l, "pe_q", b + 1))
                    A(yM[:, b], bank[4 + b % 4][:, 0:T], ACT.Copy, "q")
                act.wait_ge(S["lnv_var"], at(l, "lnv_var", 1))
                root(l, rt, msq)
                for h in range(HEADS):
                    act.wait_ge(S["nm"], at(l, "nm", h + 1))
                    if h:
                        act.wait_ge(S["pe_pt"], at(l, "pe_pt", h))
                    for t in range(2):
                        A(prob[:, M * t:M * (t + 1)], bank[4 + h % 2][:, M * t:M * (t + 1)], ACT.Exp, "pexp",
                          bias=nmax[:, t:t + 1], scale=HD ** -0.5, accum=rsum[:, t:t + 1])
                    act.wait_ge(S["pe_pt"], at(l, "pe_pt", h + 1))
                    if h:
                        act.wait_ge(S["pe_o"], at(l, "pe_o", h))
                    A(probT, bank[6][:, :], ACT.Copy, "pt")
                    act.wait_ge(S["pe_o"], at(l, "pe_o", h + 1))
                    A(yM[:, 2 * h:2 * h + 2, 0:T_P], bank[7][:, :].rearrange("p (c t) -> p c t", c=2), ACT.Copy, "o")
                    if h == 2:
                        act.wait_ge(S["cd"], at(l, "cd", 1))
                        for c in range(KB):
                            if c >= 2:
                                act.wait_ge(S["pe_csq"], at(l, "pe_csq", c - 1))
                            A(sg[:, c % 2], yB[:, c], ACT.Square, "csq")
                        act.wait_ge(S["varsum"], at(l, "varsum", 2))
                        root(l, rb, rb)
                act.wait_ge(S["nm"], at(l, "nm", 5))
                A(prob[:, 256:512], bank[3][:, 0:256], ACT.Exp, "pexp", bias=nmax[:, 0:1], scale=HD ** -0.5, accum=rsum[:, 0:1])
                act.wait_ge(S["cn"], at(l, "cn", 1))
                for c in range(KB):
                    A(yB[:, c], yB[:, c], ACT.Silu, "yb", bias=bln_b[:, c:c + 1], scale=bln_g[:, c:c + 1])
                act.wait_ge(S["pe_pt"], at(l, "pe_pt", 5))
                A(probT[:, 0:256], bank[6][:, 0:256], ACT.Copy, "pt")
                act.wait_ge(S["pe_so"], at(l, "pe_so", 8))
                for h in range(HEADS):
                    r = slice(T_S * h, T_S * (h + 1))
                    A(osel[r], bank[4 + h // 2][r, 256 * (h % 2):256 * (h % 2 + 1)], ACT.Copy, "osel")
                act.wait_ge(S["pe_ot"], at(l, "pe_ot", 1))
                A(yM[:, :, T_P:T].rearrange("p (h d) t -> p h d t", h=HEADS),
                  bank[7][:, 0:256].rearrange("p (d h t) -> p h d t", d=2, h=HEADS), ACT.Copy, "o")
                act.wait_ge(S["pe_csq"], at(l, "pe_csq", 8))
                with act.Fori(0, 3) as m:
                    for c in range(KB):
                        act.wait_ge(S["pe_mg"], at(l, "pe_mg", m * 16 + 2 * c + 1))
                        act.wait_ge(S["mg"], at(l, "mg", m * 8 + c - 1))
                        A(sg[:, c % 2], bank[2 * (c % 2)][:, 0:T], ACT.Sigmoid, "sig")

                def turned(*parts):
                    for i in parts:
                        t, k0, nk, b = XT[i]
                        a, n = TOK[t]
                        act.wait_ge(S["pe_xt2"], at(l, "pe_xt2", i + 1))
                        A(xnT[:, k0:k0 + nk, a:a + n], bank[b][:, 0:nk * n].rearrange("p (k t) -> p k t", k=nk), ACT.Copy, "xnt2")

                def stage(s):
                    act.wait_ge(S["ids"], at(l, "ids", s))
                    A(stg, scores[:, bass.ds(s * 256, 256)] if not isinstance(s, int) else scores[:, 256 * s:256 * (s + 1)], ACT.Copy, "stage")

                def gate_exp(s):
                    act.wait_ge(S["cmax"], at(l, "cmax", s + 1))
                    A(gexp, cand_v, ACT.Exp, "gexp", bias=ncmax, accum=gsum)

                def step(s, q, last, begun=False):
                    if not last and not begun:
                        stage(s + 1)
                    for g in range(1 if begun else 0, GROUPS):
                        gelu(s, q, g)
                        if g == 1 and not last:
                            gate_exp(s + 1)

                def gelu(s, q, g):
                    act.wait_ge(S["dots"], at(l, "dots", GROUPS * s + g + 1))
                    a = 16 * q + 4 * g
                    A(gel[:, a:a + 4], hid[:, a:a + 4], ACT.Gelu, "gel")

                def tile_of(j):
                    act.wait_ge(S["dots"], at(l, "dots", j * 8))
                    t = j // 4
                    A(xcur, xn_region[:, bass.ds(t * D, D)] if not isinstance(t, int) else xn[:, t], ACT.Copy, "xcur")
                    act.wait_ge(S["diag"], at(l, "diag", j * 8))
                    A(selcur, consts[:, bass.ds(t * P, P)] if not isinstance(t, int) else consts[:, P * t:P * (t + 1)], ACT.Copy, "xcur")

                def score(i):
                    h, t = SCORES[i]
                    s = PH * t + h
                    act.wait_ge(S["pe_sc"], at(l, "pe_sc", i + 1))
                    A(scores[:, 256 * s:256 * (s + 1)], bank[6 + i % 2 if i else 3][:, 0:256], ACT.Copy, "score")

                row_squares(l, 0, 2)
                row_root(l, 0, 3)
                turned(0, 1)
                act.wait_ge(vn_stored, l * 16 + 16)
                act.wait_ge(S["pe_wq"], at(l, "pe_wq", 1))
                A(pqT[:, 0, 0:P], bank[2][:, 0:P], ACT.Copy, "pq")
                score(0)
                act.wait_ge(S["score"], at(l, "score", 1))
                stage(0)
                row_squares(l, 1, 4)
                gate_exp(0)
                row_root(l, 1, 3)
                turned(2, 3)
                row_squares(l, 2, 6)
                row_root(l, 2, 3)
                turned(4)
                act.wait_ge(S["qpad_zero"], at(l, "qpad_zero", 1))
                for h in range(PH):
                    act.wait_ge(S["pe_wq"], at(l, "pe_wq", h + 2))
                    a = P if h == 0 else 0
                    A(pqT[:, h, a:T], bank[4 + h % 2][:, a:T], ACT.Copy, "pq")
                    j0 = T_S * (h // 2)
                    A(qpad[:, h, j0:j0 + T_S], bank[4 + h % 2][:, T_P:T], ACT.Copy, "pq")
                    if h == 0:
                        tile_of(0)
                    if h == 2:
                        score(1)
                        act.wait_ge(S["score"], at(l, "score", 2))
                        stage(1)
                    if h == 4:
                        gelu(0, 0, 0)
                for i in range(2, STEPS):
                    score(i)
                act.wait_ge(S["score"], at(l, "score", STEPS))
                step(0, 0, False, begun=True)
                step(1, 1, False)
                tile_of(1)
                with act.Fori(1, STEPS // 2 - 1) as j:
                    step(j * 2, 0, False)
                    step(j * 2 + 1, 1, False)
                    tile_of(j + 1)
                step(STEPS - 2, 0, False)
                step(STEPS - 1, 1, True)
                norm_rows(l + 1, (0, 1), -4)
            norm_rows(DEPTH, (2,), 0)

        @block.vector
        def _(dve):
            V = nc.vector
            for name in ("x_updated", "mg", "dots", "diag"):
                dve.sem_inc(S[name], PRIME[name])
            V.memset(eoff, 0.0)
            dve.wait_ge(consts_landed, 16)
            for t in range(TILES):
                dve.wait_ge(x_landed[t], 16)

            def mix_norm(l, tiles):
                for t in tiles:
                    dve.wait_ge(S["squares"], at(l, "squares", t + 1))
                    V.tensor_scalar(msq[:, t:t + 1], ssq[:, t:t + 1], 1.0 / D, EPS, ALU.mult, ALU.add).then_inc(S["meansq"], 1)
                    dve.wait_ge(S["roots"], at(l, "roots", t + 1))
                    V.reciprocal(rstd[:, t:t + 1], rt[:, t:t + 1]).then_inc(S["rstd"], 1)
                    dve.drain()
                    V.tensor_scalar(xn[:, t], x[:, t], rstd[:, t:t + 1], None, ALU.mult).then_inc(S["xrows"], 1)

            def one_over_root(l, k):
                dve.wait_ge(S["roots"], at(l, "roots", k))
                V.reciprocal(rstd, rt).then_inc(S["rstd"], 1)
                dve.drain()

            mix_norm(0, (0, 1))
            with dve.Fori(0, DEPTH) as l:
                dve.wait_ge(small_landed, l * 16 + 16)

                def turned(*parts):
                    for i in parts:
                        t, k0, nk, _ = XT[i]
                        a, n = TOK[t]
                        dve.wait_ge(S["pe_xt"], at(l, "pe_xt", i + 1))
                        V.tensor_tensor(xnT[:, k0:k0 + nk, a:a + n], bank[XT_BANK[i]][:, 0:nk * n].rearrange("p (k t) -> p k t", k=nk),
                                        g_mix[:, k0:k0 + nk].unsqueeze(2).to_broadcast([P, nk, n]), ALU.mult).then_inc(S["xnt"], 1)

                turned(0, 1)
                mix_norm(l, (2,))
                turned(2, 3, 4)

                def memory_sum():
                    dve.wait_ge(S["pe_memsq"], at(l, "pe_memsq", 1))
                    V.tensor_scalar(rb[:, 0:M], bank[4][:, 0:M], 1.0 / D, EPS, ALU.mult, ALU.add).then_inc(S["varsum"], 1)

                def memory_norm():
                    dve.wait_ge(S["roots"], at(l, "roots", 4))
                    V.reciprocal(rb[:, 0:M], rb[:, 0:M]).then_inc(S["rstd"], 1)
                    dve.drain()
                    for k in range(KB):
                        V.scalar_tensor_tensor(out=memT[:, k], in0=memT[:, k], scalar=g_mem[:, k:k + 1], in1=rb[:, 0:M],
                                               op0=ALU.mult, op1=ALU.mult).then_inc(S["memn"], 1)

                dve.wait_ge(state_landed, l * 16 + 16)
                for c in range(KB):
                    dve.wait_ge(S["pe_glu"], at(l, "pe_glu", 2 * c + 2))
                    dve.wait_ge(S["sig"], at(l, "sig", c + 1))
                    val = bank[2 * (c % 2) + 1]
                    V.tensor_tensor(ext_p[:, c, PAST:], val[:, 0:T_P], sg[:, c % 2, 0:T_P], ALU.mult).then_inc(S["glu"], 1)
                    V.tensor_tensor(ext_s[:, c, :, PAST:], val[:, T_P:T].rearrange("p (n t) -> p n t", n=NSEQ),
                                    sg[:, c % 2, T_P:T].rearrange("p (n t) -> p n t", n=NSEQ), ALU.mult).then_inc(S["glu"], 1)
                    if c == 1:
                        memory_sum()
                    if c == 2:
                        memory_norm()
                dve.wait_ge(S["past_zero"], at(l, "past_zero", 1))
                dve.sem_inc(dve_passed, 1)
                dve.drain()
                for c0 in (0, 4):
                    for c in range(c0, c0 + 4):
                        V.tensor_scalar(yB[:, c, 0:T_P], ext_p[:, c, 0:T_P], wconv[:, c, 0:1], conv_b[:, c:c + 1], ALU.mult, ALU.add)
                        V.tensor_scalar(yB[:, c, T_P:T].rearrange("p (n t) -> p n t", n=NSEQ), ext_s[:, c, :, 0:DSEQ],
                                        wconv[:, c, 0:1], conv_b[:, c:c + 1], ALU.mult, ALU.add)
                    for w in range(1, CONV_W):
                        dve.drain()
                        for c in range(c0, c0 + 4):
                            V.scalar_tensor_tensor(out=yB[:, c, 0:T_P], in0=ext_p[:, c, w:w + T_P], scalar=wconv[:, c, w:w + 1],
                                                   in1=yB[:, c, 0:T_P], op0=ALU.mult, op1=ALU.add)
                            ys = yB[:, c, T_P:T].rearrange("p (n t) -> p n t", n=NSEQ)
                            ins = V.scalar_tensor_tensor(out=ys, in0=ext_s[:, c, :, w:w + DSEQ], scalar=wconv[:, c, w:w + 1],
                                                         in1=ys, op0=ALU.mult, op1=ALU.add)
                ins.then_inc(S["conv"], 1)
                dve.wait_ge(S["va"], at(l, "va", 6))
                for t, n in enumerate((P, P, T_S)):
                    for i in range(2):
                        V.bn_stats(bnst[0:n, 6 * i:6 * i + 6], vn[0:n, t, 512 * i:512 * (i + 1)])
                    dve.drain()
                    V.bn_aggr(mv[0:n, t], bnst[0:n, :])
                    dve.drain()
                V.memset(msq, 1.0)
                dve.drain()
                for t, n in enumerate((P, P, T_S)):
                    ins = V.tensor_scalar(msq[0:n, t:t + 1], mv[0:n, t, 1:2], 1.0, EPS, ALU.mult, ALU.add)
                ins.then_inc(S["lnv_var"], 1)
                one_over_root(l, 5)
                for t, n in enumerate((P, P, T_S)):
                    V.tensor_scalar(vn[0:n, t], vn[0:n, t], mv[0:n, t, 0:1], rstd[0:n, t:t + 1], ALU.subtract, ALU.mult).then_inc(S["ln_norm"], 1)
                def att_max(h):
                    dve.wait_ge(S["pe_s"], at(l, "pe_s", h + 1))
                    V.tensor_reduce(rmax, bank[4 + h % 2][:, :].rearrange("p (t m) -> p t m", t=2), AX.X, ALU.max)
                    dve.drain()
                    V.tensor_scalar(nmax, rmax, -HD ** -0.5, None, ALU.mult).then_inc(S["nm"], 1)

                def att_norm(h):
                    dve.wait_ge(S["pexp"], at(l, "pexp", 2 * h + 2))
                    V.reciprocal(rinv, rsum)
                    dve.drain()
                    pr = prob.rearrange("p (t m) -> p t m", t=2)
                    V.tensor_tensor(pr, pr, rinv.unsqueeze(2).to_broadcast([P, 2, M]), ALU.mult).then_inc(S["p"], 1)

                att_max(0)
                att_norm(0)
                dve.wait_ge(S["pe_csum"], at(l, "pe_csum", 1))
                for c in range(KB):
                    ins = V.scalar_tensor_tensor(out=yB[:, c], in0=bank[0][:, 0:T], scalar=-1.0 / D, in1=yB[:, c], op0=ALU.mult, op1=ALU.add)
                ins.then_inc(S["cd"], 1)
                for h in (1, 2):
                    att_max(h)
                    att_norm(h)
                dve.wait_ge(S["pe_csq"], at(l, "pe_csq", 8))
                V.tensor_scalar(rb, bank[1][:, 0:T], 1.0 / D, EPS, ALU.mult, ALU.add).then_inc(S["varsum"], 1)
                att_max(3)
                att_norm(3)
                dve.wait_ge(S["roots"], at(l, "roots", 6))
                V.reciprocal(rb, rb).then_inc(S["rstd"], 1)
                dve.drain()
                V.tensor_tensor(yB, yB, rb.unsqueeze(1).to_broadcast([P, KB, T]), ALU.mult).then_inc(S["cn"], 1)
                dve.wait_ge(S["pe_sk"], at(l, "pe_sk", 8))
                V.tensor_reduce(rmax[:, 0:1], bank[3][:, 0:256], AX.X, ALU.max)
                dve.drain()
                V.tensor_scalar(nmax[:, 0:1], rmax[:, 0:1], -HD ** -0.5, None, ALU.mult).then_inc(S["nm"], 1)
                dve.wait_ge(S["pexp"], at(l, "pexp", 9))
                V.reciprocal(rinv[:, 0:1], rsum[:, 0:1])
                dve.drain()
                V.tensor_scalar(prob[:, 256:512], prob[:, 256:512], rinv[:, 0:1], None, ALU.mult).then_inc(S["p"], 1)
                for g in range(KB):
                    dve.wait_ge(S["pe_sgu"], at(l, "pe_sgu", g + 1))
                    V.tensor_tensor(yA[:, g], yA[:, g], bank[g % 3][:, 0:T], ALU.mult).then_inc(S["ya"], 1)
                dve.wait_ge(S["merged_zero"], at(l, "merged_zero", 1))
                dve.sem_inc(dve_passed, 1)
                with dve.Fori(0, 3) as m:
                    for c in range(KB):
                        dve.wait_ge(S["pe_mg"], at(l, "pe_mg", m * 16 + 2 * c + 2))
                        dve.wait_ge(S["sig"], at(l, "sig", m * 8 + 8 + c + 1))
                        V.tensor_tensor(sg[:, c % 2], sg[:, c % 2], bank[2 * (c % 2) + 1][:, 0:T], ALU.mult)
                        dve.drain()
                        V.tensor_tensor(merged[:, c, 0:T], merged[:, c, 0:T], sg[:, c % 2], ALU.add).then_inc(S["mg"], 1)
                dve.drain()
                src = merged[:, :, T_P:T].unsqueeze(2).to_broadcast([P, KB, 3, T_S])
                V.tensor_copy(merged[:, :, T:384].rearrange("p c (j t) -> p c j t", j=3), src).then_inc(S["mrep"], 1)
                def add_out(t):
                    for r in (2 * t, 2 * t + 1):
                        dve.wait_ge(S["pe_out"], at(l, "pe_out", r + 1))
                        xs = x[:, t, 512 * (r % 2):512 * (r % 2 + 1)]
                        V.tensor_tensor(xs, xs, bank[4 + r % 4][:, :], ALU.add).then_inc(S["x_updated"], 1)

                def ffn_norm(t):
                    dve.wait_ge(S["squares"], at(l, "squares", 3 + t + 1))
                    V.tensor_scalar(msq[:, t:t + 1], ssq[:, t:t + 1], 1.0 / D, EPS, ALU.mult, ALU.add).then_inc(S["meansq"], 1)
                    dve.wait_ge(S["roots"], at(l, "roots", 6 + t + 1))
                    V.reciprocal(rstd[:, t:t + 1], rt[:, t:t + 1]).then_inc(S["rstd"], 1)
                    dve.drain()
                    V.scalar_tensor_tensor(out=xn[:, t], in0=x[:, t], scalar=rstd[:, t:t + 1], in1=ffn_g,
                                           op0=ALU.mult, op1=ALU.mult).then_inc(S["xrows"], 1)

                def top16(vals, idx, src, scratch):
                    V.max(vals[:, 0:8], src)
                    dve.drain()
                    V.max_index(idx[:, 0:8], vals[:, 0:8], src)
                    V.match_replace(scratch, vals[:, 0:8], src, NEG)
                    dve.drain()
                    V.max(vals[:, 8:16], scratch)
                    dve.drain()
                    V.max_index(idx[:, 8:16], vals[:, 8:16], scratch)

                def pick_halves(s):
                    dve.wait_ge(S["stage"], at(l, "stage", s + 1))
                    dve.sem_inc(dve_passed, 1)
                    dve.drain()
                    for half in range(2):
                        top16(top_v[:, 16 * half:16 * half + 16], top_i[:, 16 * half:16 * half + 16],
                              stg[:, NK * half:NK * (half + 1)], rest[:, NK * half:NK * (half + 1)])
                    dve.drain()
                    V.tensor_tensor(cand.rearrange("p (a b) -> p a b", a=16), top_v[:, 0:16].unsqueeze(2).to_broadcast([P, 16, 16]),
                                    top_v[:, 16:32].unsqueeze(1).to_broadcast([P, 16, 16]), ALU.add)
                    V.tensor_copy(top_if, top_i)
                    dve.drain()

                def pick_experts(q):
                    top16(cand_v, cand_i, cand, rest)
                    dve.drain()
                    V.tensor_scalar(ncmax, cand_v[:, 0:1], -1.0, None, ALU.mult).then_inc(S["cmax"], 1)
                    V.tensor_scalar(ab_u[:, 0:16], cand_i, 4, None, ALU.logical_shift_right)
                    V.tensor_scalar(ab_u[:, 16:32], cand_i, 15, None, ALU.bitwise_and)
                    dve.drain()
                    V.tensor_copy(ab_f, ab_u)
                    dve.drain()
                    oh3 = onehot.rearrange("p (k a) -> p k a", a=16)
                    V.tensor_tensor(oh3, ab_f.unsqueeze(2).to_broadcast([P, 32, 16]),
                                    iota16.unsqueeze(1).to_broadcast([P, 32, 16]), ALU.is_equal)
                    dve.drain()
                    for half in range(2):
                        part = oh3[:, 16 * half:16 * half + 16]
                        V.tensor_tensor(part, part, top_if[:, 16 * half:16 * half + 16].unsqueeze(1).to_broadcast([P, 16, 16]), ALU.mult)
                    dve.drain()
                    V.tensor_reduce(pick_k, oh3, AX.X, ALU.add)
                    dve.drain()
                    V.scalar_tensor_tensor(out=eid_f, in0=pick_k[:, 0:16], scalar=float(NK), in1=pick_k[:, 16:32], op0=ALU.mult, op1=ALU.add)
                    dve.drain()
                    V.tensor_scalar(ids[:, 16 * q:16 * q + 16], eid_f, eoff, None, ALU.add).then_inc(S["ids"], 1)

                def diags(s, q, g):
                    dve.wait_ge(S["gel"], at(l, "gel", GROUPS * s + g + 1))
                    dve.wait_ge(S["v_used"], at(l, "v_used", GROUPS * s + g - 1))
                    for i in range(4):
                        a = 16 * q + 4 * g + i
                        ins = V.tensor_scalar(diag[:, 4 * (g % 2) + i], selcur, gel[:, a:a + 1], gate[:, a:a + 1], ALU.mult, ALU.mult)
                    ins.then_inc(S["diag"], 1)

                def gates(s, q):
                    dve.wait_ge(S["gexp"], at(l, "gexp", s + 1))
                    V.reciprocal(grec, gsum)
                    dve.drain()
                    V.tensor_scalar(gate[:, 16 * q:16 * q + 16], gexp, grec, None, ALU.mult)
                    dve.drain()

                def dots(s, q, g):
                    dve.wait_ge(uv_landed[g], l * (64 * STEPS) + (s * 64 + 64))
                    for i in range(4 * g, 4 * g + 4):
                        ins = V.tensor_tensor_reduce(out=uvbuf[i][:, 0:D], in0=uvbuf[i][:, 0:D], in1=xcur, scale=1.0, scalar=0.0,
                                                     op0=ALU.mult, op1=ALU.add, accum_out=hid[:, 16 * q + i:16 * q + i + 1])
                    ins.then_inc(S["dots"], 1)

                def add_share(s, q, tile):
                    dve.wait_ge(S["v_used"], at(l, "v_used", GROUPS * s + GROUPS))
                    for n in range(2):
                        if isinstance(tile, int):
                            xs = x[:, tile, 512 * n:512 * (n + 1)]
                        else:
                            xs = x[:, :, :].rearrange("p t d -> p (t d)")[:, bass.ds(tile * D + 512 * n, 512)]
                        V.tensor_tensor(xs, xs, bank[2 * q + n][:, :], ALU.add).then_inc(S["x_updated"], 1)
                    dve.drain()

                def step(s, q, last, before=None):
                    dots(s, q, 0)
                    if not last:
                        pick_halves(s + 1)
                    diags(s, q, 0)
                    dots(s, q, 1)
                    if not last:
                        pick_experts(1 - q)
                    diags(s, q, 1)
                    dots(s, q, 2)
                    if before is not None:
                        add_share(*before)
                    diags(s, q, 2)
                    dots(s, q, 3)
                    if not last:
                        gates(s + 1, 1 - q)
                    diags(s, q, 3)

                def pair(j, last):
                    s = j * 2
                    tile = j // 4
                    dve.wait_ge(S["xcur"], at(l, "xcur", j * 2 + 2))
                    step(s, 0, False)
                    step(s + 1, 1, last, (s, 0, tile))
                    if last:
                        mix_norm(l + 1, (0, 1))
                    add_share(s + 1, 1, tile)

                add_out(0)
                dve.wait_ge(keys_landed, l * 32 + 32)
                ffn_norm(0)
                add_out(1)
                pick_halves(0)
                pick_experts(0)
                ffn_norm(1)
                add_out(2)
                ffn_norm(2)
                gates(0, 0)
                with dve.Fori(0, STEPS // 2 - 1) as j:
                    pair(j, False)
                pair(STEPS // 2 - 1, True)
                V.tensor_scalar(eoff, eoff, float(NEXP), None, ALU.add).then_inc(S["offset"], 1)
                dve.drain()
            dve.wait_ge(fing_landed, 16)
            dve.drain()
            for t in (0, 1):
                V.tensor_tensor(xn[:, t], xn[:, t], fing, ALU.mult).then_inc(y_rows, 1)
            mix_norm(DEPTH, (2,))
            dve.drain()
            V.tensor_tensor(xn[:, 2], xn[:, 2], fing, ALU.mult).then_inc(y_rows, 1)

        @block.tensor
        def _(pe):
            MM = nc.tensor.matmul
            pe.sem_inc(S["v_used"], PRIME["v_used"])
            pe.wait_ge(consts_landed, 16)

            with pe.Fori(0, DEPTH) as l:
                def tile_in(i):
                    pe.wait_ge(w_landed[wslot(i)], l * (16 * WUSES[wslot(i)]) + 16 * (wuse(i) + 1))
                    return wbuf[wslot(i)]

                def down(out, w, b, rhs):
                    for k in range(KB):
                        ins = MM(out, w[:, k, P * b:P * (b + 1)], rhs[:, k], start=k == 0, stop=k == KB - 1)
                    return ins

                def transposes(rows_before, name, parts, banks):
                    for i in parts:
                        t, k0, nk, _ = XT[i]
                        n = TOK[t][1]
                        pe.wait_ge(S["xrows"], at(l, "xrows", rows_before + t + 1))
                        if i == 4:
                            if rows_before:
                                pe.wait_ge(S["xnt2"], at(l, "xnt2", 1))
                            pe.sem_inc(pe_passed, 1)
                        for k in range(nk):
                            ins = nc.tensor.transpose(bank[banks[i]][:, n * k:n * (k + 1)], xn[0:n, t, P * (k0 + k):P * (k0 + k + 1)],
                                                      ident[0:n, 0:n])
                        ins.then_inc(S[name], 1)

                pe.wait_ge(S["x_updated"], at(l, "x_updated", -2))
                transposes(0, "pe_xt", range(5), XT_BANK)
                pe.wait_ge(S["xnt"], at(l, "xnt", 5))
                for c in range(KB):
                    if c % 2 == 0:
                        w = tile_in(WFIRST["glu"] + c // 2)
                    if c >= 2:
                        pe.wait_ge(S["glu"], at(l, "glu", 2 * (c - 1)))
                    for v in range(2):
                        down(bank[2 * (c % 2) + v][:, 0:T], w, 2 * (c % 2) + v, xnT).then_inc(S["pe_glu"], 1)
                    if c == 1:
                        pe.wait_ge(S["memsq"], at(l, "memsq", 1))
                        for k in range(KB):
                            ins = MM(bank[4][:, 0:M], ones, kT[:, k], start=k == 0, stop=k == KB - 1)
                        ins.then_inc(S["pe_memsq"], 1)
                pe.wait_ge(S["memn"], at(l, "memn", 8))
                for b in range(KB):
                    if b % 4 == 0:
                        w = tile_in(WFIRST["mk"] + b // 4)
                    else:
                        pass
                    if b >= 4:
                        pe.wait_ge(S["kv"], at(l, "kv", b - 3))
                    down(bank[4 + b % 4][:, 0:M], w, b % 4, memT).then_inc(S["pe_mk"], 1)
                pe.wait_ge(S["glu"], at(l, "glu", 16))
                for r in range(4):
                    if r % 2 == 0:
                        w = tile_in(WFIRST["mv"] + r // 2)
                    for k in range(KB):
                        ins = MM(bank[r][:, :], memT[:, k, P * (r % 2):P * (r % 2 + 1)], w[:, k, :], start=k == 0, stop=k == KB - 1)
                    ins.then_inc(S["pe_mv"], 1)
                for r in range(6):
                    if r % 3 == 0:
                        w = tile_in(WFIRST["va"] + r // 3)
                    if r < 4:
                        pe.wait_ge(S["kv"], at(l, "kv", 5 + r))
                    else:
                        pe.wait_ge(S["va"], at(l, "va", r - 3))
                    a, n = TOK[r % 3]
                    for k in range(KB):
                        ins = MM(bank[4 + r % 4][0:n, :], xnT[:, k, a:a + n], w[:, k, :], start=k == 0, stop=k == KB - 1)
                    ins.then_inc(S["pe_va"], 1)
                for b in range(KB):
                    if b % 4 == 0:
                        w = tile_in(WFIRST["ua"] + b // 4)
                    if b < 4:
                        pe.wait_ge(S["kv"], at(l, "kv", 9 + b))
                    else:
                        pe.wait_ge(S["ua"], at(l, "ua", b - 3))
                    down(bank[b % 4][:, 0:T], w, b % 4, xnT).then_inc(S["pe_ua"], 1)
                for b in range(KB):
                    if b % 4 == 0:
                        w = tile_in(WFIRST["q"] + b // 4)
                    if b < 4:
                        pe.wait_ge(S["va"], at(l, "va", 6))
                    else:
                        pe.wait_ge(S["q"], at(l, "q", b - 3))
                    down(bank[4 + b % 4][:, 0:T], w, b % 4, xnT).then_inc(S["pe_q"], 1)
                pe.wait_ge(S["q"], at(l, "q", 8))

                def att_scores(h):
                    if h >= 2:
                        pe.wait_ge(S["pexp"], at(l, "pexp", 2 * (h - 1)))
                    for t in range(2):
                        for d in range(2):
                            ins = MM(bank[4 + h % 2][:, M * t:M * (t + 1)], yM[:, 2 * h + d, P * t:P * (t + 1)], kT[:, 2 * h + d],
                                     start=d == 0, stop=d == 1)
                    ins.then_inc(S["pe_s"], 1)

                def att_out(h):
                    pe.wait_ge(S["p"], at(l, "p", h + 1))
                    if h:
                        pe.wait_ge(S["pt"], at(l, "pt", h))
                    for m in range(2):
                        for t in range(2):
                            ins = nc.tensor.transpose(bank[6][:, 256 * m + P * t:256 * m + P * (t + 1)],
                                                      prob[:, M * t + P * m:M * t + P * (m + 1)], ident)
                    ins.then_inc(S["pe_pt"], 1)

                def att_out2(h):
                    pe.wait_ge(S["pt"], at(l, "pt", h + 1))
                    if h:
                        pe.wait_ge(S["o"], at(l, "o", h))
                    for d in range(2):
                        for m in range(2):
                            ins = MM(bank[7][:, T_P * d:T_P * (d + 1)], vmem[:, m, HD * h + P * d:HD * h + P * (d + 1)],
                                     probT[:, 256 * m:256 * (m + 1)], start=m == 0, stop=m == 1)
                    ins.then_inc(S["pe_o"], 1)

                def sample_scores(n):
                    pe.wait_ge(S["qz"], at(l, "qz", n + 1))
                    pe.wait_ge(cache_landed[n % 3], l * (16 * (6 if n % 3 == 0 else 5)) + 16 * (n // 3 + 1))
                    kc = cache[n % 3].rearrange("p (c t) -> p c t", c=KB)
                    for c in range(KB):
                        ins = MM(bank[3][:, 0:M], qz_flat[n % 2][:, P * c:P * (c + 1)], kc[:, c],
                                 start=n == 0 and c == 0, stop=n == NSEQ - 1 and c == KB - 1)
                    ins.then_inc(S["pe_sk"], 1)

                pe.wait_ge(S["ua"], at(l, "ua", 8))
                att_scores(0)
                att_scores(1)
                sample_scores(0)
                sample_scores(1)
                att_out(0)
                pe.wait_ge(S["conv"], at(l, "conv", 1))
                for c in range(KB):
                    ins = MM(bank[0][:, 0:T], ones, yB[:, c], start=c == 0, stop=c == KB - 1)
                ins.then_inc(S["pe_csum"], 1)
                att_out2(0)
                att_scores(2)
                sample_scores(2)
                att_out(1)
                sample_scores(3)
                att_out2(1)
                att_scores(3)
                sample_scores(4)
                att_out(2)
                sample_scores(5)
                att_out2(2)
                for c in range(KB):
                    pe.wait_ge(S["csq"], at(l, "csq", c + 1))
                    MM(bank[1][:, 0:T], ones, sg[:, c % 2], start=c == 0, stop=c == KB - 1).then_inc(S["pe_csq"], 1)
                sample_scores(6)
                att_out(3)
                sample_scores(7)
                att_out2(3)
                pe.wait_ge(S["ln_done"], at(l, "ln_done", 3))
                pe.wait_ge(S["ws_masked"], at(l, "ws_masked", 2))
                pe.wait_ge(bs_landed, l * 16 + 16)
                pe.wait_ge(S["varsum"], at(l, "varsum", 2))

                def spatial(g):
                    if g >= 3:
                        pe.wait_ge(S["ya"], at(l, "ya", g - 2))
                    ch = slice(P * g, P * (g + 1))
                    out = bank[g % 3]
                    for t in range(2):
                        MM(out[:, P * t:P * (t + 1)], vn[:, t, ch], wsT[:, g], start=True, stop=False)
                        MM(out[:, P * t:P * (t + 1)], ones[0:1, :], bsrow[:, g, 0:P], start=False, stop=True)
                    MM(out[:, T_P:T], vn[0:T_S, 2, ch], wsS[0:T_S, g], start=True, stop=False)
                    MM(out[:, T_P:T], ones[0:1, :], bsrow[:, g, P:160], start=False, stop=True).then_inc(S["pe_sgu"], 1)

                for g in range(3):
                    spatial(g)
                pe.wait_ge(S["p"], at(l, "p", 5))
                pe.wait_ge(S["pt"], at(l, "pt", 4))
                for m in range(2):
                    ins = nc.tensor.transpose(bank[6][:, P * m:P * (m + 1)], prob[:, 256 + P * m:256 + P * (m + 1)], ident)
                ins.then_inc(S["pe_pt"], 1)
                for g in range(3, 6):
                    spatial(g)
                for n in range(NSEQ):
                    i = 8 + n
                    pe.wait_ge(S["pz"], at(l, "pz", n + 1))
                    pe.wait_ge(cache_landed[i % 3], l * (16 * (6 if i % 3 == 0 else 5)) + 16 * (i // 3 + 1))
                    vc = cache[i % 3].rearrange("p (m d) -> p m d", m=2)
                    for m in range(2):
                        for f in range(2):
                            ins = MM(bank[4 + f][:, :], pz[n % 2][:, P * m:P * (m + 1)], vc[:, m, 512 * f:512 * (f + 1)],
                                     start=n == 0 and m == 0, stop=n == NSEQ - 1 and m == 1)
                    ins.then_inc(S["pe_so"], 1)
                for g in range(6, KB):
                    spatial(g)
                pe.wait_ge(S["osel"], at(l, "osel", 4))
                pe.wait_ge(S["o"], at(l, "o", 4))
                for d in range(2):
                    ins = nc.tensor.transpose(bank[7][:, P * d:P * (d + 1)], osel[:, P * d:P * (d + 1)], ident)
                ins.then_inc(S["pe_ot"], 1)
                pe.wait_ge(S["ya"], at(l, "ya", 8))
                pe.sem_inc(pe_passed, 1)
                with pe.Fori(0, 3) as m:
                    for c in range(KB):
                        i = WFIRST["merge"] + c // 2
                        if c % 2 == 0:
                            s = wslot(i)
                            pe.wait_ge(w_landed[s], l * (16 * WUSES[s]) + (m * 16 + 16 * (wuse(i) + 1)))
                        pe.wait_ge(S["mg"], at(l, "mg", m * 8 + c - 1))
                        if c == 2:
                            pe.wait_ge(S["o"], at(l, "o", 5))
                            pe.wait_ge(S["yb"], at(l, "yb", 8))
                            pe.sem_inc(pe_passed, 1)
                        for k in range(KB):
                            ins = MM(bank[2 * (c % 2)][:, 0:T], wbuf[wslot(i)][:, k, 256 * (c % 2):256 * (c % 2) + P], xnT[:, k],
                                     start=k == 0, stop=k == KB - 1)
                        ins.then_inc(S["pe_mg"], 1)
                        for k in range(KB):
                            ins = MM(bank[2 * (c % 2) + 1][:, 0:T], wbuf[wslot(i)][:, k, 256 * (c % 2) + P:256 * (c % 2) + 2 * P],
                                     y_flat[:, bass.ds(m * (KB * T) + k * T, T)], start=k == 0, stop=k == KB - 1)
                        ins.then_inc(S["pe_mg"], 1)
                pe.wait_ge(S["mg"], at(l, "mg", 24))
                w = [tile_in(WFIRST["out"] + i) for i in range(2)]

                def project(r):
                    if r == 4:
                        pe.wait_ge(S["mrep"], at(l, "mrep", 1))
                    if r >= 4:
                        pe.wait_ge(S["x_updated"], at(l, "x_updated", r - 3))
                    for k in range(KB):
                        ins = MM(bank[4 + r % 4][:, :], merged[:, k, P * (r // 2):P * (r // 2 + 1)], w[r % 2][:, k, :], start=k == 0, stop=k == KB - 1)
                    ins.then_inc(S["pe_out"], 1)

                def query(h, out, a, b):
                    wq = tile_in(WFIRST["wq"] + h // 4)
                    for k in range(KB):
                        ins = MM(out, wq[:, k, P * (h % 4):P * (h % 4 + 1)], xnT[:, k, a:b], start=k == 0, stop=k == KB - 1)
                    ins.then_inc(S["pe_wq"], 1)

                def score(i):
                    h, t = SCORES[i]
                    out = bank[6 + i % 2 if i else 3][:, 0:256]
                    if i >= 3:
                        pe.wait_ge(S["score"], at(l, "score", i - 1))
                    if t < 2:
                        MM(out, pqT[:, h, P * t:P * (t + 1)], keys[:, h], start=True, stop=True).then_inc(S["pe_sc"], 1)
                    else:
                        for j in range(4):
                            ins = MM(out, qpad[:, 2 * j + h], keys[:, 2 * j + h], start=j == 0, stop=j == 3)
                        ins.then_inc(S["pe_sc"], 1)

                for r in range(3):
                    project(r)
                transposes(3, "pe_xt2", (0, 1), XT2_BANK)
                project(3)
                pe.wait_ge(S["xnt2"], at(l, "xnt2", 2))
                query(0, bank[2][:, 0:P], 0, P)
                pe.wait_ge(keys_landed, l * 32 + 32)
                pe.wait_ge(S["pq"], at(l, "pq", 1))
                score(0)
                project(4)
                project(5)
                pe.wait_ge(S["score"], at(l, "score", 1))
                transposes(3, "pe_xt2", (2, 3, 4), XT2_BANK)
                pe.wait_ge(S["xnt2"], at(l, "xnt2", 5))
                pe.wait_ge(S["x_updated"], at(l, "x_updated", 6))
                for h in range(PH):
                    if h >= 2:
                        pe.wait_ge(S["pq"], at(l, "pq", 2 * (h - 1) + 1))
                    a = P if h == 0 else 0
                    query(h, bank[4 + h % 2][:, a:T], a, T)
                    if h == 2:
                        pe.wait_ge(S["pq"], at(l, "pq", 5))
                        score(1)
                pe.wait_ge(S["pq"], at(l, "pq", 2 * PH + 1))
                for i in range(2, STEPS):
                    score(i)

                with pe.Fori(0, STEPS // 2) as j:
                    for q in range(2):
                        s = j * 2 + q
                        pe.wait_ge(S["x_updated"], at(l, "x_updated", s * 2 + 4))
                        for g in range(GROUPS):
                            pe.wait_ge(S["diag"], at(l, "diag", GROUPS * s + g + 1))
                            pe.wait_ge(uv_landed[g], l * (64 * STEPS) + (s * 64 + 64))
                            for i in range(4):
                                for n in range(2):
                                    ins = MM(bank[2 * q + n][:, :], diag[:, 4 * (g % 2) + i], uvbuf[4 * g + i][:, D + 512 * n:D + 512 * (n + 1)],
                                             start=g == 0 and i == 0, stop=g == GROUPS - 1 and i == 3)
                            ins.then_inc(S["v_used"], 1)


def kernel(**inputs):
    import concourse.bacc as bacc
    from concourse.bass_utils import run_bass_kernel_spmd

    I = {k: np.asarray(v) for k, v in inputs.items()}
    L = DEPTH

    def cols(w):
        return w.reshape(KB, P, -1).transpose(1, 0, 2)

    xs = I["x_sample"].reshape(T_S, D)
    x_rows = np.stack([I["x_prompt"][0, :P], I["x_prompt"][0, P:], np.concatenate([xs] * 4)], axis=1)

    sel = np.zeros((P, 3, P), np.float32)
    for t in range(2):
        sel[:, t] = np.eye(P)
    sel[:, 2] = np.tile(np.eye(T_S), (4, 4))
    consts = np.concatenate([sel.reshape(P, -1), np.ones((P, P)), np.tile(np.arange(16), (P, 1))], axis=1).astype(np.float32)

    memT = cols(np.ascontiguousarray(I["mem_prompt"][0].T)).reshape(P, -1)
    ck = I["cache_mem_k"].reshape(L, NSEQ, M, HEADS, 2, P).transpose(0, 1, 5, 3, 4, 2).reshape(L, NSEQ, P, -1)
    cv = I["cache_mem_v"].reshape(L, NSEQ, 2, P, D).transpose(0, 1, 3, 2, 4).reshape(L, NSEQ, P, -1)
    cache = np.concatenate([ck, cv], axis=1)
    st = I["state_conv"].reshape(L, NSEQ, PAST, KB, P).transpose(0, 4, 3, 1, 2)
    state = np.concatenate([st, np.zeros(st.shape[:-1] + (DSEQ,), st.dtype)], axis=-1)

    wl = []
    for l in range(L):
        w = cols(I["w_in"][l])
        part = [w[:, :, D * i:D * (i + 1)] for i in range(8)]

        def blocks(a, b):
            return [np.concatenate([y[:, :, P * c:P * (c + 1)] for c in (2 * i, 2 * i + 1) for y in (a, b)], axis=2) for i in range(4)]

        def halves(a):
            return [a[:, :, :512], a[:, :, 512:]]

        tiles = blocks(part[3], part[2])
        tiles += halves(cols(I["w_mem_k"][l])) + halves(cols(I["w_mem_v"][l])) + halves(part[1]) + halves(part[0]) + halves(part[4])
        for g, name in ((part[5], "w_o_a"), (part[7], "w_o_m"), (part[6], "w_o_b")):
            tiles += blocks(g, cols(I[name][l]))
        tiles += halves(cols(I["w_out"][l])) + halves(cols(I["peer_wq"][l]))
        wl.append(np.stack(tiles))
    wall = np.stack(wl)

    def chan(a):
        return a.reshape(L, KB, P).transpose(0, 2, 1)

    wc = I["b_conv_w"].reshape(L, CONV_W, KB, P).transpose(0, 3, 2, 1).reshape(L, P, -1)
    small = np.concatenate([wc] + [chan(I[n]) for n in ("norm_mix_g", "mem_norm_g", "b_conv_b", "b_ln_g", "b_ln_b")], axis=2)
    rows = np.concatenate([I["a_ln_g"], I["a_ln_b"], I["norm_ffn_g"]], axis=1)
    rows = np.broadcast_to(rows[:, None], (L, P, 3 * D))
    fing = np.broadcast_to(I["final_norm_g"][None], (P, D))
    ws = I["a_ws"].transpose(0, 3, 1, 2)
    wss = np.zeros((L, NSEQ, DSEQ, KB, NSEQ, DSEQ), ws.dtype)
    for n in range(NSEQ):
        wss[:, n, :, :, n, :] = ws[:, :DSEQ, :, :DSEQ]
    bs = np.concatenate([I["a_bs"], np.tile(I["a_bs"][:, :, :DSEQ], (1, 1, NSEQ))], axis=2)
    kt = I["peer_keys"].transpose(0, 2, 4, 1, 3)
    keys = np.zeros((L, 2, 64, PH, 2, NK), kt.dtype)
    for half in range(2):
        keys[:, half, :, :, half, :] = kt[:, half]

    arrays = {
        "x_in": x_rows.reshape(P, TILES, D), "consts_in": consts, "mem_in": memT, "cache_in": cache.reshape(-1, 2 * D),
        "state_in": state.reshape(L * P, -1), "w_in": wall.reshape(L * NW * P, -1), "small_in": small.reshape(L * P, -1),
        "rows_in": rows.reshape(L * P, -1), "fing_in": fing, "ws_in": ws.reshape(L * P, -1), "wss_in": wss.reshape(L * T_S, -1),
        "bs_in": bs.reshape(L, -1), "keys_in": keys.reshape(L * P, -1),
        "uv_in": np.concatenate([I["peer_u"], I["peer_v"]], axis=2).reshape(-1, 2 * D),
    }
    arrays = {k: np.ascontiguousarray(a) for k, a in arrays.items()}
    outs = {
        "y_out": (P, 3 * D), "memk_out": (L * P, 2 * D), "memv_out": (L * P, 2 * D), "convp_out": (L * P, KB * PAST),
        "convs_out": (L * P, KB * NSEQ * (PAST + DSEQ)), "vn_out": (L * T_S, D),
    }
    nc = bacc.Bacc("TRN2", target_bir_lowering=False, num_devices=1)
    args = {k: nc.dram_tensor(k, a.shape, mybir.dt.from_np(a.dtype), kind="ExternalInput").ap() for k, a in arrays.items()}
    args.update({k: nc.dram_tensor(k, s, F32, kind="ExternalOutput").ap() for k, s in outs.items()})
    build(nc, **args)
    r = run_bass_kernel_spmd(nc, [arrays], core_ids=[0]).results[0]

    y = r["y_out"].reshape(P, TILES, D)
    y_prompt = np.concatenate([y[:, 0], y[:, 1]])[None]
    y_sample = y[:T_S, 2].reshape(NSEQ, DSEQ, D)
    mk = r["memk_out"].reshape(L, P, KB, M).transpose(0, 3, 2, 1).reshape(L, 1, M, HEADS, HD)
    mvv = r["memv_out"].reshape(L, P, 2, D).transpose(0, 2, 1, 3).reshape(L, 1, M, HEADS, HD)
    cp = r["convp_out"].reshape(L, P, KB, PAST).transpose(0, 3, 2, 1).reshape(L, 1, PAST, D)
    cs = r["convs_out"].reshape(L, P, KB, NSEQ, PAST + DSEQ)[..., DSEQ:].transpose(0, 3, 4, 2, 1).reshape(L, NSEQ, PAST, D)
    vn = r["vn_out"].reshape(L, NSEQ, DSEQ, D)
    return tuple(np.ascontiguousarray(a) for a in (y_prompt, y_sample, mk, mvv, cp, cs, vn))
```
